# Optimizing a Trainium2 kernel written in Bass

```python
import jax, jax.numpy as jnp
from jax import lax
import numpy as np

D_MODEL = 1024
BATCH = 1
SEQ = 1024
DEPTH = 1

N_HEADS = 8
N_KV = 2
HEAD_DIM = 64
GQA_R = N_HEADS // N_KV
NSA_WIDTH = N_HEADS * HEAD_DIM
KV_WIDTH = N_KV * HEAD_DIM
CMP_BLOCK = 32
CMP_STRIDE = 16
SEL_BLOCK = 64
SEL_TOPK = 16
N_FORCED_LOCAL = 2
WINDOW = 512
QBLK = 128
FORCE_SCORE = 1e9
POOL_SIZES = (2, 4, 8, 16)
POOL_GROUP = 128
POOL_WIDTH = POOL_GROUP * len(POOL_SIZES)
D_FF = 4 * D_MODEL
ROPE_THETA = 10000.0
EPS = 1e-6
N_MOD = 6
IN_SIZES = (NSA_WIDTH, KV_WIDTH, KV_WIDTH, KV_WIDTH, KV_WIDTH, KV_WIDTH, KV_WIDTH,
            3 * N_HEADS, POOL_WIDTH, 2 * D_MODEL)
IN_WIDTH = int(sum(IN_SIZES))
IN_SPLITS = [int(v) for v in np.cumsum(IN_SIZES)[:-1]]

kernel_name = "hybrid_nsa_pool_block"

def rms_norm(x, g):
    xf = x.astype(jnp.float32)
    y = xf * lax.rsqrt(jnp.mean(xf * xf, axis=-1, keepdims=True) + EPS)
    return (y * g.astype(jnp.float32)).astype(x.dtype)

def rope(x):
    s = x.shape[1]
    half = HEAD_DIM // 2
    inv = ROPE_THETA ** (-jnp.arange(half, dtype=jnp.float32) / half)
    ang = jnp.arange(s, dtype=jnp.float32)[:, None] * inv[None, :]
    cos = jnp.cos(ang)[None, :, None, :]
    sin = jnp.sin(ang)[None, :, None, :]
    xf = x.astype(jnp.float32)
    x1, x2 = xf[..., :half], xf[..., half:]
    return jnp.concatenate([x1 * cos - x2 * sin, x2 * cos + x1 * sin], axis=-1).astype(x.dtype)

def masked_softmax(s, mask):
    s = jnp.where(mask, s.astype(jnp.float32), -jnp.inf)
    m = jnp.max(s, axis=-1, keepdims=True)
    m = jnp.where(jnp.isfinite(m), m, 0.0)
    e = jnp.exp(s - m)
    return e / jnp.maximum(jnp.sum(e, axis=-1, keepdims=True), 1e-30)

def compress(k, pe, w1, w2):
    b, s, g, dh = k.shape
    n_cmp = (s - CMP_BLOCK) // CMP_STRIDE + 1
    idx = np.arange(n_cmp)[:, None] * CMP_STRIDE + np.arange(CMP_BLOCK)[None, :]
    blk = k[:, idx] + pe[None, None, :, None, :]
    blk = blk.transpose(0, 1, 3, 2, 4).reshape(b, n_cmp, g, CMP_BLOCK * dh)
    return jax.nn.gelu(blk @ w1) @ w2

def nsa_attention(q, kc, vc, ks, vs, kw, vw, gate_logits):
    b, s = q.shape[0], q.shape[1]
    nq = s // QBLK
    n_cmp = kc.shape[1]
    n_sel = s // SEL_BLOCK
    topk = min(SEL_TOPK, n_sel)
    scale = HEAD_DIM ** -0.5
    cmp_start = np.arange(n_cmp) * CMP_STRIDE
    cmp_end = jnp.asarray(cmp_start + CMP_BLOCK - 1)
    sel_start = np.arange(n_sel) * SEL_BLOCK
    overlap = jnp.asarray(((cmp_start[:, None] < sel_start[None, :] + SEL_BLOCK) &
                           (cmp_start[:, None] + CMP_BLOCK > sel_start[None, :])).astype(np.float32))
    ks_blk = ks.reshape(b, n_sel, SEL_BLOCK, N_KV, HEAD_DIM).transpose(0, 3, 1, 2, 4)
    vs_blk = vs.reshape(b, n_sel, SEL_BLOCK, N_KV, HEAD_DIM).transpose(0, 3, 1, 2, 4)
    pad = ((0, 0), (WINDOW, 0), (0, 0), (0, 0))
    kw_pad = jnp.pad(kw, pad)
    vw_pad = jnp.pad(vw, pad)
    q_blocks = q.reshape(b, nq, QBLK, N_KV, GQA_R, HEAD_DIM).transpose(1, 0, 2, 3, 4, 5)
    g_blocks = gate_logits.reshape(b, nq, QBLK, N_HEADS, 3).transpose(1, 0, 2, 3, 4)
    bi = jnp.arange(b)[:, None, None, None]
    gi = jnp.arange(N_KV)[None, :, None, None]
    blk_id = jnp.arange(n_sel)

    def one_block(args):
        qb, gb, c = args
        t = c * QBLK + jnp.arange(QBLK)
        sc = jnp.einsum('bqgrd,bngd->bgrqn', qb, kc) * scale
        p_cmp = masked_softmax(sc, cmp_end[None, :] <= t[:, None])
        o_cmp = jnp.einsum('bgrqn,bngd->bqgrd', p_cmp.astype(vc.dtype), vc)
        imp = jnp.einsum('bgrqn,nm->bgqm', p_cmp, overlap)
        cur = t // SEL_BLOCK
        causal_blk = blk_id[None, :] <= cur[:, None]
        forced = (blk_id[None, :] == 0) | (causal_blk & (blk_id[None, :] > cur[:, None] - N_FORCED_LOCAL))
        imp = jnp.where(forced, FORCE_SCORE, jnp.where(causal_blk, imp, -jnp.inf))
        _, idx = lax.top_k(imp, topk)
        kg = ks_blk[bi, gi, idx].reshape(b, N_KV, QBLK, topk * SEL_BLOCK, HEAD_DIM)
        vg = vs_blk[bi, gi, idx].reshape(b, N_KV, QBLK, topk * SEL_BLOCK, HEAD_DIM)
        kpos = (idx[..., None] * SEL_BLOCK + jnp.arange(SEL_BLOCK)).reshape(b, N_KV, QBLK, topk * SEL_BLOCK)
        sel_mask = (kpos <= t[None, None, :, None])[:, :, None]
        ss = jnp.einsum('bqgrd,bgqjd->bgrqj', qb, kg) * scale
        p_sel = masked_softmax(ss, sel_mask)
        o_sel = jnp.einsum('bgrqj,bgqjd->bqgrd', p_sel.astype(vg.dtype), vg)
        kwb = lax.dynamic_slice_in_dim(kw_pad, c * QBLK, QBLK + WINDOW, axis=1)
        vwb = lax.dynamic_slice_in_dim(vw_pad, c * QBLK, QBLK + WINDOW, axis=1)
        kp = c * QBLK - WINDOW + jnp.arange(QBLK + WINDOW)
        wmask = (kp[None, :] <= t[:, None]) & (kp[None, :] > t[:, None] - WINDOW) & (kp[None, :] >= 0)
        sw = jnp.einsum('bqgrd,bjgd->bgrqj', qb, kwb) * scale
        p_win = masked_softmax(sw, wmask)
        o_win = jnp.einsum('bgrqj,bjgd->bqgrd', p_win.astype(vwb.dtype), vwb)
        g = jax.nn.sigmoid(gb.astype(jnp.float32)).reshape(b, QBLK, N_KV, GQA_R, 3).astype(qb.dtype)
        return g[..., 0:1] * o_cmp + g[..., 1:2] * o_sel + g[..., 2:3] * o_win

    out = lax.map(one_block, (q_blocks, g_blocks, jnp.arange(nq)))
    return out.transpose(1, 0, 2, 3, 4, 5).reshape(b, s, NSA_WIDTH)

def pool_mixer(u, w_pool, pool_scale):
    b, s, _ = u.shape
    uf = u.astype(jnp.float32)
    cs = jnp.concatenate([jnp.zeros((b, 1, POOL_WIDTH), jnp.float32), jnp.cumsum(uf, axis=1)], axis=1)
    t = np.arange(s)
    outs = []
    for gidx, w in enumerate(POOL_SIZES):
        sl = slice(gidx * POOL_GROUP, (gidx + 1) * POOL_GROUP)
        start = np.maximum(t + 1 - w, 0)
        cnt = jnp.asarray((t + 1 - start).astype(np.float32))[None, :, None]
        mean = (cs[:, t + 1, sl] - cs[:, start, sl]) / cnt
        outs.append(mean - uf[:, :, sl])
    pooled = jnp.stack(outs, axis=2).astype(u.dtype)
    mixed = jnp.einsum('bsgc,gcd->bsgd', pooled, w_pool).reshape(b, s, POOL_WIDTH)
    return mixed * pool_scale

def setup_inputs(seed: int = 0) -> dict:
    key = jax.random.key(seed)
    ks = jax.random.split(key, 24)
    n = lambda k, shape, s: jax.random.normal(k, shape, jnp.float32) * s
    L = DEPTH
    return {
        "x": n(ks[0], (BATCH, SEQ, D_MODEL), 1.0),
        "c": n(ks[1], (BATCH, D_MODEL), 1.0),
        "w_ada": n(ks[2], (L, D_MODEL, N_MOD * D_MODEL), D_MODEL ** -0.5),
        "b_ada": n(ks[3], (L, N_MOD * D_MODEL), 0.02),
        "g_pre_mix": 1.0 + n(ks[4], (L, D_MODEL), 0.05),
        "g_post_mix": 1.0 + n(ks[5], (L, D_MODEL), 0.05),
        "w_in": n(ks[6], (L, D_MODEL, IN_WIDTH), D_MODEL ** -0.5),
        "cmp_pe_k": n(ks[7], (L, CMP_BLOCK, HEAD_DIM), 0.1),
        "cmp_w1_k": n(ks[8], (L, CMP_BLOCK * HEAD_DIM, HEAD_DIM), (CMP_BLOCK * HEAD_DIM) ** -0.5),
        "cmp_w2_k": n(ks[9], (L, HEAD_DIM, HEAD_DIM), HEAD_DIM ** -0.5),
        "cmp_pe_v": n(ks[10], (L, CMP_BLOCK, HEAD_DIM), 0.1),
        "cmp_w1_v": n(ks[11], (L, CMP_BLOCK * HEAD_DIM, HEAD_DIM), (CMP_BLOCK * HEAD_DIM) ** -0.5),
        "cmp_w2_v": n(ks[12], (L, HEAD_DIM, HEAD_DIM), HEAD_DIM ** -0.5),
        "w_pool": n(ks[13], (L, len(POOL_SIZES), POOL_GROUP, POOL_GROUP), POOL_GROUP ** -0.5),
        "pool_scale": 1.0 + n(ks[14], (L, POOL_WIDTH), 0.1),
        "w_br_nsa": n(ks[15], (L, NSA_WIDTH, D_MODEL), NSA_WIDTH ** -0.5),
        "w_br_pool": n(ks[16], (L, POOL_WIDTH, D_MODEL), POOL_WIDTH ** -0.5),
        "w_out": n(ks[17], (L, D_MODEL, D_MODEL), D_MODEL ** -0.5),
        "g_pre_mlp": 1.0 + n(ks[18], (L, D_MODEL), 0.05),
        "g_post_mlp": 1.0 + n(ks[19], (L, D_MODEL), 0.05),
        "w_fc1": n(ks[20], (L, D_MODEL, D_FF), D_MODEL ** -0.5),
        "w_fc2": n(ks[21], (L, D_FF, D_MODEL), D_FF ** -0.5),
    }

def reference(x, c, w_ada, b_ada, g_pre_mix, g_post_mix, w_in, cmp_pe_k, cmp_w1_k, cmp_w2_k,
              cmp_pe_v, cmp_w1_v, cmp_w2_v, w_pool, pool_scale, w_br_nsa, w_br_pool, w_out,
              g_pre_mlp, g_post_mlp, w_fc1, w_fc2):
    b, s, _ = x.shape
    for l in range(DEPTH):
        mod = (jax.nn.silu(c) @ w_ada[l] + b_ada[l]).astype(x.dtype)[:, None, :]
        sh1, sc1, gt1, sh2, sc2, gt2 = jnp.split(mod, N_MOD, axis=-1)

        h = rms_norm(x, g_pre_mix[l]) * (1.0 + sc1) + sh1
        proj = h @ w_in[l]
        q, kc, vc, ksl, vsl, kwn, vwn, nsa_g, u, br_g = jnp.split(proj, IN_SPLITS, axis=-1)
        kv = lambda a: a.reshape(b, s, N_KV, HEAD_DIM)
        q = rope(q.reshape(b, s, N_HEADS, HEAD_DIM))
        kc_c = compress(rope(kv(kc)), cmp_pe_k[l], cmp_w1_k[l], cmp_w2_k[l])
        vc_c = compress(kv(vc), cmp_pe_v[l], cmp_w1_v[l], cmp_w2_v[l])
        o_nsa = nsa_attention(q, kc_c, vc_c, rope(kv(ksl)), kv(vsl), rope(kv(kwn)), kv(vwn),
                              nsa_g.reshape(b, s, N_HEADS, 3))
        o_pool = pool_mixer(u, w_pool[l], pool_scale[l])
        gate_a, gate_b = jnp.split(jax.nn.sigmoid(br_g), 2, axis=-1)
        merged = gate_a * (o_nsa @ w_br_nsa[l]) + gate_b * (o_pool @ w_br_pool[l])
        y = merged @ w_out[l]
        x = x + gt1 * rms_norm(y, g_post_mix[l])

        h = rms_norm(x, g_pre_mlp[l]) * (1.0 + sc2) + sh2
        y = jnp.square(jax.nn.relu(h @ w_fc1[l])) @ w_fc2[l]
        x = x + gt2 * rms_norm(y, g_post_mlp[l])
    return x


_drawn_inputs = setup_inputs


def setup_inputs(seed=0):
    import zlib

    import numpy as np

    out = dict(_drawn_inputs(seed))
    spreads = {}
    factors = {'cmp_pe_k': 22.013, 'cmp_pe_v': 3.37}
    for name, (base, spread) in spreads.items():
        noise = np.random.default_rng([zlib.crc32(name.encode()), seed]).standard_normal(out[name].shape)
        drawn = base * np.exp(spread * noise) if base else spread * noise
        out[name] = __import__('jax').numpy.asarray(drawn.astype(out[name].dtype))
    for name, factor in factors.items():
        out[name] = (out[name] * factor).astype(out[name].dtype)
    return out
```

```python
import numpy as np
import concourse.bass as bass
from concourse import mybir

D_MODEL, SEQ, D_FF = 1024, 1024, 4096
N_HEADS, HEAD_DIM, KV_WIDTH = 8, 64, 128
CMP_BLOCK, CMP_STRIDE, WINDOW, SEL_BLOCK, SEL_TOPK = 32, 16, 512, 64, 16
POOL_SIZES = (2, 4, 8, 16)
POOL_WIDTH = 512
EPS = 1e-6
P = 128
KT = D_MODEL // P
TT = SEQ // P
CH = 512
N_CMP = (SEQ - CMP_BLOCK) // CMP_STRIDE + 1
NEG = -1e30
assert SEQ // SEL_BLOCK <= SEL_TOPK

C_Q, C_KC, C_VC, C_KS, C_VS, C_KW, C_VW, C_G, C_U, C_BR = 0, 512, 640, 768, 896, 1024, 1152, 1280, 1304, 1816
N_GATE = 3 * N_HEADS
WV_COLS = 2 * KV_WIDTH + N_GATE

FM_COLS = [C_KC, C_VC, C_KS, C_KW] + [C_Q + P * i for i in range(4)] + [C_U + P * i for i in range(4)] \
    + [C_BR + P * i for i in range(16)]
FM_ROPE = {0: 0, 2: 1, 3: 2, 4: 3, 5: 4, 6: 5, 7: 6}
N_FM = 12
N_BR = 16
UNITS = TT * N_HEADS // 2
STEPS = 5

R_WV, R_FM, R_MERGE, R_OUT, R_MLP = 0, 3, 3 + N_FM + N_BR, 11 + N_FM + N_BR, 19 + N_FM + N_BR
A_MERGE, A_MLP = N_FM + N_BR, N_FM + N_BR + KT


def raw_dmas(r):
    return 2 if r < R_FM or R_MERGE <= r < R_OUT else 1


def raw_count(r):
    return 16 * sum(raw_dmas(x) for x in range(r % 2, r + 1, 2))


def merge_free(i, b):
    return 4 * i + (2 * b - 2)


def key_tiles(c):
    first = max(0, c - WINDOW // P)
    return [(0, j) for j in range(c + 1)] + [(1, j) for j in range(first, c + 1)] + [(2, 0)]


def n_banks(u):
    return (len(key_tiles(u // 4)) + 1) // 2


BANKS_BEFORE = [sum(n_banks(v) for v in range(u)) for u in range(UNITS + 1)]


def portion(u, s):
    n = n_banks(u) + 1
    return range(s * n // STEPS, (s + 1) * n // STEPS)


def score_parts(c, branch):
    first = max(0, c - WINDOW // P) * P if branch else 0
    width = (c + 1) * P - first
    if width <= CH:
        return [(first, width, 0)]
    return [(first, width // 2, 0), (first + width // 2, width // 2, CH)]


def hybrid_block(nc, A, out):
    f32, f32r, bf16 = mybir.dt.float32, mybir.dt.float32r, mybir.dt.bfloat16
    ALU, ACT, AX = mybir.AluOpType, mybir.ActivationFunctionType, mybir.AxisListType

    def place(name, kb, shape, dt):
        pad = nc.sbuf_tensor(name + "_pad", [P, int(kb * 1024)], mybir.dt.uint8) if kb else None
        if pad:
            pad.__enter__()
        guard = nc.sbuf_tensor(name, shape, dt)
        t = guard.__enter__()
        guard.__exit__(None, None, None)
        if pad:
            pad.__exit__(None, None, None)
        return t

    def sem(name):
        return nc.semaphore(name).__enter__()

    def full(t):
        return t.bitcast(f32)

    ident = place("ident", 0, [P, P], f32)
    ones = place("ones", 0.5, [P, P], f32)
    ident_b = place("ident_b", 1, [P, P], bf16)
    mask_diag = place("mask_diag", 1.25, [P, P], bf16)
    mask_far = place("mask_far", 1.5, [P, P], bf16)
    mask_cmp = place("mask_cmp", 1.75, [P, TT, 64], bf16)
    gates = place("gates", 2.75, [P, TT, N_GATE], f32)
    col = place("col", 3.5, [P, 128], f32)
    c_col, silu_c, g_pre = col[:, 0:8], col[:, 8:16], col[:, 16:24]
    g_mlp, pool_sc, shift, scale = col[:, 24:32], col[:, 32:36], col[:, 40:48], col[:, 48:56]
    msq, rstd, half_neg = col[:, 56:64], col[:, 64:72], col[:, 72:76]
    stat = col[:, 80:128]
    smax = place("smax", 4, [P, 4, 2], f32)
    negm = place("negm", 4.125, [P, 4, 2], f32)
    ssum = place("ssum", 4.25, [P, 4, 2], f32)
    srec = place("srec", 4.375, [P, 4, 2], f32)
    inv_cnt = place("inv_cnt", 4.5, [P, 4, 16], f32)
    pe_col = place("pe_col", 4.75, [P, 2, 16], f32)
    w2k = place("w2k", 5, [64, 64], f32)
    w2v = place("w2v", 5.25, [64, 64], f32)
    gelu_x = place("gelu_x", 5.5, [64, 2, 126], f32)
    gelu_t = place("gelu_t", 6.5, [64, 2, 126], f32)
    raw = place("raw", 8, [P, 2, 1024], f32)
    a_hi = place("a_hi", 16, [P, 2, 1024], f32r)
    a_lo = place("a_lo", 24, [P, 2, 1024], f32r)
    act_hi = place("act_hi", 32, [P, KT, SEQ], f32r)
    act_lo = place("act_lo", 64, [P, KT, SEQ], f32r)
    k_hi = place("k_hi", 96, [P, 4, SEQ], f32r)
    k_lo = place("k_lo", 112, [P, 4, SEQ], f32r)
    v_st = place("v_st", 128, [P, TT, 4, P], f32r)
    kc_hi = place("kc_hi", 144, [P, 2, 64], f32r)
    kc_lo = place("kc_lo", 144.5, [P, 2, 64], f32r)
    vc_st = place("vc_st", 145, [P, 2, P], f32r)
    xt = place("xt", 96, [P, TT, D_MODEL], f32)
    ada = place("ada", 128, [P, 4, 1024], f32)
    ada_acc = place("ada_acc", 146, [P, 2048], f32)
    h_tmp = place("h_tmp", 154, [P, 2, CH], f32)
    junk = place("junk", 166, [P, 1024], f32)
    kc_f = place("kc_f", 146, [P, SEQ], f32)
    vc_f = place("vc_f", 150, [P, SEQ], f32)
    cw1 = place("cw1", 154, [P, 16, 64], f32)
    cos = place("cos", 158, [P, SEQ], f32)
    sin = place("sin", 162, [P, SEQ], f32)
    r_swap = place("r_swap", 166, [P, 2, CH], f32)
    r_cos = place("r_cos", 170, [P, 2, CH], f32)
    r_sin = place("r_sin", 174, [P, 2, CH], f32)
    r_hi = place("r_hi", 178, [P, 2, CH], f32r)
    r_lo = place("r_lo", 182, [P, 2, CH], f32r)
    wv_hi = place("wv_hi", 186, [P, KT, WV_COLS], f32r)
    wv_lo = place("wv_lo", 194.75, [P, KT, WV_COLS], f32r)
    bkx = place("bkx", 186, [P, 2, SEQ], f32)
    bk = place("bk", 194, [P, 16, 2, N_CMP], f32)
    PAD = 16
    pu = place("pu", 186, [P, PAD + SEQ], f32)
    ps_ab = [place("ps_a", 190.25, [P, PAD + SEQ], f32), place("ps_b", 194.5, [P, PAD + SEQ], f32)]
    pp_hi = place("pp_hi", 198.75, [P, SEQ], f32r)
    pp_lo = place("pp_lo", 202.75, [P, SEQ], f32r)
    wp_raw = place("wp_raw", 166, [P, 4, P], f32)
    wp_hi = place("wp_hi", 168, [P, 4, P], f32r)
    wp_lo = place("wp_lo", 170, [P, 4, P], f32r)
    pm = place("pm", 172, [P, 2, CH], f32)
    q_st = place("q_st", 146, [P, 2, N_HEADS, P], f32r)
    p_sel = place("p_sel", 154, [P, 2, 2, SEQ], f32)
    p_win = place("p_win", 170, [P, 2, 2, 640], f32)
    p_cmp = place("p_cmp", 180, [P, 2, 2, P], f32)
    pt_hi = place("pt_hi", 182, [P, 3, CH], f32r)
    pt_lo = place("pt_lo", 188, [P, 3, CH], f32r)
    o_tmp = place("o_tmp", 194, [64, 2, 256], f32)
    o_out = place("o_out", 196, [64, 2, 256], f32)
    g_out = place("g_out", 198, [P, 2, CH], f32)
    op_hi = place("op_hi", 96, [P, KT, SEQ], f32r)
    op_lo = place("op_lo", 128, [P, KT, SEQ], f32r)
    stage = place("stage", 160, [P, 2, 1024], f32)
    ada_acc2 = place("ada_acc2", 168, [P, 4, 1024], f32)
    mg = place("mg", 184, [P, 2, 2, CH], f32)
    m_a = place("m_a", 192, [P, 2, CH], f32)
    m_b = place("m_b", 196, [P, 2, CH], f32)
    b_hi = place("b_hi", 96, [P, 4, 1024], f32r)
    b_lo = place("b_lo", 112, [P, 4, 1024], f32r)
    y = place("y", 128, [P, TT, D_MODEL], f32)
    gt1 = place("gt1", 160, [P, 1024], f32)
    gt2 = place("gt2", 164, [P, 1024], f32)
    x_in = place("x_in", 184, [P, 2, 1024], f32)
    h2_tmp = place("h2_tmp", 180, [P, 2, CH], f32)
    x1 = place("x1", 192, [P, 2, 1024], f32)
    y_sq = place("y_sq", 200, [P, 1024], f32)
    hid_hi = place("hid_hi", 168, [P, 4, SEQ], f32r)
    hid_lo = place("hid_lo", 184, [P, 4, SEQ], f32r)
    relu = place("relu", 200, [P, 2, CH], f32)
    x1_in = place("x1_in", 32, [P, 2, 1024], f32)
    fin = place("fin", 40, [P, 2, 1024], f32)

    ps = nc.psum_tensor("ps", [P, 8, CH], f32).__enter__()

    q_dram = nc.dram_tensor("q_dram", (TT, P, N_HEADS, P), f32, kind="Internal").ap()
    pool_dram = nc.dram_tensor("pool_dram", (POOL_WIDTH, SEQ), f32, kind="Internal").ap()
    o_dram = nc.dram_tensor("o_dram", (N_HEADS * HEAD_DIM, SEQ), f32, kind="Internal").ap()
    g_dram = nc.dram_tensor("g_dram", (2, KT, 2, P, CH), f32, kind="Internal").ap()
    x1_dram = nc.dram_tensor("x1_dram", (SEQ, D_MODEL), f32, kind="Internal").ap()

    x_v = A["x"][0].rearrange("(t p) d -> p t d", p=P)
    x1_v = x1_dram.rearrange("(t p) d -> p t d", p=P)
    out_v = out[0].rearrange("(t p) d -> p t d", p=P)
    w_ada, b_ada = A["w_ada"][0], A["b_ada"]
    w_in_v = A["w_in"][0].rearrange("(k p) n -> p k n", p=P)
    w_brn_v = A["w_br_nsa"][0].rearrange("(k p) n -> p k n", p=P)
    w_brp_v = A["w_br_pool"][0].rearrange("(k p) n -> p k n", p=P)
    w_out_v = A["w_out"][0].rearrange("(k p) n -> p k n", p=P)
    w_fc1_v = A["w_fc1"][0].rearrange("(k p) n -> p k n", p=P)
    w_fc2_v = A["w_fc2"][0].rearrange("(k p) n -> p k n", p=P)

    const_in, cos_in, wp_in = sem("const_in"), sem("cos_in"), sem("wp_in")
    consts_made, acc_zero, acc_bias = sem("consts_made"), sem("acc_zero"), sem("acc_bias")
    silu_t, silu_done = sem("silu_t"), sem("silu_done")
    ada_in = [sem(f"ada_in{i}") for i in range(4)]
    ada_added, mod_mm, mod_done = sem("ada_added"), sem("mod_mm"), sem("mod_done")
    x_arr = [sem(f"x_arr{i}") for i in range(TT)]
    x_sq, x_ms, x_rstd, x_norm = sem("x_sq"), sem("x_ms"), sem("x_rstd"), sem("x_norm")
    xt_mm, h_made, h_hi, h_lo = sem("xt_mm"), sem("h_made"), sem("h_hi"), sem("h_lo")
    raw_in = [sem("raw_in0"), sem("raw_in1")]
    hi_done, lo_done = sem("hi_done"), sem("lo_done")
    v_mm, v_hi, v_lo = sem("v_mm"), sem("v_hi"), sem("v_lo")
    fm_mm, fm_act = sem("fm_mm"), sem("fm_act")
    rope_cos, rope_sin, rope_sum, rope_hi, rope_lo = (sem("rope_" + n) for n in ("cos", "sin", "sum", "hi", "lo"))
    rope_out = [sem("rope_out0"), sem("rope_out1")]
    cw_in, bkx_in, bk_made = sem("cw_in"), sem("bkx_in"), sem("bk_made")
    cmp_mm, gelu_c, gelu_d, cmp2_mm = sem("cmp_mm"), sem("gelu_c"), sem("gelu_d"), sem("cmp2_mm")
    cmp_hi, cmp_lo = sem("cmp_hi"), sem("cmp_lo")
    pool_zero, pool_add, pooled, pooled_hi, pooled_lo = (
        sem(n) for n in ("pool_zero", "pool_add", "pooled", "pooled_hi", "pooled_lo"))
    wp_hi_s, wp_lo_s, mix_mm, mix_out = sem("wp_hi_s"), sem("wp_lo_s"), sem("mix_mm"), sem("mix_out")
    mix_st = [sem("mix_st0"), sem("mix_st1")]
    gates_done, cmp_zero = sem("gates_done"), sem("cmp_zero")
    q_in = [sem("q_in0"), sem("q_in1")]
    score_mm, max_done, negm_done, exp_done, guard_done, rec_done, norm_done = (
        sem(n) for n in ("score_mm", "max_done", "negm_done", "exp_done", "guard_done", "rec_done", "norm_done"))
    tp_mm, pthi, ptlo, pv_mm = (sem(n) for n in ("tp_mm", "pthi", "ptlo", "pv_mm"))
    o_half, o_sum, gate_mm, gate_tanh = sem("o_half"), sem("o_sum"), sem("gate_mm"), sem("gate_tanh")
    o_st = [sem("o_st0"), sem("o_st1")]
    g_st = [sem("g_st0"), sem("g_st1")]
    stage_in = [sem("stage_in0"), sem("stage_in1")]
    op_hi_s, op_lo_s, acc2_zero, acc2_bias, ada2_added = (
        sem(n) for n in ("op_hi_s", "op_lo_s", "acc2_zero", "acc2_bias", "ada2_added"))
    mg_in = [sem("mg_in0"), sem("mg_in1")]
    merge_mm, merge_ab, merge_sum, merge_hi, merge_lo = (
        sem(n) for n in ("merge_mm", "merge_ab", "merge_sum", "merge_hi", "merge_lo"))
    gp_in, bc_mm, mod2_mm, g_made, mod2_done = (
        sem(n) for n in ("gp_in", "bc_mm", "mod2_mm", "g_made", "mod2_done"))
    pooled_w, y_gated, x1n_made, f_gated = sem("pooled_w"), sem("y_gated"), sem("x1n_made"), sem("f_gated")
    y_mm, y_out, y_ms, y_rstd, y_scaled, x1_made, x1_ms, x1_rstd, x1_norm = (
        sem(n) for n in ("y_mm", "y_out", "y_ms", "y_rstd", "y_scaled", "x1_made", "x1_ms", "x1_rstd", "x1_norm"))
    xi_in = [sem("xi_in0"), sem("xi_in1")]
    x1_st = [sem("x1_st0"), sem("x1_st1")]
    x1t_mm, h2_made, h2_hi, h2_lo = sem("x1t_mm"), sem("h2_made"), sem("h2_hi"), sem("h2_lo")
    fc1_mm, relu_done, sq_done, hid_hi_s, hid_lo_s = (
        sem(n) for n in ("fc1_mm", "relu_done", "sq_done", "hid_hi_s", "hid_lo_s"))
    fc2_mm, y2_added = sem("fc2_mm"), sem("y2_added")
    x1i_in = [sem("x1i_in0"), sem("x1i_in1")]
    f_ms, f_rstd, f_scaled, f_made = sem("f_ms"), sem("f_rstd"), sem("f_scaled"), sem("f_made")
    out_st = [sem("out_st0"), sem("out_st1")]

    N_SMALL, CONSTS = 9, 12
    ROPES = 2 * len(FM_ROPE)
    K_DMAS, Q_DMAS = 8, 4

    def rope_out_count(i):
        return 16 * sum((K_DMAS if j < 6 else Q_DMAS) for j in range(2 + i % 2, i + 1, 2))

    block = nc.Block().__enter__()

    @block.sync
    def _(sp):
        def load_raw(r, count_only=False, **src):
            if r >= 2:
                sp.wait_ge(lo_done, r - 1)
            for dst, s in src["parts"]:
                sp.dma_start(dst, s).then_inc(raw_in[r % 2], 16)

        def raw_k(r):
            return raw[:, r % 2, :].rearrange("p (k n) -> p k n", n=P)

        def ada_piece(n):
            if n >= 4:
                sp.wait_ge(ada_added, n - 3)
            sp.dma_start(ada[:, n % 4, :], w_ada[(n // 2) * P:(n // 2 + 1) * P, (n % 2) * 1024:(n % 2 + 1) * 1024]) \
              .then_inc(ada_in[n % 4], 16)

        for dst, s in ((c_col, A["c"].rearrange("a (k p) -> p (a k)", p=P)),
                       (g_pre, A["g_pre_mix"].rearrange("a (k p) -> p (a k)", p=P)),
                       (g_mlp, A["g_pre_mlp"].rearrange("a (k p) -> p (a k)", p=P)),
                       (pool_sc, A["pool_scale"].rearrange("a (k p) -> p (a k)", p=P)),
                       (inv_cnt[:, :, :], A["inv_cnt"]),
                       (pe_col[:, 0, :], A["cmp_pe_k"][0].rearrange("(l two) d -> (two d) l", two=2)),
                       (pe_col[:, 1, :], A["cmp_pe_v"][0].rearrange("(l two) d -> (two d) l", two=2)),
                       (w2k[:, :], A["cmp_w2_k"][0]), (w2v[:, :], A["cmp_w2_v"][0])):
            if len(dst.shape) == 2 and dst.shape[0] == P and dst.shape[1] <= 16:
                with nc.allow_non_contiguous_dma(reason="a few columns"):
                    sp.dma_start(dst, s).then_inc(const_in, 16)
            else:
                sp.dma_start(dst, s).then_inc(const_in, 16)
        for n in range(4):
            ada_piece(n)
        sp.wait_ge(acc_zero, 1)
        sp.dma_start(ada_acc[0:1, :], b_ada[:, 0:2048]).then_inc(acc_bias, 16)
        for n in range(4, 16):
            ada_piece(n)
            if n % 2:
                t = n // 2 - 2
                sp.dma_start(xt[:, t, :], x_v[:, t, :]).then_inc(x_arr[t], 16)
        for t in (6, 7):
            sp.dma_start(xt[:, t, :], x_v[:, t, :]).then_inc(x_arr[t], 16)
        for r, (k0, k1) in enumerate(((0, 3), (3, 6), (6, 8))):
            dst = raw[:, r % 2, 0:(k1 - k0) * WV_COLS].rearrange("p (k n) -> p k n", n=WV_COLS)
            load_raw(r, parts=((dst[:, :, 0:P], w_in_v[:, k0:k1, C_VS:C_VS + P]),
                               (dst[:, :, P:WV_COLS], w_in_v[:, k0:k1, C_VW:C_VW + P + N_GATE])))
        sp.dma_start(cos[:, :], A["cos"]).then_inc(cos_in, 16)
        sp.dma_start(sin[:, :], A["sin"]).then_inc(cos_in, 16)

        def rope_stores(a):
            for ch in range(2):
                i = 2 * FM_ROPE[a] + ch
                sp.wait_ge(rope_lo, i - 1)
                for part, kd in ((r_hi, k_hi), (r_lo, k_lo)):
                    for g in range(2):
                        src = full(part[64 * g:64 * g + 64, i % 2, :])
                        if a in (2, 3):
                            for half in range(2):
                                sp.dma_start(full(kd[64 * half:64 * half + 64, 2 * (a - 2) + g, ch * CH:(ch + 1) * CH]),
                                             src).then_inc(rope_out[i % 2], 16)
                        else:
                            row = 0 if part is r_hi else 64
                            sp.dma_start(q_dram[4 * ch:4 * ch + 4, row:row + 64, 2 * (a - 4) + g, :]
                                         .rearrange("c d q -> d c q"),
                                         src.rearrange("d (c q) -> d c q", q=P)).then_inc(rope_out[i % 2], 16)

        def cmp_load(kv):
            if kv:
                sp.wait_ge(cmp_mm, 1)
            else:
                sp.wait_ge(h_lo, 16)
            sp.dma_start(cw1[:, :, :], A["cmp_w1_v" if kv else "cmp_w1_k"][0]
                         .rearrange("(l p) j -> p l j", p=P)).then_inc(cw_in, 16)
            if kv:
                sp.wait_ge(fm_act, 4)
                sp.wait_ge(bk_made, 1)
            else:
                sp.wait_ge(rope_sum, 2)
                sp.wait_ge(v_mm, TT)
            src = vc_f if kv else kc_f
            for g in range(2):
                for odd in range(2):
                    sp.dma_start(bkx[64 * odd:64 * odd + 64, g, 0:SEQ - odd],
                                 src[64 * g:64 * g + 64, odd:SEQ]).then_inc(bkx_in, 16)

        for a in range(N_FM):
            r = R_FM + a
            load_raw(r, parts=((raw_k(r), w_in_v[:, :, FM_COLS[a]:FM_COLS[a] + P]),))
            if a == 3:
                cmp_load(0)
            if a - 2 in FM_ROPE and a - 2 != 0:
                rope_stores(a - 2)
            if a == 5:
                cmp_load(1)
            if a == N_FM - 1:
                sp.wait_ge(rope_sum, ROPES)
                sp.wait_ge(rope_lo, ROPES - 2)
                sp.dma_start(wp_raw[:, :, :], A["w_pool"][0].rearrange("g c d -> c g d")).then_inc(wp_in, 16)

        def load_q(c):
            if c == 0:
                for s in range(2):
                    sp.wait_ge(rope_out[s], rope_out_count(ROPES - 2 + s))
                sp.wait_ge(bkx_in, 128)
            if c >= 2:
                sp.wait_ge(score_mm, STEPS * 4 * (c - 1))
            sp.dma_start(full(q_st[:, c % 2, :, :]), q_dram[c]).then_inc(q_in[c % 2], 16)

        load_q(0)
        load_q(1)
        for m in range(N_BR):
            r = R_FM + N_FM + m
            load_raw(r, parts=((raw_k(r), w_in_v[:, :, FM_COLS[N_FM + m]:FM_COLS[N_FM + m] + P]),))
            if m % 2 == 1 and m // 2 + 1 < TT and m >= 3:
                load_q(m // 2 + 1)

        def load_merge(m):
            r0 = R_MERGE % 2
            for b in range(2):
                sp.wait_ge(lo_done, m + (R_MERGE + b - 1))
                dst = raw_k(r0 + b)
                cols = bass.ds((m + b) * P, P)
                sp.dma_start(dst[:, 0:4, :], w_brp_v[:, :, cols]).then_inc(raw_in[(r0 + b) % 2], 16)
                sp.dma_start(dst[:, 4:8, :], w_brn_v[:, :, cols]).then_inc(raw_in[(r0 + b) % 2], 16)

        def merge_loads(i, first=False):
            load_merge(2 * i)
            for b in range(2):
                for ch in range(2):
                    if not (b == 0 and first):
                        sp.wait_ge(merge_ab, 4 * i + (2 * b + ch - 1))
                    sp.dma_start(mg[:, ch, :, :], g_dram[:, bass.ds(2 * i + b, 1), ch, :, :]
                                 .rearrange("h m p n -> p (h m) n")).then_inc(mg_in[ch], 16)
                for part in range(4):
                    s = part % 2
                    if first and b == 0 and part < 2:
                        sp.wait_ge(op_lo_s, 7 + part)
                    else:
                        sp.wait_ge(ada2_added, 8 * i + (4 * b + part - 1))
                    sp.dma_start(stage[:, s, :], w_ada[bass.ds((2 * i + b) * P, P), 2048 + part * 1024:3072 + part * 1024]) \
                      .then_inc(stage_in[s], 16)

        sp.wait_ge(pv_mm, BANKS_BEFORE[UNITS])
        for s in range(2):
            sp.wait_ge(mix_st[s], 16 * 4)
        for i in range(8):
            if i == 4:
                for s in range(2):
                    sp.wait_ge(o_st[s], 16 * UNITS // 2)
            if i >= 2:
                sp.wait_ge(op_lo_s, i - 1)
            src = pool_dram if i < 4 else o_dram
            sp.dma_start(stage[:, i % 2, :], src[(i % 4) * P:(i % 4 + 1) * P, :]).then_inc(stage_in[i % 2], 16)
        for s in range(2):
            sp.wait_ge(g_st[s], 16 * UNITS // 2)
        sp.wait_ge(acc2_zero, 1)
        sp.dma_start(ada_acc2[0:1, :, :], b_ada[:, 2048:6144].rearrange("a (f n) -> a f n", n=1024)) \
          .then_inc(acc2_bias, 16)
        merge_loads(0, first=True)
        with sp.Fori(1, KT // 2) as i:
            merge_loads(i)

        for n in range(8):
            r, half, s = R_OUT + n, n // 4, n % 4
            sp.wait_ge(lo_done, r - 1)
            sp.dma_start(raw[:, r % 2, :].rearrange("p (k n) -> p k n", n=CH),
                         w_out_v[:, 2 * s:2 * s + 2, half * CH:(half + 1) * CH]).then_inc(raw_in[r % 2], 16)
            if n == 2:
                sp.wait_ge(ada2_added, 32)
                for g, dst in (("g_post_mix", gt1), ("g_post_mlp", gt2)):
                    sp.dma_start(dst[:, :], A[g].to_broadcast([P, D_MODEL])).then_inc(gp_in, 16)
                sp.wait_ge(merge_lo, 2 * KT)
                for t in range(2):
                    sp.dma_start(x_in[:, t, :], x_v[:, t, :]).then_inc(xi_in[t], 16)

        def mlp_loads(j, ns=range(8)):
            for n in ns:
                sp.wait_ge(lo_done, 8 * j + (R_MLP + n - 1))
                s = (R_MLP + n) % 2
                if n < 4:
                    src = w_fc1_v[:, :, bass.ds(j * CH + n * P, P)]
                    sp.dma_start(raw_k(s), src).then_inc(raw_in[s], 16)
                else:
                    sp.dma_start(raw[:, s, :], w_fc2_v[:, bass.ds(4 * j + (n - 4), 1), :]
                                 .rearrange("p k n -> p (k n)")).then_inc(raw_in[s], 16)

        for t in range(2, TT):
            sp.wait_ge(x1_made, t - 1)
            sp.dma_start(x_in[:, t % 2, :], x_v[:, t, :]).then_inc(xi_in[t % 2], 16)
            if t == 5:
                mlp_loads(0, range(0, 2))
        mlp_loads(0, range(2, 8))
        with sp.Fori(1, D_FF // CH) as j:
            mlp_loads(j)
        sp.wait_ge(fc1_mm, 8 * (D_FF // CH))
        for s in range(2):
            sp.wait_ge(x1_st[s], 16 * TT // 2)
        for t in range(TT):
            if t >= 2:
                sp.wait_ge(f_made, t - 1)
            sp.dma_start(x1_in[:, t % 2, :], x1_v[:, t, :]).then_inc(x1i_in[t % 2], 16)
        for s in range(2):
            sp.wait_ge(out_st[s], 16 * TT // 2)

    @block.gpsimd
    def _(pool):
        def made(ins):
            made.n += 1
            ins.then_inc(consts_made, 1)
        made.n = 0
        pool.memset(ada_acc[:, :], 0.0).then_inc(acc_zero, 1)
        for t, v in ((ident, 0.0), (ident_b, 0.0), (mask_diag, 0.0), (mask_far, 0.0), (ones, 1.0), (half_neg, -0.5)):
            made(pool.memset(t if t is half_neg else t[:, :], v))
        made(pool.memset(mask_cmp[:, :, :], 0.0))
        pool.wait_ge(consts_made, made.n)
        for t in (ident, ident_b):
            made(pool.affine_select(out=t[:, :], in_=t[:, :], compare_op=ALU.not_equal, fill=1.0,
                                    base=0, pattern=[[-1, P]], channel_multiplier=1))
        made(pool.affine_select(out=mask_diag[:, :], in_=mask_diag[:, :], compare_op=ALU.is_ge, fill=NEG,
                                base=0, pattern=[[-1, P]], channel_multiplier=1))
        made(pool.affine_select(out=mask_far[:, :], in_=mask_far[:, :], compare_op=ALU.is_gt, fill=NEG,
                                base=0, pattern=[[1, P]], channel_multiplier=-1))
        made(pool.affine_select(out=mask_cmp[:, :, :], in_=mask_cmp[:, :, :], compare_op=ALU.is_ge, fill=NEG,
                                base=1 - CMP_BLOCK, pattern=[[P, TT], [-CMP_STRIDE, 64]], channel_multiplier=1))
        assert made.n == CONSTS
        pool.memset(full(kc_hi[:, :, :]), 0.0).then_inc(cmp_zero, 1)
        pool.memset(full(kc_lo[:, :, :]), 0.0).then_inc(cmp_zero, 1)
        pool.memset(full(vc_st[:, :, :]), 0.0).then_inc(cmp_zero, 1)
        for ch in range(2):
            sl = slice(4 * ch, 4 * ch + 4)
            pool.wait_ge(x_sq, 4 * ch + 4)
            pool.tensor_scalar(msq[:, sl], msq[:, sl], 1.0 / D_MODEL, EPS, ALU.mult, ALU.add).then_inc(x_ms, 1)
            pool.wait_ge(x_ms, ch + 1)
            pool.tensor_tensor(rstd[:, sl], msq[:, sl], half_neg, ALU.pow).then_inc(x_rstd, 1)
        pool.wait_ge(cos_in, 32)
        for a, k in FM_ROPE.items():
            for ch in range(2):
                i, sl = 2 * k + ch, slice(ch * CH, (ch + 1) * CH)
                pool.wait_ge(fm_act, 2 * a + ch + 1)
                pool.tensor_tensor(r_sin[:, i % 2, :], r_swap[:, i % 2, :], sin[:, sl], ALU.mult).then_inc(rope_sin, 1)
                pool.wait_ge(rope_sin, i + 1)
                pool.wait_ge(rope_cos, i + 1)
                dst = kc_f[:, sl] if a == 0 else r_cos[:, i % 2, :]
                pool.tensor_tensor(dst, r_cos[:, i % 2, :], r_sin[:, i % 2, :], ALU.add).then_inc(rope_sum, 1)
        pool.wait_ge(cmp_mm, 2)
        for t in (pu, ps_ab[0], ps_ab[1]):
            pool.memset(t[:, 0:PAD], 0.0).then_inc(pool_zero, 1)
        pool.wait_ge(pool_zero, 3)
        n_add = 0

        def mix_store(g):
            for n in (2 * g, 2 * g + 1):
                pool.wait_ge(mix_out, n + 1)
                pool.dma_start(pool_dram[g * P:(g + 1) * P, (n % 2) * CH:(n % 2 + 1) * CH],
                               pm[:, n % 2, :]).then_inc(mix_st[n % 2], 16)

        for g in range(4):
            pool.wait_ge(fm_act, 2 * (8 + g) + 2)
            if g:
                pool.wait_ge(pooled_lo, g)
            src = pu
            for step in range(g + 1):
                dst, back = ps_ab[step % 2], 1 << step
                if step:
                    pool.wait_ge(pool_add, n_add)
                pool.tensor_tensor(dst[:, PAD:], src[:, PAD:], src[:, PAD - back:PAD + SEQ - back], ALU.add) \
                    .then_inc(pool_add, 1)
                n_add += 1
                src = dst
            if g:
                mix_store(g - 1)
        mix_store(3)
        pool.wait_ge(rope_out[0], rope_out_count(ROPES - 2))
        pool.wait_ge(rope_out[1], rope_out_count(ROPES - 1))
        pool.memset(p_cmp[:, :, :, :], 0.0).then_inc(cmp_zero, 1)
        for u in range(UNITS + 1):
            if u < UNITS:
                pool.wait_ge(gate_tanh, u + 1)
                m = u // 2
                pool.dma_start(g_dram[m // KT, m % KT, u % 2], g_out[:, u % 2, :]).then_inc(g_st[u % 2], 16)
            if u:
                v = u - 1
                pool.wait_ge(o_sum, v + 1)
                c, pair = v // 4, v % 4
                pool.dma_start(o_dram[pair * P:(pair + 1) * P, c * P:(c + 1) * P].rearrange("(h d) q -> d h q", h=2),
                               o_out[:, v % 2, :].rearrange("d (h q) -> d h q", h=2)).then_inc(o_st[v % 2], 16)
        pool.wait_ge(pv_mm, BANKS_BEFORE[UNITS])
        pool.memset(ada_acc2[:, :, :], 0.0).then_inc(acc2_zero, 1)

        def merge_sums(i):
            for n in range(4):
                pool.wait_ge(merge_ab, 4 * i + (n + 1))
                pool.tensor_tensor(m_a[:, n % 2, :], m_a[:, n % 2, :], m_b[:, n % 2, :], ALU.add).then_inc(merge_sum, 1)

        merge_sums(0)
        with pool.Fori(1, KT // 2) as i:
            merge_sums(i)

        def rstd_of(ms, sem_in, sem_ms, sem_out, t):
            pool.wait_ge(sem_in, t + 1)
            pool.tensor_scalar(ms, ms, 1.0 / D_MODEL, EPS, ALU.mult, ALU.add).then_inc(sem_ms, 1)
            pool.wait_ge(sem_ms, t + 1)
            pool.tensor_tensor(ms, ms, half_neg[:, 0:1], ALU.pow).then_inc(sem_out, 1)

        for t in range(TT):
            rstd_of(stat[:, t:t + 1], y_ms, y_scaled, y_rstd, t)
            rstd_of(stat[:, 8 + t:9 + t], x1_ms, x1_norm, x1_rstd, t)
            pool.dma_start(x1_v[:, t, :], x1[:, t % 2, :]).then_inc(x1_st[t % 2], 16)

        def squares(j):
            for n in range(8):
                pool.wait_ge(relu_done, 8 * j + (n + 1))
                pool.tensor_tensor(relu[:, n % 2, :], relu[:, n % 2, :], relu[:, n % 2, :], ALU.mult).then_inc(sq_done, 1)

        squares(0)
        with pool.Fori(1, D_FF // CH) as j:
            squares(j)
        for t in range(TT):
            rstd_of(stat[:, 16 + t:17 + t], f_ms, f_scaled, f_rstd, t)
            pool.wait_ge(f_made, t + 1)
            pool.dma_start(out_v[:, t, :], fin[:, t % 2, :]).then_inc(out_st[t % 2], 16)

    @block.scalar
    def _(act):
        def split_hi(r, dst, free):
            act.wait_ge(raw_in[r % 2], raw_count(r))
            if free:
                act.wait_ge(*free)
            act.activation(dst, raw[:, r % 2, :], ACT.Copy).then_inc(hi_done, 1)

        def split_a(a):
            free = None
            if a >= 2:
                free = (fm_mm, 2 * a - 2) if a - 2 < N_FM else (gate_mm, 2 * (a - 2 - N_FM) + 2)
            split_hi(R_FM + a, a_hi[:, a % 2, :], free)

        act.wait_ge(const_in, 16 * N_SMALL)
        act.activation(silu_c, c_col, ACT.Tanh, scale=0.5).then_inc(silu_t, 1)
        for ch in range(2):
            for t in range(4 * ch, 4 * ch + 4):
                act.wait_ge(x_arr[t], 16)
                if t:
                    act.wait_ge(x_sq, t)
                act.activation(junk[:, :], xt[:, t, :], ACT.Square, accum_out=msq[:, t:t + 1]).then_inc(x_sq, 1)
        for r, (k0, k1) in enumerate(((0, 3), (3, 6), (6, 8))):
            act.wait_ge(raw_in[r % 2], raw_count(r))
            act.activation(wv_hi[:, k0:k1, :], raw[:, r % 2, 0:(k1 - k0) * WV_COLS]
                           .rearrange("p (k n) -> p k n", n=WV_COLS), ACT.Copy).then_inc(hi_done, 1)
        act.wait_ge(mod_done, 2)
        for n in range(2 * KT):
            act.wait_ge(xt_mm, n + 1)
            if n >= 2:
                act.wait_ge(h_lo, n - 1)
            k = n % KT
            act.activation(h_tmp[:, n % 2, :], ps[:, n % 4, :], ACT.Identity, scale=scale[:, k:k + 1],
                           bias=shift[:, k:k + 1]).then_inc(h_made, 1)
        split_a(0)
        split_a(1)
        for t in range(TT):
            b = 4 + t % 2
            act.wait_ge(v_mm, t + 1)
            act.activation(v_st[:, t, :, 0:64], ps[:, b, 0:256].rearrange("p (f d) -> p f d", d=64),
                           ACT.Copy).then_inc(v_hi, 1)
            act.activation(gates[:, t, :], ps[:, b, 256:WV_COLS], ACT.Tanh, scale=0.5).then_inc(v_hi, 1)

        def rope_hi_part(i):
            act.wait_ge(rope_sum, i + 1)
            if i >= 4:
                act.wait_ge(rope_out[i % 2], rope_out_count(i - 2))
            act.activation(r_hi[:, i % 2, :], r_cos[:, i % 2, :], ACT.Copy).then_inc(rope_hi, 1)

        def fm_evict(a, ch):
            g = 2 * a + ch
            act.wait_ge(fm_mm, g + 1)
            bank, sl = g % 4, slice(ch * CH, (ch + 1) * CH)
            if a in FM_ROPE:
                i = 2 * FM_ROPE[a] + ch
                if i >= 2:
                    act.wait_ge(rope_sin, i - 1)
                for q in range(4):
                    ins = act.activation(r_swap[32 * q:32 * q + 32, i % 2, :],
                                         ps[32 * (q ^ 1):32 * (q ^ 1) + 32, bank, :], ACT.Copy)
                ins.then_inc(fm_act, 1)
            elif a == 1:
                act.activation(vc_f[:, sl], ps[:, bank, :], ACT.Copy).then_inc(fm_act, 1)
            else:
                if ch == 0:
                    if a == 8:
                        act.wait_ge(pool_zero, 3)
                    else:
                        act.wait_ge(pooled_lo, a - 8)
                act.activation(pu[:, PAD + ch * CH:PAD + (ch + 1) * CH], ps[:, bank, :], ACT.Copy).then_inc(fm_act, 1)

        def gelu(kv):
            act.wait_ge(cmp_mm, kv + 1)
            act.activation(gelu_x[:, kv, :], ps[0:64, 6, P * kv:P * kv + 126], ACT.Copy).then_inc(gelu_c, 1)
            act.wait_ge(gelu_d, 5 * kv + 3)
            act.activation(gelu_t[:, kv, :], gelu_t[:, kv, :], ACT.Tanh, scale=float(np.sqrt(2 / np.pi))).then_inc(gelu_c, 1)

        def cmp_store():
            act.wait_ge(cmp_zero, 3)
            act.wait_ge(cmp2_mm, 2)
            for half in range(2):
                act.activation(kc_hi[64 * half:64 * half + 64, :, 0:N_CMP],
                               ps[0:64, 6, 256:382].rearrange("p (g n) -> p g n", g=2), ACT.Copy).then_inc(cmp_hi, 1)
            act.activation(vc_st[0:N_CMP, :, 0:64], ps[0:N_CMP, 6, 384:512].rearrange("p (g d) -> p g d", g=2),
                           ACT.Copy).then_inc(cmp_hi, 1)

        def pooled_hi_part(g):
            act.wait_ge(pooled, 2 * g + 2)
            if g:
                act.wait_ge(mix_mm, 2 * g)
            act.activation(pp_hi[:, :], ps_ab[(g + 1) % 2][:, PAD:], ACT.Copy).then_inc(pooled_hi, 1)

        def mix_evict(g):
            for ch in range(2):
                n = 2 * g + ch
                act.wait_ge(mix_mm, n + 1)
                if n >= 2:
                    act.wait_ge(mix_st[n % 2], 16 * (n // 2))
                act.activation(pm[:, n % 2, :], ps[:, 4 + n % 2, :], ACT.Copy, scale=pool_sc[:, g:g + 1]) \
                    .then_inc(mix_out, 1)

        for a in range(N_FM):
            for ch in range(2):
                fm_evict(a, ch)
            if a in FM_ROPE and a:
                for ch in range(2):
                    rope_hi_part(2 * FM_ROPE[a] + ch)
            split_a(a + 2)
            if a == 5:
                gelu(0)
            if a == 7:
                gelu(1)
            if a == 8:
                cmp_store()
            if a == 8:
                act.wait_ge(wp_in, 16)
                act.activation(wp_hi[:, :, :], wp_raw[:, :, :], ACT.Copy).then_inc(wp_hi_s, 1)
            if a >= 8:
                pooled_hi_part(a - 8)
            if a >= 9:
                mix_evict(a - 9)
        mix_evict(3)

        def hi_banks(u, s):
            for b in portion(u, s):
                if b < n_banks(u):
                    n = BANKS_BEFORE[u] + b
                    act.wait_ge(tp_mm, n + 1)
                    if n >= 3:
                        act.wait_ge(pv_mm, n - 2)
                    w = 256 * min(2, len(key_tiles(u // 4)) - 2 * b)
                    act.activation(pt_hi[:, n % 3, 0:w], ps[:, 4 + n % 2, 0:w], ACT.Copy).then_inc(pthi, 1)

        act.wait_ge(cmp_zero, 4)
        for s in range(2):
            act.wait_ge(mix_st[s], 16 * 4)
        for u in range(UNITS + 1):
            for s in range(STEPS):
                if u < UNITS:
                    c, n = u // 4, STEPS * u + s
                    act.wait_ge(negm_done, n + 1)
                    if u >= 2 and s == 0:
                        act.wait_ge(tp_mm, BANKS_BEFORE[u - 1])
                    if s < 4:
                        hh, branch = s % 2, s // 2
                        parts = score_parts(c, branch)
                        w = parts[0][1]
                        buf = (p_sel, p_win)[branch]
                        src = ps[:, 2 * (n % 2):2 * (n % 2) + len(parts), 0:w]
                        dst = buf[:, u % 2, hh, 0:w * len(parts)].rearrange("p (a w) -> p a w", w=w)
                        act.activation(dst, src, ACT.Exp, bias=negm[:, n % 4, 0:1], scale=HEAD_DIM ** -0.5,
                                       accum_out=ssum[:, n % 4, 0:1]).then_inc(exp_done, 1)
                    else:
                        for hh in range(2):
                            ins = act.activation(p_cmp[:, u % 2, hh, 0:64], ps[:, 2 * (n % 2), 64 * hh:64 * hh + 64],
                                                 ACT.Exp, bias=negm[:, n % 4, hh:hh + 1], scale=HEAD_DIM ** -0.5,
                                                 accum_out=ssum[:, n % 4, hh:hh + 1])
                        ins.then_inc(exp_done, 1)
                    if s == 1 and u % 2 == 0 and 0 < u // 2 + 1 < N_BR and u // 2 >= 1:
                        split_a(N_FM + u // 2 + 1)
                if u:
                    hi_banks(u - 1, s)
            if u < UNITS:
                act.wait_ge(gate_mm, u + 1)
                if u >= 2:
                    act.wait_ge(g_st[u % 2], 16 * (u // 2))
                act.activation(g_out[:, u % 2, :], ps[:, 7, :], ACT.Tanh, scale=0.5).then_inc(gate_tanh, 1)
            if u:
                v = u - 1
                act.wait_ge(pv_mm, BANKS_BEFORE[v + 1])
                if v >= 2:
                    act.wait_ge(o_sum, v - 1)
                act.activation(o_tmp[:, v % 2, :], ps[64:128, 6, 0:256], ACT.Copy) \
                    .then_inc(o_half, 1)

        for i in range(8):
            act.wait_ge(stage_in[i % 2], 16 * (i // 2 + 1))
            act.activation(op_hi[:, i, :], stage[:, i % 2, :], ACT.Copy).then_inc(op_hi_s, 1)

        def merge_split(i, first=False):
            for b in range(2):
                s = (R_MERGE + b) % 2
                act.wait_ge(raw_in[s], 32 * i + raw_count(R_MERGE + b))
                if first:
                    act.wait_ge(gate_mm, 2 * (N_BR - 2 + b) + 2)
                else:
                    act.wait_ge(merge_mm, merge_free(i, b))
                act.activation(a_hi[:, b, :], raw[:, s, :], ACT.Copy).then_inc(hi_done, 1)

        merge_split(0, first=True)
        with act.Fori(1, KT // 2) as i:
            merge_split(i)

        def h2_evict(half):
            for k in range(KT):
                m = KT * half + k
                act.wait_ge(x1t_mm, m + 1)
                if m >= 2:
                    act.wait_ge(h2_lo, m - 1)
                act.activation(h2_tmp[:, m % 2, :], ps[:, 4 * half + m % 4, :], ACT.Identity, scale=scale[:, k:k + 1],
                               bias=shift[:, k:k + 1]).then_inc(h2_made, 1)

        def y_half(half):
            for t in range(TT):
                n = TT * half + t
                act.wait_ge(y_mm, n + 1)
                act.activation(y[:, t, half * CH:(half + 1) * CH], ps[:, 4 + n % 4, :], ACT.Copy).then_inc(y_out, 1)
                if half:
                    act.wait_ge(y_out, n + 1)
                    if t:
                        act.wait_ge(x1_ms, t)
                    act.activation(y_sq[:, :], y[:, t, :], ACT.Square, accum_out=stat[:, t:t + 1]).then_inc(y_ms, 1)
                    act.wait_ge(x1_made, t + 1)
                    act.wait_ge(y_ms, t + 1)
                    act.activation(y_sq[:, :], x1[:, t % 2, :], ACT.Square, accum_out=stat[:, 8 + t:9 + t]) \
                        .then_inc(x1_ms, 1)
                    if t == 5:
                        h2_evict(0)
                        mlp_split(0, 0, first=True)
                        mlp_split(0, 1, first=True)

        def mlp_split(j, n, first=False):
            s = (R_MLP + n) % 2
            act.wait_ge(raw_in[s], 64 * j + raw_count(R_MLP + n))
            if n < 4:
                if first and n < 2:
                    act.wait_ge(merge_mm, 2 * KT - 2 + 2 * n)
                else:
                    act.wait_ge(fc1_mm, 8 * j + (-1, 0, 3, 4)[n])
                act.activation(a_hi[:, (A_MLP + n) % 2, :], raw[:, s, :], ACT.Copy).then_inc(hi_done, 1)
            else:
                if first:
                    act.wait_ge(y_mm, 2 * TT)
                else:
                    act.wait_ge(fc2_mm, 2 * TT * j)
                act.activation(b_hi[:, n - 4, :], raw[:, s, :], ACT.Copy).then_inc(hi_done, 1)

        def out_split(n):
            r = R_OUT + n
            act.wait_ge(raw_in[r % 2], raw_count(r))
            if n >= 4:
                act.wait_ge(y_mm, TT)
            act.activation(b_hi[:, n % 4, :], raw[:, r % 2, :], ACT.Copy).then_inc(hi_done, 1)

        act.wait_ge(merge_mm, 2 * KT)
        for n in range(4):
            out_split(n)
        y_half(0)
        for n in range(4, 8):
            out_split(n)
        y_half(1)

        def mlp(j, first=False):
            if not first:
                mlp_split(j, 0)
                mlp_split(j, 1)
            for n in range(8):
                m, ch = 2 * (n // 4) + n % 2, (n // 2) % 2
                act.wait_ge(fc1_mm, 8 * j + (n + 1))
                if not (first and n < 2):
                    act.wait_ge(hid_lo_s, 8 * j + (n - 1))
                act.activation(relu[:, n % 2, :], ps[:, n % 4, :], ACT.Relu).then_inc(relu_done, 1)
                if n >= 2:
                    mlp_split(j, n, first)
                act.wait_ge(sq_done, 8 * j + (n + 1))
                act.activation(hid_hi[:, m, ch * CH:(ch + 1) * CH], relu[:, n % 2, :], ACT.Copy).then_inc(hid_hi_s, 1)

        h2_evict(1)
        mlp(0, first=True)
        with act.Fori(1, D_FF // CH) as j:
            mlp(j)
        for t in range(TT):
            act.wait_ge(y2_added, 2 * TT * (D_FF // CH - 1) + 2 * t + 2)
            if t:
                act.wait_ge(f_ms, t)
            act.activation(y_sq[:, :], y[:, t, :], ACT.Square, accum_out=stat[:, 16 + t:17 + t]).then_inc(f_ms, 1)

    @block.vector
    def _(dve):
        def split_lo(r, dst, hi, src=None):
            dve.wait_ge(hi_done, r + 1)
            dve.tensor_tensor(dst, raw[:, r % 2, :] if src is None else src, full(hi), ALU.subtract).then_inc(lo_done, 1)

        def split_a(a):
            split_lo(R_FM + a, a_lo[:, a % 2, :], a_hi[:, a % 2, :])

        dve.wait_ge(silu_t, 1)
        dve.tensor_scalar(silu_c, silu_c, 0.5, 0.5, ALU.mult, ALU.add).then_inc(silu_done, 1)
        dve.wait_ge(silu_done, 1)
        dve.tensor_tensor(silu_c, silu_c, c_col, ALU.mult).then_inc(silu_done, 1)
        dve.wait_ge(silu_done, 2)
        dve.wait_ge(acc_bias, 16)
        for n in range(16):
            dve.wait_ge(ada_in[n % 4], 16 * (n // 4 + 1))
            if n >= 2:
                dve.wait_ge(ada_added, n - 1)
            sl = slice((n % 2) * 1024, (n % 2 + 1) * 1024)
            dve.scalar_tensor_tensor(out=ada_acc[:, sl], in0=ada[:, n % 4, :], scalar=silu_c[:, n // 2:n // 2 + 1],
                                     in1=ada_acc[:, sl], op0=ALU.mult, op1=ALU.add).then_inc(ada_added, 1)

        def normalise_x(ch):
            dve.wait_ge(x_rstd, ch + 1)
            for t in range(4 * ch, 4 * ch + 4):
                dve.tensor_scalar(xt[:, t, :], xt[:, t, :], rstd[:, t:t + 1], None, ALU.mult).then_inc(x_norm, 1)

        normalise_x(0)
        normalise_x(1)
        dve.wait_ge(mod_mm, 1)
        dve.tensor_copy(shift, ps[:, 7, 0:8]).then_inc(mod_done, 1)
        dve.scalar_tensor_tensor(out=scale, in0=ps[:, 7, 8:16], scalar=1.0, in1=g_pre, op0=ALU.add,
                                 op1=ALU.mult).then_inc(mod_done, 1)
        for r, (k0, k1) in enumerate(((0, 3), (3, 6), (6, 8))):
            split_lo(r, wv_lo[:, k0:k1, :], wv_hi[:, k0:k1, :],
                     raw[:, r % 2, 0:(k1 - k0) * WV_COLS].rearrange("p (k n) -> p k n", n=WV_COLS))

        def split_h(src, n, made, hi_s, lo_s):
            k, sl = n % KT, slice((n // KT) * CH, (n // KT + 1) * CH)
            dve.wait_ge(made, n + 1)
            dve.tensor_copy(act_hi[:, k, sl], src[:, n % 2, :]).then_inc(hi_s, 1)
            dve.wait_ge(hi_s, n + 1)
            dve.tensor_tensor(act_lo[:, k, sl], src[:, n % 2, :], full(act_hi[:, k, sl]), ALU.subtract).then_inc(lo_s, 1)

        for n in range(2 * KT):
            split_h(h_tmp, n, h_made, h_hi, h_lo)
        split_a(0)
        split_a(1)
        for t in range(TT):
            b = 4 + t % 2
            dve.wait_ge(v_hi, 2 * t + 2)
            dve.tensor_tensor(v_st[:, t, :, 64:128], ps[:, b, 0:256].rearrange("p (f d) -> p f d", d=64),
                              full(v_st[:, t, :, 0:64]), ALU.subtract).then_inc(v_lo, 1)
        dve.wait_ge(v_hi, 2 * TT)
        dve.tensor_scalar(gates[:, :, :], gates[:, :, :], 0.5, 0.5, ALU.mult, ALU.add).then_inc(gates_done, 1)

        def rope_cos_part(a, ch):
            i, g = 2 * FM_ROPE[a] + ch, 2 * a + ch
            dve.wait_ge(fm_act, g + 1)
            if i == 0:
                dve.wait_ge(cos_in, 32)
            if i in (2, 3):
                dve.wait_ge(rope_sum, i - 1)
            if i >= 4:
                dve.wait_ge(rope_hi, i - 3)
                dve.wait_ge(rope_lo, i - 3)
            dve.tensor_tensor(r_cos[:, i % 2, :], ps[:, g % 4, :], cos[:, ch * CH:(ch + 1) * CH], ALU.mult) \
                .then_inc(rope_cos, 1)

        def rope_lo_part(i):
            dve.wait_ge(rope_hi, i - 1)
            dve.tensor_tensor(r_lo[:, i % 2, :], r_cos[:, i % 2, :], full(r_hi[:, i % 2, :]), ALU.subtract) \
                .then_inc(rope_lo, 1)

        def make_blocks(kv):
            dve.wait_ge(bkx_in, 64 * (kv + 1))
            if kv:
                dve.wait_ge(cmp_mm, 1)
            for g in range(2):
                for h in range(2):
                    src = bkx[:, g, 16 * h:16 * h + 16 * N_CMP].rearrange("p (n l two) -> p l n two", l=8, two=2)[:, :, :, 0]
                    pe_b = pe_col[:, kv, 8 * h:8 * h + 8].unsqueeze(2).to_broadcast([P, 8, N_CMP])
                    ins = dve.tensor_tensor(bk[:, 8 * h:8 * h + 8, g, :], src, pe_b, ALU.add)
            ins.then_inc(bk_made, 1)

        def gelu(kv):
            x, t = gelu_x[:, kv, :], gelu_t[:, kv, :]
            n = 5 * kv
            dve.wait_ge(gelu_c, 2 * kv + 1)
            dve.tensor_tensor(t, x, x, ALU.mult).then_inc(gelu_d, 1)
            dve.wait_ge(gelu_d, n + 1)
            dve.tensor_scalar(t, t, 0.044715, 1.0, ALU.mult, ALU.add).then_inc(gelu_d, 1)
            dve.wait_ge(gelu_d, n + 2)
            dve.tensor_tensor(t, t, x, ALU.mult).then_inc(gelu_d, 1)
            dve.wait_ge(gelu_c, 2 * kv + 2)
            dve.scalar_tensor_tensor(out=t, in0=t, scalar=1.0, in1=x, op0=ALU.add, op1=ALU.mult).then_inc(gelu_d, 1)
            dve.wait_ge(gelu_d, n + 4)
            dve.tensor_scalar(t, t, 0.5, None, ALU.mult).then_inc(gelu_d, 1)

        def cmp_store():
            dve.wait_ge(cmp_hi, 3)
            for half in range(2):
                dve.tensor_tensor(kc_lo[64 * half:64 * half + 64, :, 0:N_CMP],
                                  ps[0:64, 6, 256:382].rearrange("p (g n) -> p g n", g=2),
                                  full(kc_hi[0:64, :, 0:N_CMP]), ALU.subtract).then_inc(cmp_lo, 1)
            dve.tensor_tensor(vc_st[0:N_CMP, :, 64:128], ps[0:N_CMP, 6, 384:512].rearrange("p (g d) -> p g d", g=2),
                              full(vc_st[0:N_CMP, :, 0:64]), ALU.subtract).then_inc(cmp_lo, 1)

        def pooled_part(g):
            w = POOL_SIZES[g]
            s, p = ps_ab[g % 2], ps_ab[(g + 1) % 2]
            dve.wait_ge(pool_add, sum(range(1, g + 2)))
            dve.tensor_tensor(s[:, PAD:PAD + w], s[:, PAD:PAD + w], inv_cnt[:, g, 0:w], ALU.mult).then_inc(pooled_w, 1)
            dve.scalar_tensor_tensor(out=p[:, PAD + w:], in0=s[:, PAD + w:], scalar=1.0 / w, in1=pu[:, PAD + w:],
                                     op0=ALU.mult, op1=ALU.subtract).then_inc(pooled, 1)
            dve.wait_ge(pooled_w, g + 1)
            dve.tensor_tensor(p[:, PAD:PAD + w], s[:, PAD:PAD + w], pu[:, PAD:PAD + w], ALU.subtract).then_inc(pooled, 1)
            dve.wait_ge(pooled_hi, g + 1)
            dve.tensor_tensor(pp_lo[:, :], p[:, PAD:], full(pp_hi[:, :]), ALU.subtract).then_inc(pooled_lo, 1)

        for a in range(N_FM):
            if a in FM_ROPE:
                for ch in range(2):
                    rope_cos_part(a, ch)
                if a:
                    for ch in range(2):
                        rope_lo_part(2 * FM_ROPE[a] + ch)
            split_a(a + 2)
            if a == 3:
                make_blocks(0)
            if a == 5:
                gelu(0)
            if a == 5:
                make_blocks(1)
            if a == 7:
                gelu(1)
            if a == 8:
                cmp_store()
                dve.wait_ge(wp_hi_s, 1)
                dve.tensor_tensor(wp_lo[:, :, :], wp_raw[:, :, :], full(wp_hi[:, :, :]), ALU.subtract).then_inc(wp_lo_s, 1)
            if a >= 8:
                pooled_part(a - 8)

        def lo_banks(u, s):
            for b in portion(u, s):
                if b < n_banks(u):
                    n = BANKS_BEFORE[u] + b
                    dve.wait_ge(pthi, n + 1)
                    w = 256 * min(2, len(key_tiles(u // 4)) - 2 * b)
                    dve.tensor_tensor(pt_lo[:, n % 3, 0:w], ps[:, 4 + n % 2, 0:w], full(pt_hi[:, n % 3, 0:w]),
                                      ALU.subtract).then_inc(ptlo, 1)

        def neg_max(u, s):
            c, n = u // 4, STEPS * u + s
            dve.wait_ge(score_mm, n + 1)
            k = 2 if s == 4 else 1
            if s < 4:
                parts = score_parts(c, s // 2)
                src = ps[:, 2 * (n % 2):2 * (n % 2) + len(parts), 0:parts[0][1]]
                dve.tensor_reduce(smax[:, n % 4, 0:1], src, AX.XY, ALU.max).then_inc(max_done, 1)
            else:
                src = ps[:, 2 * (n % 2), 0:P].rearrange("p (h n) -> p h n", h=2)
                dve.tensor_reduce(smax[:, n % 4, 0:2], src, AX.X, ALU.max).then_inc(max_done, 1)
            dve.wait_ge(max_done, n + 1)
            dve.tensor_scalar(negm[:, n % 4, 0:k], smax[:, n % 4, 0:k], NEG / 10, -HEAD_DIM ** -0.5, ALU.max,
                              ALU.mult).then_inc(negm_done, 1)

        def normalise(u, s):
            c, n = u // 4, STEPS * u + s
            heads = (0, 1) if s == 4 else (s % 2,)
            k = len(heads)
            dve.wait_ge(exp_done, n + 1)
            dve.tensor_scalar(ssum[:, n % 4, 0:k], ssum[:, n % 4, 0:k], 1e-30, None, ALU.max).then_inc(guard_done, 1)
            dve.wait_ge(guard_done, n + 1)
            dve.reciprocal(srec[:, n % 4, 0:k], ssum[:, n % 4, 0:k]).then_inc(rec_done, 1)
            dve.wait_ge(rec_done, n + 1)
            for x, hh in enumerate(heads):
                branch = s // 2
                head = 2 * (u % 4) + hh
                buf = (p_sel, p_win, p_cmp)[branch]
                w = 64 if s == 4 else sum(q[1] for q in score_parts(c, branch))
                gate = gates[:, c, 3 * head + (1, 2, 0)[branch]:3 * head + (1, 2, 0)[branch] + 1]
                ins = dve.tensor_scalar(buf[:, u % 2, hh, 0:w], buf[:, u % 2, hh, 0:w], srec[:, n % 4, x:x + 1], gate,
                                        ALU.mult, ALU.mult)
            ins.then_inc(norm_done, 1)

        dve.wait_ge(gates_done, 1)
        for u in range(UNITS + 1):
            for s in range(STEPS):
                if u < UNITS:
                    neg_max(u, s)
                if 0 < STEPS * u + s <= STEPS * UNITS:
                    n = STEPS * u + s - 1
                    normalise(n // STEPS, n % STEPS)
                if u < UNITS and s == 1 and u % 2 == 0 and 1 <= u // 2 < N_BR - 1:
                    split_a(N_FM + u // 2 + 1)
                if u:
                    lo_banks(u - 1, s)
            if u:
                v = u - 1
                dve.wait_ge(o_half, v + 1)
                if v >= 2:
                    dve.wait_ge(o_st[v % 2], 16 * (v // 2))
                dve.tensor_tensor(o_out[:, v % 2, :], ps[0:64, 6, 0:256], o_tmp[:, v % 2, :],
                                  ALU.add).then_inc(o_sum, 1)

        for i in range(8):
            dve.wait_ge(op_hi_s, i + 1)
            dve.tensor_tensor(op_lo[:, i, :], stage[:, i % 2, :], full(op_hi[:, i, :]), ALU.subtract).then_inc(op_lo_s, 1)
        dve.wait_ge(acc2_bias, 16)

        def merge_split(i, b):
            s = (R_MERGE + b) % 2
            dve.wait_ge(hi_done, 2 * i + (R_MERGE + b + 1))
            dve.tensor_tensor(a_lo[:, b % 2, :], raw[:, s, :], full(a_hi[:, b % 2, :]), ALU.subtract).then_inc(lo_done, 1)

        def merge(i, first=False, last=False):
            for b in range(2):
                for part in range(4):
                    dve.wait_ge(stage_in[part % 2], 64 * i + (64 + 32 * b + 16 * (part // 2 + 1)))
                    if not (first and b == 0):
                        dve.wait_ge(ada2_added, 8 * i + (4 * b + part - 3))
                    dve.scalar_tensor_tensor(out=ada_acc2[:, part, :], in0=stage[:, part % 2, :],
                                             scalar=silu_c[:, bass.ds(2 * i + b, 1)], in1=ada_acc2[:, part, :],
                                             op0=ALU.mult, op1=ALU.add).then_inc(ada2_added, 1)
                if not (last and b == 1):
                    merge_split(i, b + 1)
                for ch in range(2):
                    g = 2 * b + ch
                    dve.wait_ge(merge_mm, 4 * i + (g + 1))
                    dve.wait_ge(mg_in[ch], 32 * i + 16 * (b + 1))
                    for h, dst in ((0, m_a), (1, m_b)):
                        ins = dve.scalar_tensor_tensor(out=dst[:, ch, :], in0=mg[:, ch, h, :], scalar=1.0,
                                                       in1=ps[:, 2 * g + (1 - h), :], op0=ALU.add, op1=ALU.mult)
                    ins.then_inc(merge_ab, 1)
                for ch in range(2):
                    n = 2 * b + ch
                    dst = bass.ds(2 * i + b, 1)
                    sl = slice(ch * CH, (ch + 1) * CH)
                    dve.wait_ge(merge_sum, 4 * i + (n + 1))
                    dve.tensor_scalar(act_hi[:, dst, sl].rearrange("p k n -> p (k n)"), m_a[:, ch, :], 0.5, None,
                                      ALU.mult).then_inc(merge_hi, 1)
                    dve.wait_ge(merge_hi, 4 * i + (n + 1))
                    dve.scalar_tensor_tensor(out=act_lo[:, dst, sl].rearrange("p k n -> p (k n)"), in0=m_a[:, ch, :],
                                             scalar=0.5, in1=full(act_hi[:, dst, sl]).rearrange("p k n -> p (k n)"),
                                             op0=ALU.mult, op1=ALU.subtract).then_inc(merge_lo, 1)

        merge_split(0, 0)
        merge(0, first=True)
        with dve.Fori(1, KT // 2 - 1) as i:
            merge(i)
        merge(KT // 2 - 1, last=True)

        def out_split(n):
            split_lo(R_OUT + n, b_lo[:, n % 4, :], b_hi[:, n % 4, :])

        for n in range(4):
            out_split(n)
        dve.wait_ge(gp_in, 32)
        dve.wait_ge(bc_mm, 1)
        for half in range(2):
            sl = slice(half * CH, (half + 1) * CH)
            dve.tensor_tensor(gt1[:, sl], ps[:, half, :], gt1[:, sl], ALU.mult).then_inc(g_made, 1)
            dve.tensor_tensor(gt2[:, sl], ps[:, 2 + half, :], gt2[:, sl], ALU.mult).then_inc(g_made, 1)
        dve.wait_ge(mod2_mm, 1)
        dve.tensor_copy(shift, ps[:, 7, 0:8]).then_inc(mod2_done, 1)
        dve.scalar_tensor_tensor(out=scale, in0=ps[:, 7, 8:16], scalar=1.0, in1=g_mlp, op0=ALU.add,
                                 op1=ALU.mult).then_inc(mod2_done, 1)
        for n in range(4, 8):
            out_split(n)
        def mlp_split(j, n):
            s = (R_MLP + n) % 2
            dve.wait_ge(hi_done, 8 * j + (R_MLP + n + 1))
            dst, hi = (a_lo[:, (A_MLP + n) % 2, :], a_hi[:, (A_MLP + n) % 2, :]) if n % 8 < 4 else \
                (b_lo[:, n - 4, :], b_hi[:, n - 4, :])
            dve.tensor_tensor(dst, raw[:, s, :], full(hi), ALU.subtract).then_inc(lo_done, 1)

        dve.wait_ge(g_made, 4)
        for t in range(TT):
            yt = y[:, t, :]
            dve.wait_ge(y_rstd, t + 1)
            dve.scalar_tensor_tensor(out=yt, in0=yt, scalar=stat[:, t:t + 1], in1=gt1[:, :], op0=ALU.mult,
                                     op1=ALU.mult).then_inc(y_gated, 1)
            dve.wait_ge(y_gated, t + 1)
            dve.wait_ge(xi_in[t % 2], 16 * (t // 2 + 1))
            if t >= 2:
                dve.wait_ge(x1_st[t % 2], 16 * (t // 2))
                dve.wait_ge(x1_ms, t - 1)
            dve.tensor_tensor(x1[:, t % 2, :], yt, x_in[:, t % 2, :], ALU.add).then_inc(x1_made, 1)
            dve.wait_ge(x1_rstd, t + 1)
            dve.tensor_scalar(yt, x1[:, t % 2, :], stat[:, 8 + t:9 + t], None, ALU.mult).then_inc(x1n_made, 1)
            if t == 5:
                for m in range(KT):
                    split_h(h2_tmp, m, h2_made, h2_hi, h2_lo)
                mlp_split(0, 0)
                mlp_split(0, 1)

        for m in range(KT, 2 * KT):
            split_h(h2_tmp, m, h2_made, h2_hi, h2_lo)

        def mlp(j, first=False, last=False):
            if first:
                for s in range(2):
                    dve.wait_ge(x1_st[s], 16 * TT // 2)
            for n in range(8):
                m, ch = 2 * (n // 4) + n % 2, (n // 2) % 2
                sl = slice(ch * CH, (ch + 1) * CH)
                if n >= 2:
                    mlp_split(j, n)
                dve.wait_ge(hid_hi_s, 8 * j + (n + 1))
                dve.tensor_tensor(hid_lo[:, m, sl], relu[:, n % 2, :], full(hid_hi[:, m, sl]), ALU.subtract) \
                    .then_inc(hid_lo_s, 1)
            if not last:
                mlp_split(j, 8)
                mlp_split(j, 9)
            for n in range(2 * TT):
                t, half = n // 2, n % 2
                yt = y[:, t, half * CH:(half + 1) * CH]
                dve.wait_ge(fc2_mm, 2 * TT * j + (n + 1))
                if first:
                    dve.tensor_copy(yt, ps[:, 4 + n % 4, :]).then_inc(y2_added, 1)
                else:
                    dve.wait_ge(y2_added, 2 * TT * j + (n - 2 * TT + 1))
                    dve.tensor_tensor(yt, ps[:, 4 + n % 4, :], yt, ALU.add).then_inc(y2_added, 1)

        mlp(0, first=True)
        with dve.Fori(1, D_FF // CH - 1) as j:
            mlp(j)
        mlp(D_FF // CH - 1, last=True)
        for t in range(TT):
            yt = y[:, t, :]
            dve.wait_ge(f_rstd, t + 1)
            dve.scalar_tensor_tensor(out=yt, in0=yt, scalar=stat[:, 16 + t:17 + t], in1=gt2[:, :], op0=ALU.mult,
                                     op1=ALU.mult).then_inc(f_gated, 1)
            dve.wait_ge(f_gated, t + 1)
            dve.wait_ge(x1i_in[t % 2], 16 * (t // 2 + 1))
            if t >= 2:
                dve.wait_ge(out_st[t % 2], 16 * (t // 2))
            dve.tensor_tensor(fin[:, t % 2, :], yt, x1_in[:, t % 2, :], ALU.add).then_inc(f_made, 1)

    @block.tensor
    def _(pe):
        def three(dst, wh, wl, mh, ml, start, stop):
            pe.matmul(dst, wh, mh, start=start, stop=False)
            pe.matmul(dst, wh, ml, start=False, stop=False)
            return pe.matmul(dst, wl, mh, start=False, stop=stop)

        pe.wait_ge(consts_made, CONSTS)
        pe.wait_ge(ada_added, 16)
        for n in range(16):
            ins = pe.matmul(ps[:, 7, n:n + 1], ada_acc[:, n * P:(n + 1) * P], ones[:, 0:1], start=True, stop=True)
        ins.then_inc(mod_mm, 1)
        for n in range(2 * KT):
            ch, k = n // KT, n % KT
            if n % KT == 0:
                pe.wait_ge(x_norm, 4 * ch + 4)
            if n >= 4:
                pe.wait_ge(h_made, n - 3)
            for t in range(4):
                ins = pe.transpose(ps[:, n % 4, t * P:(t + 1) * P], xt[:, 4 * ch + t, k * P:(k + 1) * P], ident[:, :])
            ins.then_inc(xt_mm, 1)
        pe.wait_ge(lo_done, 3)
        for t in range(TT):
            if t % 4 == 0:
                pe.wait_ge(h_lo, KT * (t // 4 + 1))
            if t >= 2:
                pe.wait_ge(v_lo, t - 1)
                pe.wait_ge(v_hi, 2 * t - 2)
            for k in range(KT):
                tok = slice(t * P, (t + 1) * P)
                ins = three(ps[:, 4 + t % 2, 0:WV_COLS], act_hi[:, k, tok], act_lo[:, k, tok], wv_hi[:, k, :],
                            wv_lo[:, k, :], k == 0, k == KT - 1)
            ins.then_inc(v_mm, 1)

        def project(a, bank, ch, ks, done=None):
            sl = slice(ch * CH, (ch + 1) * CH)
            for k in ks:
                w = slice(k * P, (k + 1) * P)
                ins = three(ps[:, bank, :], a_hi[:, a % 2, w], a_lo[:, a % 2, w], act_hi[:, k, sl], act_lo[:, k, sl],
                            k == 0, k == KT - 1)
            return ins

        def compress(kv):
            pe.wait_ge(cw_in, 16 * (kv + 1))
            pe.wait_ge(bk_made, kv + 1)
            if kv:
                pe.wait_ge(gelu_c, 1)
            for l in range(16):
                ins = pe.matmul(ps[0:64, 6, P * kv:P * kv + 126], cw1[:, l, :],
                                bk[:, l, :, :].rearrange("p g n -> p (g n)"), start=l == 0, stop=l == 15)
            ins.then_inc(cmp_mm, 1)

        def compress2():
            pe.wait_ge(gelu_d, 10)
            pe.matmul(ps[0:64, 6, 256:382], w2k[:, :], gelu_t[:, 0, :], start=True, stop=True).then_inc(cmp2_mm, 1)
            for g in range(2):
                ins = pe.matmul(ps[0:N_CMP, 6, 384 + 64 * g:448 + 64 * g], gelu_t[:, 1, N_CMP * g:N_CMP * (g + 1)],
                                w2v[:, :], start=True, stop=True)
            ins.then_inc(cmp2_mm, 1)

        def mix(g):
            pe.wait_ge(pooled_lo, g + 1)
            if g == 0:
                pe.wait_ge(wp_lo_s, 1)
            for ch in range(2):
                n, sl = 2 * g + ch, slice(ch * CH, (ch + 1) * CH)
                if n >= 2:
                    pe.wait_ge(mix_out, n - 1)
                three(ps[:, 4 + n % 2, :], wp_hi[:, g, :], wp_lo[:, g, :], pp_hi[:, sl], pp_lo[:, sl], True, True) \
                    .then_inc(mix_mm, 1)

        for a in range(N_FM):
            pe.wait_ge(lo_done, R_FM + a + 1)
            for ch in range(2):
                g = 2 * a + ch
                if g >= 4:
                    pe.wait_ge(fm_act, g - 3)
                    if a - 2 in FM_ROPE:
                        pe.wait_ge(rope_cos, 2 * FM_ROPE[a - 2] + ch + 1)
                ins = project(a, g % 4, ch, range(KT))
                ins.then_inc(fm_mm, 1)
            if a == 4:
                compress(0)
            if a == 6:
                compress(1)
            if a == 8:
                compress2()
            if a >= 9:
                mix(a - 9)
        mix(3)

        def scores(u, s):
            c, n = u // 4, STEPS * u + s
            g = (u % 4) // 2
            if n >= 2:
                pe.wait_ge(exp_done, n - 1)
            if s == 0 and u % 4 == 0:
                pe.wait_ge(q_in[c % 2], 16 * (c // 2 + 1))
            base = 2 * (n % 2)
            if s < 4:
                branch, q = s // 2, q_st[:, c % 2, 2 * (u % 4) + s % 2, :]
                parts = score_parts(c, branch)
                for x, (k0, w, _) in enumerate(parts):
                    dst = ps[:, base + x, 0:w]
                    last, far = x == len(parts) - 1, branch == 1 and c >= WINDOW // P and x == 0
                    pe.matmul(dst, q, k_hi[:, 2 * branch + g, k0:k0 + w], start=True, stop=False)
                    ins = pe.matmul(dst, q, k_lo[:, 2 * branch + g, k0:k0 + w], start=False, stop=True)
                    if far:
                        ins = pe.matmul(ps[:, base + x, 0:P], ident_b[:, :], mask_far[:, :], start=False, stop=True,
                                        skip_group_check=True)
                    if last:
                        ins = pe.matmul(ps[:, base + x, w - P:w], ident_b[:, :], mask_diag[:, :], start=False, stop=True,
                                        skip_group_check=True)
                ins.then_inc(score_mm, 1)
            else:
                for hh in range(2):
                    dst, q = ps[:, base, 64 * hh:64 * hh + 64], q_st[:, c % 2, 2 * (u % 4) + hh, :]
                    pe.matmul(dst, q, kc_hi[:, g, :], start=True, stop=False)
                    pe.matmul(dst, q, kc_lo[:, g, :], start=False, stop=False)
                    ins = pe.matmul(dst, ident_b[:, :], mask_cmp[:, c, :], start=False, stop=True)
                ins.then_inc(score_mm, 1)

        def attend(u, s):
            c = u // 4
            tiles = key_tiles(c)
            for b in portion(u, s):
                n = BANKS_BEFORE[u] + b
                if b < n_banks(u):
                    if n >= 2:
                        pe.wait_ge(ptlo, n - 1)
                    elif n == 0:
                        pe.wait_ge(mix_out, 8)
                    for x, (branch, j) in enumerate(tiles[2 * b:2 * b + 2]):
                        pe.wait_ge(norm_done, STEPS * u + (2, 4, 5)[branch])
                        for hh in range(2):
                            at = ps[:, 4 + n % 2, 256 * x + P * hh:256 * x + P * hh + P]
                            if branch == 2:
                                src = p_cmp[:, u % 2, hh, :]
                            else:
                                k = (j - (max(0, c - WINDOW // P) if branch else 0)) * P
                                src = (p_sel, p_win)[branch][:, u % 2, hh, k:k + P]
                            ins = pe.transpose(at, src, ident[:, :])
                    ins.then_inc(tp_mm, 1)
                if b:
                    n -= 1
                    pe.wait_ge(ptlo, n + 1)
                    if b == 1 and u:
                        pe.wait_ge(o_sum, u)
                    g = (u % 4) // 2
                    for x, (branch, j) in enumerate(tiles[2 * b - 2:2 * b]):
                        v = vc_st[:, g, :] if branch == 2 else v_st[:, j, 2 * branch + g, :]
                        dst = ps[:, 6, 0:256]
                        first, last = b == 1 and x == 0, 2 * b - 2 + x == len(tiles) - 1
                        pe.matmul(dst, v, pt_hi[:, n % 3, 256 * x:256 * x + 256], start=first, stop=False)
                        ins = pe.matmul(dst, v, pt_lo[:, n % 3, 256 * x:256 * x + 256], start=False, stop=last)
                    ins.then_inc(pv_mm, 1)

        pe.wait_ge(fm_act, 2 * N_FM)
        pe.wait_ge(rope_out[0], rope_out_count(ROPES - 2))
        pe.wait_ge(rope_out[1], rope_out_count(ROPES - 1))
        pe.wait_ge(cmp_lo, 3)
        for u in range(UNITS + 1):
            for s in range(STEPS):
                if u < UNITS:
                    scores(u, s)
                    a = N_FM + u // 2
                    if s == 0:
                        pe.wait_ge(lo_done, R_FM + a + 1)
                        if u:
                            pe.wait_ge(gate_tanh, u)
                    if s < 4:
                        ins = project(a, 7, u % 2, range(2 * s, 2 * s + 2))
                        if s == 3:
                            ins.then_inc(gate_mm, 1)
                if u:
                    attend(u - 1, s)

        def merge(i, first=False):
            for b in range(2):
                pe.wait_ge(lo_done, 2 * i + (R_MERGE + b + 1))
                for part in range(2):
                    if first and b == 0:
                        pe.wait_ge(op_lo_s, 4 * part + 4)
                    for ch in range(2):
                        g = 2 * b + ch
                        if part == 0 and not first:
                            pe.wait_ge(merge_ab, 4 * i + (g - 3))
                        for k in range(4 * part, 4 * part + 4):
                            w, sl = slice(k * P, (k + 1) * P), slice(ch * CH, (ch + 1) * CH)
                            ins = three(ps[:, 2 * g + part, :], a_hi[:, b, w], a_lo[:, b, w], op_hi[:, k, sl],
                                        op_lo[:, k, sl], k % 4 == 0, k % 4 == 3)
                        if part:
                            ins.then_inc(merge_mm, 1)

        pe.wait_ge(gate_tanh, UNITS)
        pe.wait_ge(o_sum, UNITS)
        merge(0, first=True)
        with pe.Fori(1, KT // 2) as i:
            merge(i)

        pe.wait_ge(ada2_added, 32)
        pe.wait_ge(merge_ab, 2 * KT)
        for f, bank in ((0, 0), (3, 2)):
            for half in range(2):
                ins = pe.matmul(ps[:, bank + half, :], ones[:, :], ada_acc2[:, f, half * CH:(half + 1) * CH],
                                start=True, stop=True)
        ins.then_inc(bc_mm, 1)
        for f in range(2):
            for k in range(KT):
                ins = pe.matmul(ps[:, 7, 8 * f + k:8 * f + k + 1], ada_acc2[:, 1 + f, k * P:(k + 1) * P], ones[:, 0:1],
                                start=True, stop=True)
        ins.then_inc(mod2_mm, 1)

        def x1_transposes(half):
            pe.wait_ge(x1n_made, 4 * half + 4)
            pe.wait_ge(g_made, 4)
            for k in range(KT):
                m = KT * half + k
                if k >= 4:
                    pe.wait_ge(h2_made, m - 3)
                for t in range(4):
                    ins = pe.transpose(ps[:, 4 * half + m % 4, t * P:(t + 1) * P], y[:, 4 * half + t, k * P:(k + 1) * P],
                                       ident[:, :])
                ins.then_inc(x1t_mm, 1)

        pe.wait_ge(merge_lo, 2 * KT)
        for n in range(2 * TT):
            half, t = n // TT, n % TT
            if t == 0:
                pe.wait_ge(lo_done, R_OUT + 4 * half + 4)
            if n == 3:
                pe.wait_ge(mod2_done, 2)
            if n >= 4:
                pe.wait_ge(y_out, n - 3)
            tok = slice(t * P, (t + 1) * P)
            for k in range(KT):
                w = slice((k % 2) * CH, (k % 2 + 1) * CH)
                ins = three(ps[:, 4 + n % 4, :], act_hi[:, k, tok], act_lo[:, k, tok], b_hi[:, k // 2, w],
                            b_lo[:, k // 2, w], k == 0, k == KT - 1)
            ins.then_inc(y_mm, 1)
            if n == TT + 5:
                x1_transposes(0)

        def mlp(j, first=False):
            for n in range(8):
                m, ch = 2 * (n // 4) + n % 2, (n // 2) % 2
                a = (A_MLP + m) % 2
                if ch == 0:
                    pe.wait_ge(lo_done, 8 * j + (R_MLP + m + 1))
                if first and n in (0, 2):
                    pe.wait_ge(h2_lo, KT * (ch + 1))
                if not (first and n < 4):
                    pe.wait_ge(relu_done, 8 * j + (n - 3))
                sl = slice(ch * CH, (ch + 1) * CH)
                for k in range(KT):
                    w = slice(k * P, (k + 1) * P)
                    ins = three(ps[:, n % 4, :], a_hi[:, a, w], a_lo[:, a, w], act_hi[:, k, sl], act_lo[:, k, sl],
                                k == 0, k == KT - 1)
                ins.then_inc(fc1_mm, 1)
                if first and n == 1:
                    x1_transposes(1)
            pe.wait_ge(lo_done, 8 * j + (R_MLP + 8))
            for n in range(2 * TT):
                t, half = n // 2, n % 2
                if n == 0:
                    pe.wait_ge(hid_lo_s, 8 * j + 8)
                if not (first and n < 4):
                    pe.wait_ge(y2_added, 2 * TT * j + (n - 3))
                elif n == 0:
                    pe.wait_ge(y_out, 2 * TT)
                tok, w = slice(t * P, (t + 1) * P), slice(half * CH, (half + 1) * CH)
                for k in range(4):
                    ins = three(ps[:, 4 + n % 4, :], hid_hi[:, k, tok], hid_lo[:, k, tok], b_hi[:, k, w], b_lo[:, k, w],
                                k == 0, k == 3)
                ins.then_inc(fc2_mm, 1)
        mlp(0, first=True)
        with pe.Fori(1, D_FF // CH) as j:
            mlp(j)

    block.__exit__(None, None, None)


_INS = ["x", "c", "w_ada", "b_ada", "g_pre_mix", "g_post_mix", "w_in", "cmp_pe_k", "cmp_w1_k", "cmp_w2_k", "cmp_pe_v",
        "cmp_w1_v", "cmp_w2_v", "w_pool", "pool_scale", "w_br_nsa", "w_br_pool", "w_out", "g_pre_mlp", "g_post_mlp",
        "w_fc1", "w_fc2"]


def shape_constants():
    half = HEAD_DIM // 2
    inv = (10000.0 ** (-np.arange(half, dtype=np.float64) / half)).astype(np.float32)
    ang = (inv[:, None] * np.arange(SEQ, dtype=np.float32)[None, :]).astype(np.float64)
    cos = np.tile(np.cos(ang), (4, 1)).astype(np.float32)
    sin = np.concatenate([-np.sin(ang), np.sin(ang)] * 2).astype(np.float32)
    cnt = np.minimum(np.arange(16)[None, :] + 1, np.array(POOL_SIZES)[:, None])
    inv_cnt = np.broadcast_to((1.0 / cnt).astype(np.float32), (P, 4, 16)).copy()
    return {"cos": cos, "sin": sin, "inv_cnt": inv_cnt}


def kernel(**inputs):
    import concourse.bacc as bacc
    from concourse.bass_utils import run_bass_kernel_spmd

    nc = bacc.Bacc("TRN2", target_bir_lowering=False, num_devices=1)
    arrays = {n: np.ascontiguousarray(inputs[n]) for n in _INS}
    arrays.update(shape_constants())
    aps = {n: nc.dram_tensor("in_" + n, a.shape, mybir.dt.from_np(a.dtype), kind="ExternalInput").ap()
           for n, a in arrays.items()}
    out = nc.dram_tensor("out", (1, SEQ, D_MODEL), mybir.dt.float32, kind="ExternalOutput").ap()
    hybrid_block(nc, aps, out)
    r = run_bass_kernel_spmd(nc, [{"in_" + n: a for n, a in arrays.items()}], core_ids=[0])
    return r.results[0]["out"]
```

```python
import numpy as np
import concourse.bass as bass
from concourse import mybir

D_MODEL, SEQ, D_FF = 1024, 1024, 4096
N_HEADS, HEAD_DIM, KV_WIDTH = 8, 64, 128
CMP_BLOCK, CMP_STRIDE, WINDOW, SEL_BLOCK, SEL_TOPK = 32, 16, 512, 64, 16
POOL_SIZES = (2, 4, 8, 16)
POOL_WIDTH = 512
EPS = 1e-6
P = 128
KT = D_MODEL // P
TT = SEQ // P
CH = 512
N_CMP = (SEQ - CMP_BLOCK) // CMP_STRIDE + 1
NEG = -1e30
assert SEQ // SEL_BLOCK <= SEL_TOPK

C_Q, C_KC, C_VC, C_KS, C_VS, C_KW, C_VW, C_G, C_U, C_BR = 0, 512, 640, 768, 896, 1024, 1152, 1280, 1304, 1816
N_GATE = 3 * N_HEADS
WV_COLS = 2 * KV_WIDTH + N_GATE

FM_COLS = [C_KC, C_VC] + [C_Q + P * i for i in range(4)] + [C_KS, C_KW] + [C_U + P * i for i in range(4)] \
    + [C_BR + P * i for i in range(16)]
FM_ROPE = {0: 0, 2: 1, 3: 2, 4: 3, 5: 4, 6: 5, 7: 6}
Q_BLOCKS, K_BLOCKS = (2, 3, 4, 5), (6, 7)
N_FM = 12
N_BR = 16
UNITS = TT * N_HEADS // 2
STEPS = 5
SLOTS = 9
HALVES = 2 * N_BR
HALF_OF = dict(zip([i for i in range(UNITS + 1) if i not in (22, 25, 28, 30)], range(2, HALVES - 1)))
assert len(HALF_OF) == HALVES - 3

R_WV, R_FM, R_MERGE, R_OUT, R_MLP = 0, 3, 3 + N_FM + N_BR, 11 + N_FM + N_BR, 19 + N_FM + N_BR
A_MERGE, A_MLP = N_FM + N_BR, N_FM + N_BR + KT


def raw_dmas(r):
    return 2 if r < R_FM or R_MERGE <= r < R_OUT else 1


def raw_count(r):
    return 16 * sum(raw_dmas(x) for x in range(r % 2, r + 1, 2))


def key_tiles(c):
    first = max(0, c - WINDOW // P)
    return [(0, j) for j in range(c + 1)] + [(1, j) for j in range(first, c + 1)] + [(2, 0)]


def n_banks(u):
    return (len(key_tiles(u // 4)) + 1) // 2


BANKS_BEFORE = [sum(n_banks(v) for v in range(u)) for u in range(UNITS + 1)]


def tp_slot(u, b):
    return b * 7 // n_banks(u)


def score_parts(c, branch):
    first = max(0, c - WINDOW // P) * P if branch else 0
    width = (c + 1) * P - first
    if width <= CH:
        return [(first, width, 0)]
    return [(first, width // 2, 0), (first + width // 2, width // 2, CH)]


def hybrid_block(nc, A, out):
    f32, f32r, bf16 = mybir.dt.float32, mybir.dt.float32r, mybir.dt.bfloat16
    ALU, ACT, AX = mybir.AluOpType, mybir.ActivationFunctionType, mybir.AxisListType

    def place(name, kb, shape, dt):
        pad = nc.sbuf_tensor(name + "_pad", [P, int(kb * 1024)], mybir.dt.uint8) if kb else None
        if pad:
            pad.__enter__()
        guard = nc.sbuf_tensor(name, shape, dt)
        t = guard.__enter__()
        guard.__exit__(None, None, None)
        if pad:
            pad.__exit__(None, None, None)
        return t

    def sem(name):
        return nc.semaphore(name).__enter__()

    def full(t):
        return t.bitcast(f32)

    ident = place("ident", 0, [P, P], f32)
    ones = place("ones", 0.5, [P, P], f32)
    ident_b = place("ident_b", 1, [P, P], bf16)
    mask_diag = place("mask_diag", 1.25, [P, P], bf16)
    mask_far = place("mask_far", 1.5, [P, P], bf16)
    mask_cmp = place("mask_cmp", 1.75, [P, TT, 64], bf16)
    gates = place("gates", 2.75, [P, TT, N_GATE], f32)
    col = place("col", 3.5, [P, 128], f32)
    c_col, silu_c, g_pre = col[:, 0:8], col[:, 8:16], col[:, 16:24]
    g_mlp, pool_sc, shift, scale = col[:, 24:32], col[:, 32:36], col[:, 40:48], col[:, 48:56]
    msq, rstd, half_neg = col[:, 56:64], col[:, 64:72], col[:, 72:76]
    stat = col[:, 80:128]
    smax = place("smax", 4, [P, 4, 2], f32)
    negm = place("negm", 4.125, [P, 4, 2], f32)
    ssum = place("ssum", 4.25, [P, 4, 2], f32)
    srec = place("srec", 4.375, [P, 4, 2], f32)
    inv_cnt = place("inv_cnt", 4.5, [P, 4, 16], f32)
    pe_col = place("pe_col", 4.75, [P, 2, 16], f32)
    w2k = place("w2k", 5, [64, 64], f32)
    w2v = place("w2v", 5.25, [64, 64], f32)
    gelu_x = place("gelu_x", 5.5, [64, 2, 126], f32)
    gelu_t = place("gelu_t", 6.5, [64, 2, 126], f32)
    col2 = place("col2", 7.5, [P, 16], f32)
    shift2, scale2 = col2[:, 0:8], col2[:, 8:16]
    raw = place("raw", 8, [P, 2, 1024], f32)
    a_hi = place("a_hi", 16, [P, 2, 1024], f32r)
    a_lo = place("a_lo", 24, [P, 2, 1024], f32r)
    act_hi = place("act_hi", 32, [P, KT, SEQ], f32r)
    act_lo = place("act_lo", 64, [P, KT, SEQ], f32r)
    k_hi = place("k_hi", 96, [P, 4, SEQ], f32r)
    k_lo = place("k_lo", 112, [P, 4, SEQ], f32r)
    v_st = place("v_st", 128, [P, TT, 4, P], f32r)
    kc_hi = place("kc_hi", 144, [P, 2, 64], f32r)
    kc_lo = place("kc_lo", 144.5, [P, 2, 64], f32r)
    vc_st = place("vc_st", 145, [P, 2, P], f32r)
    xt = place("xt", 96, [P, TT, D_MODEL], f32)
    ada = place("ada", 128, [P, 4, 1024], f32)
    ada_acc = place("ada_acc", 146, [P, 2048], f32)
    h_tmp = place("h_tmp", 154, [P, 2, CH], f32)
    acc2 = place("acc2", 96, [P, 4, 1024], f32)
    ada2 = place("ada2", 112, [P, 4, 1024], f32)
    junk = place("junk", 166, [P, 1024], f32)
    kc_f = place("kc_f", 146, [P, SEQ], f32)
    vc_f = place("vc_f", 150, [P, SEQ], f32)
    cw1 = place("cw1", 154, [P, 16, 64], f32)
    cos = place("cos", 158, [P, SEQ], f32)
    sin = place("sin", 162, [P, SEQ], f32)
    r_swap = place("r_swap", 166, [P, 2, CH], f32)
    r_cos = place("r_cos", 170, [P, 2, CH], f32)
    r_sin = place("r_sin", 174, [P, 2, CH], f32)
    r_hi = place("r_hi", 178, [P, 2, CH], f32r)
    r_lo = place("r_lo", 182, [P, 2, CH], f32r)
    wv_hi = place("wv_hi", 186, [P, KT, WV_COLS], f32r)
    wv_lo = place("wv_lo", 194.75, [P, KT, WV_COLS], f32r)
    bkx = place("bkx", 186, [P, 2, SEQ], f32)
    bk = place("bk", 194, [P, 16, 2, N_CMP], f32)
    PAD = 16
    pu = place("pu", 186, [P, PAD + SEQ], f32)
    ps_ab = [place("ps_a", 190.25, [P, PAD + SEQ], f32), place("ps_b", 194.5, [P, PAD + SEQ], f32)]
    pp_hi = place("pp_hi", 158, [P, SEQ], f32r)
    pp_lo = place("pp_lo", 162, [P, SEQ], f32r)
    wp_raw = place("wp_raw", 166, [P, 4, P], f32)
    wp_hi = place("wp_hi", 168, [P, 4, P], f32r)
    wp_lo = place("wp_lo", 170, [P, 4, P], f32r)
    pm = place("pm", 172, [P, 2, CH], f32)
    q_st = place("q_st", 146, [P, 2, N_HEADS, P], f32r)
    p_sel = place("p_sel", 154, [P, 2, 2, SEQ], f32)
    p_win = place("p_win", 170, [P, 2, 2, 640], f32)
    p_cmp = place("p_cmp", 180, [P, 2, 2, P], f32)
    pt_hi = place("pt_hi", 182, [P, 3, CH], f32r)
    pt_lo = place("pt_lo", 188, [P, 3, CH], f32r)
    o_tmp = place("o_tmp", 194, [64, 2, 256], f32)
    o_out = place("o_out", 196, [64, 2, 256], f32)
    g_out = place("g_out", 198.75, [P, 2, CH], f32)
    op_hi = place("op_hi", 96, [P, KT, SEQ], f32r)
    op_lo = place("op_lo", 128, [P, KT, SEQ], f32r)
    stage = place("stage", 160, [P, 2, 1024], f32)
    mg = place("mg", 184, [P, 2, 2, CH], f32)
    m_a = place("m_a", 192, [P, 2, SEQ], f32)
    m_b = place("m_b", 200, [P, 2, CH], f32)
    b_at = (168, 176, 96, 104, 112, 120)
    b_hi = [place(f"b_hi{i}", kb, [P, 1024], f32r) for i, kb in enumerate(b_at)]
    b_lo = [place(f"b_lo{i}", kb + 4, [P, 1024], f32r) for i, kb in enumerate(b_at)]
    y = place("y", 128, [P, TT, D_MODEL], f32)
    gt1 = place("gt1", 160, [P, 1024], f32)
    gt2 = place("gt2", 164, [P, 1024], f32)
    x_in = place("x_in", 184, [P, 2, 1024], f32)
    x1 = place("x1", 192, [P, 2, 1024], f32)
    junk2 = place("junk2", 200, [P, 1024], bf16)
    h2_tmp = place("h2_tmp", 202, [P, 2, CH], f32)
    hid_hi = place("hid_hi", 112, [P, 4, SEQ], f32r)
    hid_lo = place("hid_lo", 184, [P, 4, SEQ], f32r)
    relu = place("relu", 200, [P, 2, CH], f32)
    x1_in = place("x1_in", 32, [P, 2, 1024], f32)
    fin = place("fin", 40, [P, 2, 1024], f32)
    junk3 = place("junk3", 48, [P, 1024], bf16)

    ps = nc.psum_tensor("ps", [P, 8, CH], f32).__enter__()

    q_dram = nc.dram_tensor("q_dram", (TT, P, N_HEADS, P), f32, kind="Internal").ap()
    pool_dram = nc.dram_tensor("pool_dram", (POOL_WIDTH, SEQ), f32, kind="Internal").ap()
    o_dram = nc.dram_tensor("o_dram", (N_HEADS * HEAD_DIM, SEQ), f32, kind="Internal").ap()
    g_dram = nc.dram_tensor("g_dram", (2, KT, 2, P, CH), f32, kind="Internal").ap()
    gt_dram = nc.dram_tensor("gt_dram", (2, D_MODEL), f32, kind="Internal").ap()
    x1_dram = nc.dram_tensor("x1_dram", (SEQ, D_MODEL), f32, kind="Internal").ap()

    x_v = A["x"][0].rearrange("(t p) d -> p t d", p=P)
    x1_v = x1_dram.rearrange("(t p) d -> p t d", p=P)
    out_v = out[0].rearrange("(t p) d -> p t d", p=P)
    w_ada, b_ada = A["w_ada"][0], A["b_ada"]
    w_in_v = A["w_in"][0].rearrange("(k p) n -> p k n", p=P)
    w_brn_v = A["w_br_nsa"][0].rearrange("(k p) n -> p k n", p=P)
    w_brp_v = A["w_br_pool"][0].rearrange("(k p) n -> p k n", p=P)
    w_out_v = A["w_out"][0].rearrange("(k p) n -> p k n", p=P)
    w_fc1_v = A["w_fc1"][0].rearrange("(k p) n -> p k n", p=P)
    w_fc2_v = A["w_fc2"][0].rearrange("(k p) n -> p k n", p=P)

    c_in, g_pre_in = sem("c_in"), sem("g_pre_in")
    const_in, cos_in, wp_in = sem("const_in"), sem("cos_in"), sem("wp_in")
    consts_made, acc_zero, acc_bias = sem("consts_made"), sem("acc_zero"), sem("acc_bias")
    silu_t, silu_done = sem("silu_t"), sem("silu_done")
    ada_in = [sem(f"ada_in{i}") for i in range(4)]
    ada_added, mod_mm, mod_done = sem("ada_added"), sem("mod_mm"), sem("mod_done")
    x_arr = [sem(f"x_arr{i}") for i in range(TT)]
    x_sq, x_ms, x_rstd, x_norm = sem("x_sq"), sem("x_ms"), sem("x_rstd"), sem("x_norm")
    xt_mm, h_made, h_hi, h_lo = sem("xt_mm"), sem("h_made"), sem("h_hi"), sem("h_lo")
    raw_in = [sem("raw_in0"), sem("raw_in1")]
    hi_done, lo_done = sem("hi_done"), sem("lo_done")
    v_mm, v_hi, v_lo = sem("v_mm"), sem("v_hi"), sem("v_lo")
    fm_mm, fm_act = sem("fm_mm"), sem("fm_act")
    rope_cos, rope_sin, rope_sum, rope_hi, rope_lo = (sem("rope_" + n) for n in ("cos", "sin", "sum", "hi", "lo"))
    rope_out = [sem("rope_out0"), sem("rope_out1")]
    cw_in, bkx_in, bk_made = sem("cw_in"), sem("bkx_in"), sem("bk_made")
    cmp_mm, gelu_c, gelu_d, cmp2_mm = sem("cmp_mm"), sem("gelu_c"), sem("gelu_d"), sem("cmp2_mm")
    cmp_hi, cmp_lo = sem("cmp_hi"), sem("cmp_lo")
    pool_zero, pool_add, pooled, pooled_hi, pooled_lo = (
        sem(n) for n in ("pool_zero", "pool_add", "pooled", "pooled_hi", "pooled_lo"))
    wp_hi_s, wp_lo_s, mix_mm, mix_out = sem("wp_hi_s"), sem("wp_lo_s"), sem("mix_mm"), sem("mix_out")
    mix_st = [sem("mix_st0"), sem("mix_st1")]
    gates_done, cmp_zero = sem("gates_done"), sem("cmp_zero")
    q_in = [sem("q_in0"), sem("q_in1")]
    score_mm, max_done, negm_done, exp_done, guard_done, rec_done, norm_done = (
        sem(n) for n in ("score_mm", "max_done", "negm_done", "exp_done", "guard_done", "rec_done", "norm_done"))
    tp_mm, pthi, ptlo, pv_mm = (sem(n) for n in ("tp_mm", "pthi", "ptlo", "pv_mm"))
    o_half, o_sum, gate_mm, gate_tanh = sem("o_half"), sem("o_sum"), sem("gate_mm"), sem("gate_tanh")
    o_st = [sem("o_st0"), sem("o_st1")]
    g_st = [sem("g_st0"), sem("g_st1")]
    stage_in = [sem("stage_in0"), sem("stage_in1")]
    op_hi_s, op_lo_s, acc2_zero, acc2_bias, ada2_added = (
        sem(n) for n in ("op_hi_s", "op_lo_s", "acc2_zero", "acc2_bias", "ada2_added"))
    ada2_in = [sem(f"ada2_in{i}") for i in range(4)]
    gp_row_in, gt_mm, gt_row, gt_st, gt_in = (sem(n) for n in ("gp_row_in", "gt_mm", "gt_row", "gt_st", "gt_in"))
    merge_pool = sem("merge_pool")
    mg_in = [sem("mg_in0"), sem("mg_in1")]
    merge_mm, merge_ab, merge_sum, merge_hi, merge_lo = (
        sem(n) for n in ("merge_mm", "merge_ab", "merge_sum", "merge_hi", "merge_lo"))
    mod2_mm, mod2_done = sem("mod2_mm"), sem("mod2_done")
    pooled_w, y_gated, x1n_made, f_gated = sem("pooled_w"), sem("y_gated"), sem("x1n_made"), sem("f_gated")
    y_mm, y_out, y_ms, y_rstd, y_scaled, x1_made, x1_ms, x1_rstd, x1_norm = (
        sem(n) for n in ("y_mm", "y_out", "y_ms", "y_rstd", "y_scaled", "x1_made", "x1_ms", "x1_rstd", "x1_norm"))
    xi_in = [sem("xi_in0"), sem("xi_in1")]
    x1_st = [sem("x1_st0"), sem("x1_st1")]
    x1t_mm, h2_made, h2_hi, h2_lo = sem("x1t_mm"), sem("h2_made"), sem("h2_hi"), sem("h2_lo")
    fc1_mm, relu_done, sq_done, hid_hi_s, hid_lo_s = (
        sem(n) for n in ("fc1_mm", "relu_done", "sq_done", "hid_hi_s", "hid_lo_s"))
    fc2_mm, y2_added = sem("fc2_mm"), sem("y2_added")
    x1i_in = [sem("x1i_in0"), sem("x1i_in1")]
    f_ms, f_rstd, f_scaled, f_made = sem("f_ms"), sem("f_rstd"), sem("f_scaled"), sem("f_made")
    out_st = [sem("out_st0"), sem("out_st1")]

    OUT_SLOT = (0, 1, 2, 3, 4, 5, 0, 1)
    MLP_SPLITS = ((), (), (2,), (3,), (4,), (5, 6), (7,), ())
    N_SMALL, CONSTS = 7, 12
    ROPES = 2 * len(FM_ROPE)
    K_DMAS, Q_DMAS = 8, 4

    def rope_out_count(i):
        return 16 * sum((Q_DMAS if j < 10 else K_DMAS) for j in range(2 + i % 2, i + 1, 2))

    ADD_AT, n_pieces = {}, 0
    for a, count in enumerate((4, 7, 4, 3, 5, 3, 6)):
        ADD_AT.update((n, a) for n in range(n_pieces, n_pieces + count))
        n_pieces += count
    assert n_pieces == 4 * KT
    LOAD_AT = {n: ADD_AT[n - 4] + 2 if n >= 4 else 1 for n in range(4 * KT)}

    block = nc.Block().__enter__()

    @block.sync
    def _(sp):
        def load_raw(r, count_only=False, **src):
            if r >= 2:
                sp.wait_ge(lo_done, r - 1)
            for dst, s in src["parts"]:
                sp.dma_start(dst, s).then_inc(raw_in[r % 2], 16)

        def raw_k(r):
            return raw[:, r % 2, :].rearrange("p (k n) -> p k n", n=P)

        def ada_piece(n):
            if n >= 4:
                sp.wait_ge(ada_added, n - 3)
            k, part = n % KT, 1 - n // KT
            sp.dma_start(ada[:, n % 4, :], w_ada[k * P:(k + 1) * P, part * 1024:(part + 1) * 1024]) \
              .then_inc(ada_in[n % 4], 16)

        with nc.allow_non_contiguous_dma(reason="a few columns"):
            sp.dma_start(c_col, A["c"].rearrange("a (k p) -> p (a k)", p=P)).then_inc(c_in, 16)
        for n in range(4):
            ada_piece(n)
        sp.wait_ge(acc_zero, 1)
        sp.dma_start(ada_acc[0:1, :], b_ada[:, 0:2048]).then_inc(acc_bias, 16)
        with nc.allow_non_contiguous_dma(reason="a few columns"):
            sp.dma_start(g_pre, A["g_pre_mix"].rearrange("a (k p) -> p (a k)", p=P)).then_inc(g_pre_in, 16)
        for n in range(4, 16):
            ada_piece(n)
            if n % 2:
                t = n // 2 - 2
                sp.dma_start(xt[:, t, :], x_v[:, t, :]).then_inc(x_arr[t], 16)
        for t in (6, 7):
            sp.dma_start(xt[:, t, :], x_v[:, t, :]).then_inc(x_arr[t], 16)
        for r, (k0, k1) in enumerate(((0, 3), (3, 6), (6, 8))):
            dst = raw[:, r % 2, 0:(k1 - k0) * WV_COLS].rearrange("p (k n) -> p k n", n=WV_COLS)
            load_raw(r, parts=((dst[:, :, 0:P], w_in_v[:, k0:k1, C_VS:C_VS + P]),
                               (dst[:, :, P:WV_COLS], w_in_v[:, k0:k1, C_VW:C_VW + P + N_GATE])))
        with nc.allow_non_contiguous_dma(reason="a few columns"):
            for dst, s in ((g_mlp, A["g_pre_mlp"].rearrange("a (k p) -> p (a k)", p=P)),
                           (pool_sc, A["pool_scale"].rearrange("a (k p) -> p (a k)", p=P)),
                           (inv_cnt[:, :, :], A["inv_cnt"]),
                           (pe_col[:, 0, :], A["cmp_pe_k"][0].rearrange("(l two) d -> (two d) l", two=2)),
                           (pe_col[:, 1, :], A["cmp_pe_v"][0].rearrange("(l two) d -> (two d) l", two=2)),
                           (w2k[:, :], A["cmp_w2_k"][0]), (w2v[:, :], A["cmp_w2_v"][0])):
                sp.dma_start(dst, s).then_inc(const_in, 16)
        sp.dma_start(cos[:, :], A["cos"]).then_inc(cos_in, 16)
        sp.dma_start(sin[:, :], A["sin"]).then_inc(cos_in, 16)

        def ada2_piece(n):
            if n < 4:
                sp.wait_ge(xt_mm, 2 * KT)
            else:
                sp.wait_ge(ada2_added, n - 3)
            k, part = n // 4, n % 4
            sp.dma_start(ada2[:, part, :], w_ada[k * P:(k + 1) * P, 2048 + part * 1024:3072 + part * 1024]) \
              .then_inc(ada2_in[part], 16)

        def rope_stores(a):
            for ch in range(2):
                i = 2 * FM_ROPE[a] + ch
                sp.wait_ge(rope_lo, i - 1)
                for part, kd in ((r_hi, k_hi), (r_lo, k_lo)):
                    for g in range(2):
                        src = full(part[64 * g:64 * g + 64, i % 2, :])
                        if a in K_BLOCKS:
                            for half in range(2):
                                sp.dma_start(full(kd[64 * half:64 * half + 64, 2 * (a - K_BLOCKS[0]) + g, ch * CH:(ch + 1) * CH]),
                                             src).then_inc(rope_out[i % 2], 16)
                        else:
                            row = 0 if part is r_hi else 64
                            sp.dma_start(q_dram[4 * ch:4 * ch + 4, row:row + 64, 2 * (a - Q_BLOCKS[0]) + g, :]
                                         .rearrange("c d q -> d c q"),
                                         src.rearrange("d (c q) -> d c q", q=P)).then_inc(rope_out[i % 2], 16)

        def cmp_load(kv):
            if kv:
                sp.wait_ge(cmp_mm, 1)
            else:
                sp.wait_ge(h_lo, 16)
            sp.dma_start(cw1[:, :, :], A["cmp_w1_v" if kv else "cmp_w1_k"][0]
                         .rearrange("(l p) j -> p l j", p=P)).then_inc(cw_in, 16)
            if kv:
                sp.wait_ge(fm_act, 4)
                sp.wait_ge(bk_made, 1)
            else:
                sp.wait_ge(rope_sum, 2)
                sp.wait_ge(v_mm, TT)
            src = vc_f if kv else kc_f
            for g in range(2):
                for odd in range(2):
                    sp.dma_start(bkx[64 * odd:64 * odd + 64, g, 0:SEQ - odd],
                                 src[64 * g:64 * g + 64, odd:SEQ]).then_inc(bkx_in, 16)

        def bias2():
            sp.wait_ge(acc2_zero, 1)
            sp.dma_start(acc2[0:1, :, :], b_ada[:, 2048:6144].rearrange("a (f n) -> a f n", n=1024)) \
              .then_inc(acc2_bias, 16)

        for a in range(N_FM):
            r = R_FM + a
            load_raw(r, parts=((raw_k(r), w_in_v[:, :, FM_COLS[a]:FM_COLS[a] + P]),))
            if a == 1:
                bias2()
            if a == 3:
                cmp_load(0)
            if a == 6:
                cmp_load(1)
            for n in range(4 * KT):
                if LOAD_AT[n] == a:
                    ada2_piece(n)
            if a == 8:
                for f, g in enumerate(("g_post_mix", "g_post_mlp")):
                    sp.wait_ge(ada2_added, 4 * KT)
                    sp.dma_start(ada2[0:1, f, :], A[g]).then_inc(gp_row_in, 16)
            if a == 9:
                sp.wait_ge(gt_row, 4)
                sp.dma_start(gt_dram.rearrange("(a f) n -> a f n", a=1), ada2[0:1, 0:2, :]).then_inc(gt_st, 16)
                sp.wait_ge(gt_st, 16)
                sp.wait_ge(mod2_mm, 1)
                rope_stores(6)
            if a - 2 in FM_ROPE and a - 2 not in (0, 6):
                rope_stores(a - 2)
            if a == N_FM - 1:
                sp.wait_ge(rope_sum, ROPES)
                sp.wait_ge(rope_lo, ROPES - 2)
                sp.dma_start(wp_raw[:, :, :], A["w_pool"][0].rearrange("g c d -> c g d")).then_inc(wp_in, 16)

        def load_q(c):
            if c == 0:
                for s in range(2):
                    sp.wait_ge(rope_out[s], rope_out_count(ROPES - 2 + s))
                sp.wait_ge(bkx_in, 128)
            if c >= 2:
                sp.wait_ge(score_mm, STEPS * 4 * (c - 1))
            sp.dma_start(full(q_st[:, c % 2, :, :]), q_dram[c]).then_inc(q_in[c % 2], 16)

        load_q(0)
        load_q(1)
        for m in range(N_BR):
            r = R_FM + N_FM + m
            load_raw(r, parts=((raw_k(r), w_in_v[:, :, FM_COLS[N_FM + m]:FM_COLS[N_FM + m] + P]),))
            if m % 2 == 1 and m // 2 + 1 < TT and m >= 3:
                load_q(m // 2 + 1)

        def merge_loads(q, first=False):
            for b in range(2):
                r = R_MERGE + b
                sp.wait_ge(lo_done, 2 * q + (r - 1))
                cols = bass.ds(2 * P * q + b * P, P)
                sp.dma_start(raw_k(r)[:, 0:4, :], w_brp_v[:, :, cols]).then_inc(raw_in[r % 2], 16)
                sp.dma_start(raw_k(r)[:, 4:8, :], w_brn_v[:, :, cols]).then_inc(raw_in[r % 2], 16)
                for ch in range(2):
                    if not (first and b == 0):
                        sp.wait_ge(merge_ab, 4 * q + (2 * b + ch - 1))
                    sp.dma_start(mg[:, ch, :, :], g_dram[:, bass.ds(2 * q + b, 1), ch, :, :]
                                 .rearrange("h m p n -> p (h m) n")).then_inc(mg_in[ch], 16)

        sp.wait_ge(pv_mm, BANKS_BEFORE[UNITS])
        for s in range(2):
            sp.wait_ge(mix_st[s], 16 * 4)
        for i in range(8):
            if i == 4:
                for s in range(2):
                    sp.wait_ge(o_st[s], 16 * UNITS // 2)
            if i >= 2:
                sp.wait_ge(op_lo_s, i - 1)
            src = pool_dram if i < 4 else o_dram
            sp.dma_start(stage[:, i % 2, :], src[(i % 4) * P:(i % 4 + 1) * P, :]).then_inc(stage_in[i % 2], 16)
        for s in range(2):
            sp.wait_ge(g_st[s], 16 * HALVES // 2)
        merge_loads(0, first=True)
        with sp.Fori(1, KT // 2) as q:
            merge_loads(q)

        for n in range(8):
            r, half, s = R_OUT + n, n // 4, n % 4
            sp.wait_ge(lo_done, r - 1)
            sp.dma_start(raw[:, r % 2, :].rearrange("p (k n) -> p k n", n=CH),
                         w_out_v[:, 2 * s:2 * s + 2, half * CH:(half + 1) * CH]).then_inc(raw_in[r % 2], 16)
            if n == 3:
                sp.wait_ge(op_lo_s, 8)
                for f, dst in enumerate((gt1, gt2)):
                    sp.dma_start(dst[:, :], gt_dram[f:f + 1, :].to_broadcast([P, D_MODEL])).then_inc(gt_in, 16)
                sp.wait_ge(merge_lo, KT)
                for t in range(2):
                    sp.dma_start(x_in[:, t, :], x_v[:, t, :]).then_inc(xi_in[t], 16)

        def mlp_loads(j, ns=range(8)):
            for n in ns:
                sp.wait_ge(lo_done, 8 * j + (R_MLP + n - 1))
                s = (R_MLP + n) % 2
                if n < 4:
                    src = w_fc1_v[:, :, bass.ds(j * CH + n * P, P)]
                    sp.dma_start(raw_k(s), src).then_inc(raw_in[s], 16)
                else:
                    sp.dma_start(raw[:, s, :], w_fc2_v[:, bass.ds(4 * j + (n - 4), 1), :]
                                 .rearrange("p k n -> p (k n)")).then_inc(raw_in[s], 16)

        for t in range(2, TT):
            sp.wait_ge(x1_made, t - 1)
            sp.dma_start(x_in[:, t % 2, :], x_v[:, t, :]).then_inc(xi_in[t % 2], 16)
            if t == 5:
                mlp_loads(0, range(0, 2))
        mlp_loads(0, range(2, 8))
        with sp.Fori(1, D_FF // CH) as j:
            mlp_loads(j)
        sp.wait_ge(fc1_mm, 8 * (D_FF // CH))
        for s in range(2):
            sp.wait_ge(x1_st[s], 16 * TT // 2)
        for t in range(TT):
            if t >= 2:
                sp.wait_ge(f_made, t - 1)
            sp.dma_start(x1_in[:, t % 2, :], x1_v[:, t, :]).then_inc(x1i_in[t % 2], 16)
        for s in range(2):
            sp.wait_ge(out_st[s], 16 * TT // 2)

    @block.gpsimd
    def _(pool):
        def made(ins):
            made.n += 1
            ins.then_inc(consts_made, 1)
        made.n = 0
        pool.memset(ada_acc[:, :], 0.0).then_inc(acc_zero, 1)
        for t, v in ((ident, 0.0), (ident_b, 0.0), (mask_diag, 0.0), (mask_far, 0.0), (ones, 1.0), (half_neg, -0.5)):
            made(pool.memset(t if t is half_neg else t[:, :], v))
        made(pool.memset(mask_cmp[:, :, :], 0.0))
        pool.wait_ge(consts_made, made.n)
        for t in (ident, ident_b):
            made(pool.affine_select(out=t[:, :], in_=t[:, :], compare_op=ALU.not_equal, fill=1.0,
                                    base=0, pattern=[[-1, P]], channel_multiplier=1))
        made(pool.affine_select(out=mask_diag[:, :], in_=mask_diag[:, :], compare_op=ALU.is_ge, fill=NEG,
                                base=0, pattern=[[-1, P]], channel_multiplier=1))
        made(pool.affine_select(out=mask_far[:, :], in_=mask_far[:, :], compare_op=ALU.is_gt, fill=NEG,
                                base=0, pattern=[[1, P]], channel_multiplier=-1))
        made(pool.affine_select(out=mask_cmp[:, :, :], in_=mask_cmp[:, :, :], compare_op=ALU.is_ge, fill=NEG,
                                base=1 - CMP_BLOCK, pattern=[[P, TT], [-CMP_STRIDE, 64]], channel_multiplier=1))
        assert made.n == CONSTS
        pool.memset(full(kc_hi[:, :, :]), 0.0).then_inc(cmp_zero, 1)
        pool.memset(full(kc_lo[:, :, :]), 0.0).then_inc(cmp_zero, 1)
        pool.memset(full(vc_st[:, :, :]), 0.0).then_inc(cmp_zero, 1)
        for ch in range(2):
            sl = slice(4 * ch, 4 * ch + 4)
            pool.wait_ge(x_sq, 4 * ch + 4)
            pool.tensor_scalar(msq[:, sl], msq[:, sl], 1.0 / D_MODEL, EPS, ALU.mult, ALU.add).then_inc(x_ms, 1)
            pool.wait_ge(x_ms, ch + 1)
            pool.tensor_tensor(rstd[:, sl], msq[:, sl], half_neg, ALU.pow).then_inc(x_rstd, 1)
        pool.wait_ge(xt_mm, 2 * KT)
        pool.memset(acc2[:, :, :], 0.0).then_inc(acc2_zero, 1)
        pool.wait_ge(cos_in, 32)
        for a, k in FM_ROPE.items():
            for ch in range(2):
                i, sl = 2 * k + ch, slice(ch * CH, (ch + 1) * CH)
                pool.wait_ge(fm_act, 2 * a + ch + 1)
                pool.tensor_tensor(r_sin[:, i % 2, :], r_swap[:, i % 2, :], sin[:, sl], ALU.mult).then_inc(rope_sin, 1)
                pool.wait_ge(rope_sin, i + 1)
                pool.wait_ge(rope_cos, i + 1)
                dst = kc_f[:, sl] if a == 0 else r_cos[:, i % 2, :]
                pool.tensor_tensor(dst, r_cos[:, i % 2, :], r_sin[:, i % 2, :], ALU.add).then_inc(rope_sum, 1)
        pool.wait_ge(cmp_mm, 2)
        for t in (pu, ps_ab[0], ps_ab[1]):
            pool.memset(t[:, 0:PAD], 0.0).then_inc(pool_zero, 1)
        pool.wait_ge(pool_zero, 3)
        n_add = 0

        def mix_store(g):
            for n in (2 * g, 2 * g + 1):
                pool.wait_ge(mix_out, n + 1)
                pool.dma_start(pool_dram[g * P:(g + 1) * P, (n % 2) * CH:(n % 2 + 1) * CH],
                               pm[:, n % 2, :]).then_inc(mix_st[n % 2], 16)

        for g in range(4):
            pool.wait_ge(fm_act, 2 * (8 + g) + 2)
            if g:
                pool.wait_ge(pooled_lo, g)
            src = pu
            for step in range(g + 1):
                dst, back = ps_ab[step % 2], 1 << step
                if step:
                    pool.wait_ge(pool_add, n_add)
                pool.tensor_tensor(dst[:, PAD:], src[:, PAD:], src[:, PAD - back:PAD + SEQ - back], ALU.add) \
                    .then_inc(pool_add, 1)
                n_add += 1
                src = dst
            if g:
                mix_store(g - 1)
        mix_store(3)
        pool.wait_ge(rope_out[0], rope_out_count(ROPES - 2))
        pool.wait_ge(rope_out[1], rope_out_count(ROPES - 1))
        pool.memset(p_cmp[:, :, :, :], 0.0).then_inc(cmp_zero, 1)
        def gate_store(h):
            m = h // 2
            pool.wait_ge(gate_tanh, h + 1)
            pool.dma_start(g_dram[m // KT, m % KT, h % 2], g_out[:, h % 2, :]).then_inc(g_st[h % 2], 16)

        gate_store(0)
        gate_store(1)
        for it in range(UNITS + 1):
            if it in HALF_OF:
                gate_store(HALF_OF[it])
            if it:
                v = it - 1
                pool.wait_ge(o_sum, v + 1)
                c, pair = v // 4, v % 4
                pool.dma_start(o_dram[pair * P:(pair + 1) * P, c * P:(c + 1) * P].rearrange("(h d) q -> d h q", h=2),
                               o_out[:, v % 2, :].rearrange("d (h q) -> d h q", h=2)).then_inc(o_st[v % 2], 16)
        gate_store(HALVES - 1)

        with pool.Fori(0, KT // 2) as q:
            for b in range(2):
                for ch in range(2):
                    sl = slice(ch * CH, (ch + 1) * CH)
                    pool.wait_ge(merge_ab, 4 * q + (2 * b + ch + 1))
                    pool.tensor_tensor(m_a[:, b, sl], m_a[:, b, sl], m_b[:, ch, :], ALU.add).then_inc(merge_sum, 1)

        def rstd_of(ms, sem_in, sem_ms, sem_out, t):
            pool.wait_ge(sem_in, t + 1)
            pool.tensor_scalar(ms, ms, 1.0 / D_MODEL, EPS, ALU.mult, ALU.add).then_inc(sem_ms, 1)
            pool.wait_ge(sem_ms, t + 1)
            pool.tensor_tensor(ms, ms, half_neg[:, 0:1], ALU.pow).then_inc(sem_out, 1)

        for t in range(TT):
            rstd_of(stat[:, t:t + 1], y_ms, y_scaled, y_rstd, t)
            rstd_of(stat[:, 8 + t:9 + t], x1_ms, x1_norm, x1_rstd, t)
            pool.dma_start(x1_v[:, t, :], x1[:, t % 2, :]).then_inc(x1_st[t % 2], 16)

        def squares(j):
            for n in range(8):
                pool.wait_ge(relu_done, 8 * j + (n + 1))
                pool.tensor_tensor(relu[:, n % 2, :], relu[:, n % 2, :], relu[:, n % 2, :], ALU.mult).then_inc(sq_done, 1)

        squares(0)
        with pool.Fori(1, D_FF // CH) as j:
            squares(j)
        for t in range(TT):
            rstd_of(stat[:, 16 + t:17 + t], f_ms, f_scaled, f_rstd, t)
            pool.wait_ge(f_made, t + 1)
            pool.dma_start(out_v[:, t, :], fin[:, t % 2, :]).then_inc(out_st[t % 2], 16)

    @block.scalar
    def _(act):
        def split_hi(r, dst, free):
            act.wait_ge(raw_in[r % 2], raw_count(r))
            if free:
                act.wait_ge(*free)
            act.activation(dst, raw[:, r % 2, :], ACT.Copy).then_inc(hi_done, 1)

        def split_a(a):
            free = None
            if a >= 2:
                free = (fm_mm, 2 * a - 2) if a - 2 < N_FM else (gate_mm, 2 * (a - 2 - N_FM) + 2)
            split_hi(R_FM + a, a_hi[:, a % 2, :], free)

        act.wait_ge(c_in, 16)
        act.activation(silu_c, c_col, ACT.Tanh, scale=0.5).then_inc(silu_t, 1)
        for ch in range(2):
            for t in range(4 * ch, 4 * ch + 4):
                act.wait_ge(x_arr[t], 16)
                if t:
                    act.wait_ge(x_sq, t)
                act.activation(junk[:, :], xt[:, t, :], ACT.Square, accum_out=msq[:, t:t + 1]).then_inc(x_sq, 1)
        for r, (k0, k1) in enumerate(((0, 3), (3, 6), (6, 8))):
            act.wait_ge(raw_in[r % 2], raw_count(r))
            act.activation(wv_hi[:, k0:k1, :], raw[:, r % 2, 0:(k1 - k0) * WV_COLS]
                           .rearrange("p (k n) -> p k n", n=WV_COLS), ACT.Copy).then_inc(hi_done, 1)
        def v_evict(t):
            b = 4 + t % 4
            act.wait_ge(v_mm, t + 1)
            act.activation(v_st[:, t, :, 0:64], ps[:, b, 0:256].rearrange("p (f d) -> p f d", d=64),
                           ACT.Copy).then_inc(v_hi, 1)
            act.activation(gates[:, t, :], ps[:, b, 256:WV_COLS], ACT.Tanh, scale=0.5).then_inc(v_hi, 1)

        act.wait_ge(mod_done, 2)
        for n in range(2 * KT):
            act.wait_ge(xt_mm, n + 1)
            if n >= 2:
                act.wait_ge(h_lo, n - 1)
            k = n % KT
            act.activation(h_tmp[:, n % 2, :], ps[:, n % 4, :], ACT.Identity, scale=scale[:, k:k + 1],
                           bias=shift[:, k:k + 1]).then_inc(h_made, 1)
            if n >= 12:
                v_evict(n - 12)
        split_a(0)
        split_a(1)
        for t in range(4, TT):
            v_evict(t)

        def rope_hi_part(i):
            act.wait_ge(rope_sum, i + 1)
            if i >= 4:
                act.wait_ge(rope_out[i % 2], rope_out_count(i - 2))
            act.activation(r_hi[:, i % 2, :], r_cos[:, i % 2, :], ACT.Copy).then_inc(rope_hi, 1)

        def fm_evict(a, ch):
            g = 2 * a + ch
            act.wait_ge(fm_mm, g + 1)
            bank, sl = g % 4, slice(ch * CH, (ch + 1) * CH)
            if a in FM_ROPE:
                i = 2 * FM_ROPE[a] + ch
                if i >= 2:
                    act.wait_ge(rope_sin, i - 1)
                for q in range(4):
                    ins = act.activation(r_swap[32 * q:32 * q + 32, i % 2, :],
                                         ps[32 * (q ^ 1):32 * (q ^ 1) + 32, bank, :], ACT.Copy)
                ins.then_inc(fm_act, 1)
            elif a == 1:
                act.activation(vc_f[:, sl], ps[:, bank, :], ACT.Copy).then_inc(fm_act, 1)
            else:
                if ch == 0:
                    if a == 8:
                        act.wait_ge(pool_zero, 3)
                    else:
                        act.wait_ge(pooled_lo, a - 8)
                act.activation(pu[:, PAD + ch * CH:PAD + (ch + 1) * CH], ps[:, bank, :], ACT.Copy).then_inc(fm_act, 1)

        def gelu(kv):
            act.wait_ge(cmp_mm, kv + 1)
            act.activation(gelu_x[:, kv, :], ps[0:64, 6, P * kv:P * kv + 126], ACT.Copy).then_inc(gelu_c, 1)
            act.wait_ge(gelu_d, 5 * kv + 3)
            act.activation(gelu_t[:, kv, :], gelu_t[:, kv, :], ACT.Tanh, scale=float(np.sqrt(2 / np.pi))).then_inc(gelu_c, 1)

        def cmp_store():
            act.wait_ge(cmp_zero, 3)
            act.wait_ge(cmp2_mm, 2)
            for half in range(2):
                act.activation(kc_hi[64 * half:64 * half + 64, :, 0:N_CMP],
                               ps[0:64, 6, 256:382].rearrange("p (g n) -> p g n", g=2), ACT.Copy).then_inc(cmp_hi, 1)
            act.activation(vc_st[0:N_CMP, :, 0:64], ps[0:N_CMP, 6, 384:512].rearrange("p (g d) -> p g d", g=2),
                           ACT.Copy).then_inc(cmp_hi, 1)

        def pooled_hi_part(g):
            act.wait_ge(pooled, 2 * g + 2)
            if g:
                act.wait_ge(mix_mm, 2 * g)
            act.activation(pp_hi[:, :], ps_ab[(g + 1) % 2][:, PAD:], ACT.Copy).then_inc(pooled_hi, 1)

        def mix_evict(g):
            for ch in range(2):
                n = 2 * g + ch
                act.wait_ge(mix_mm, n + 1)
                if n >= 2:
                    act.wait_ge(mix_st[n % 2], 16 * (n // 2))
                act.activation(pm[:, n % 2, :], ps[:, 4 + n % 2, :], ACT.Copy, scale=pool_sc[:, g:g + 1]) \
                    .then_inc(mix_out, 1)

        for a in range(N_FM):
            for ch in range(2):
                fm_evict(a, ch)
            if a in FM_ROPE and a:
                for ch in range(2):
                    rope_hi_part(2 * FM_ROPE[a] + ch)
            split_a(a + 2)
            if a == 5:
                act.wait_ge(const_in, 16 * N_SMALL)
                gelu(0)
            if a == 7:
                gelu(1)
            if a == 8:
                cmp_store()
            if a == 8:
                act.wait_ge(wp_in, 16)
                act.activation(wp_hi[:, :, :], wp_raw[:, :, :], ACT.Copy).then_inc(wp_hi_s, 1)
            if a >= 8:
                pooled_hi_part(a - 8)
            if a >= 9:
                mix_evict(a - 9)

        def gate_evict(h):
            act.wait_ge(gate_mm, h + 1)
            if h >= 2:
                act.wait_ge(g_st[h % 2], 16 * (h // 2))
            act.activation(g_out[:, h % 2, :], ps[:, 6 if h == 1 else 7, :], ACT.Tanh, scale=0.5).then_inc(gate_tanh, 1)

        gate_evict(0)
        gate_evict(1)
        mix_evict(3)

        act.wait_ge(cmp_zero, 4)
        for s in range(2):
            act.wait_ge(mix_st[s], 16 * 4)

        def exps(u, s):
            c, n = u // 4, STEPS * u + s
            act.wait_ge(negm_done, n + 1)
            if u >= 2 and s == 0:
                act.wait_ge(tp_mm, BANKS_BEFORE[u - 1])
            if s < 4:
                hh, branch = s % 2, s // 2
                parts = score_parts(c, branch)
                w = parts[0][1]
                src = ps[:, 2 * (n % 2):2 * (n % 2) + len(parts), 0:w]
                dst = (p_sel, p_win)[branch][:, u % 2, hh, 0:w * len(parts)].rearrange("p (a w) -> p a w", w=w)
                act.activation(dst, src, ACT.Exp, bias=negm[:, n % 4, 0:1], scale=HEAD_DIM ** -0.5,
                               accum_out=ssum[:, n % 4, 0:1]).then_inc(exp_done, 1)
            else:
                for hh in range(2):
                    ins = act.activation(p_cmp[:, u % 2, hh, 0:64], ps[:, 2 * (n % 2), 64 * hh:64 * hh + 64],
                                         ACT.Exp, bias=negm[:, n % 4, hh:hh + 1], scale=HEAD_DIM ** -0.5,
                                         accum_out=ssum[:, n % 4, hh:hh + 1])
                ins.then_inc(exp_done, 1)

        def transposed_hi(u, b):
            n = BANKS_BEFORE[u] + b
            act.wait_ge(tp_mm, n + 1)
            if n >= 3:
                act.wait_ge(pv_mm, n - 2)
            w = 256 * min(2, len(key_tiles(u // 4)) - 2 * b)
            act.activation(pt_hi[:, n % 3, 0:w], ps[:, 4 + n % 2, 0:w], ACT.Copy).then_inc(pthi, 1)

        for it in range(UNITS + 1):
            half = HALF_OF.get(it)
            for i in range(SLOTS):
                if it:
                    for b in range(n_banks(it - 1)):
                        if tp_slot(it - 1, b) == i:
                            transposed_hi(it - 1, b)
                if i == SLOTS - 1 and half is not None:
                    gate_evict(half)
                if it < UNITS and i % 2 == 0:
                    exps(it, i // 2)
                if i == 1 and half is not None and half % 2 == 0 and half + 2 < HALVES:
                    split_a(N_FM + half // 2 + 1)
            if it:
                v = it - 1
                act.wait_ge(pv_mm, BANKS_BEFORE[v + 1])
                if v >= 2:
                    act.wait_ge(o_sum, v - 1)
                act.activation(o_tmp[:, v % 2, :], ps[64:128, 6, 0:256], ACT.Copy).then_inc(o_half, 1)

        for i in range(8):
            act.wait_ge(stage_in[i % 2], 16 * (i // 2 + 1))
            act.activation(op_hi[:, i, :], stage[:, i % 2, :], ACT.Copy).then_inc(op_hi_s, 1)
            if i == 3:
                gate_evict(HALVES - 1)

        def merge_w_hi(q, b, free):
            r = R_MERGE + b
            act.wait_ge(raw_in[r % 2], 32 * q + raw_count(r))
            act.wait_ge(*free)
            act.activation(a_hi[:, b, :], raw[:, r % 2, :], ACT.Copy).then_inc(hi_done, 1)

        def out_w_hi(n):
            r, s = R_OUT + n, OUT_SLOT[n]
            act.wait_ge(raw_in[r % 2], raw_count(r))
            if n in (2, 3):
                act.wait_ge(merge_pool, KT)
            if n in (4, 5):
                act.wait_ge(merge_mm, 2 * KT)
            if n >= 6:
                act.wait_ge(y_mm, TT)
            act.activation(b_hi[s][:, :], raw[:, r % 2, :], ACT.Copy).then_inc(hi_done, 1)

        merge_w_hi(0, 0, (gate_mm, HALVES - 2))
        merge_w_hi(0, 1, (gate_mm, HALVES))
        with act.Fori(0, KT // 2 - 1) as q:
            for b in range(2):
                act.wait_ge(merge_sum, 4 * q + (2 * b + 2))
                merge_w_hi(q + 1, b, (merge_mm, 4 * q + (2 * b + 2)))
                act.activation(act_hi[:, bass.ds(2 * q + b, 1), :].rearrange("p k n -> p (k n)"), m_a[:, b, :],
                               ACT.Copy, scale=0.5).then_inc(merge_hi, 1)
        for b in range(2):
            m = KT - 2 + b
            out_w_hi(b)
            act.wait_ge(merge_sum, 2 * m + 2)
            act.activation(act_hi[:, m, :], m_a[:, b, :], ACT.Copy, scale=0.5).then_inc(merge_hi, 1)

        def h2_evict(half):
            for k in range(KT):
                m = KT * half + k
                act.wait_ge(x1t_mm, m + 1)
                if m >= 2:
                    act.wait_ge(h2_lo, m - 1)
                act.activation(h2_tmp[:, m % 2, :], ps[:, 4 * half + m % 4, :], ACT.Identity, scale=scale2[:, k:k + 1],
                               bias=shift2[:, k:k + 1]).then_inc(h2_made, 1)

        def y_half(half):
            for t in range(TT):
                n = TT * half + t
                act.wait_ge(y_mm, n + 1)
                act.activation(y[:, t, half * CH:(half + 1) * CH], ps[:, 4 + n % 4, :], ACT.Copy).then_inc(y_out, 1)
                if half:
                    act.wait_ge(y_out, n + 1)
                    if t:
                        act.wait_ge(x1_ms, t)
                    act.activation(junk2[:, :], y[:, t, :], ACT.Square, accum_out=stat[:, t:t + 1]).then_inc(y_ms, 1)
                    act.wait_ge(x1_made, t + 1)
                    act.wait_ge(y_ms, t + 1)
                    act.activation(junk2[:, :], x1[:, t % 2, :], ACT.Square, accum_out=stat[:, 8 + t:9 + t]) \
                        .then_inc(x1_ms, 1)
                    if t == 5:
                        h2_evict(0)
                        mlp_split(0, 0, first=True)
                        mlp_split(0, 1, first=True)

        def mlp_split(j, n, first=False):
            s = (R_MLP + n) % 2
            act.wait_ge(raw_in[s], 64 * j + raw_count(R_MLP + n))
            if n < 4:
                if first and n < 2:
                    act.wait_ge(merge_mm, 2 * KT - 2 + 2 * n)
                else:
                    act.wait_ge(fc1_mm, 8 * j + (-1, 0, 3, 4)[n])
                act.activation(a_hi[:, (A_MLP + n) % 2, :], raw[:, s, :], ACT.Copy).then_inc(hi_done, 1)
            else:
                if first:
                    act.wait_ge(y_mm, 2 * TT)
                else:
                    act.wait_ge(fc2_mm, 2 * TT * j)
                act.activation(b_hi[n - 4][:, :], raw[:, s, :], ACT.Copy).then_inc(hi_done, 1)

        for n in range(2, 6):
            out_w_hi(n)
        y_half(0)
        out_w_hi(6)
        out_w_hi(7)
        y_half(1)

        def mlp(j, first=False):
            if not first:
                mlp_split(j, 0)
                mlp_split(j, 1)
            for n in range(8):
                m, ch = 2 * (n // 4) + n % 2, (n // 2) % 2
                act.wait_ge(fc1_mm, 8 * j + (n + 1))
                if not (first and n < 2):
                    act.wait_ge(hid_lo_s, 8 * j + (n - 1))
                elif n == 1:
                    act.wait_ge(h2_lo, 2 * KT)
                act.activation(relu[:, n % 2, :], ps[:, n % 4, :], ACT.Relu).then_inc(relu_done, 1)
                for x in MLP_SPLITS[n]:
                    mlp_split(j, x, first)
                act.wait_ge(sq_done, 8 * j + (n + 1))
                act.activation(hid_hi[:, m, ch * CH:(ch + 1) * CH], relu[:, n % 2, :], ACT.Copy).then_inc(hid_hi_s, 1)

        h2_evict(1)
        mlp(0, first=True)
        with act.Fori(1, D_FF // CH) as j:
            mlp(j)
        for t in range(TT):
            act.wait_ge(y2_added, 2 * TT * (D_FF // CH - 1) + 2 * t + 2)
            if t:
                act.wait_ge(f_ms, t)
            act.activation(junk3[:, :], y[:, t, :], ACT.Square, accum_out=stat[:, 16 + t:17 + t]).then_inc(f_ms, 1)

    @block.vector
    def _(dve):
        def split_lo(r, dst, hi, src=None):
            dve.wait_ge(hi_done, r + 1)
            dve.tensor_tensor(dst, raw[:, r % 2, :] if src is None else src, full(hi), ALU.subtract).then_inc(lo_done, 1)

        def split_a(a):
            split_lo(R_FM + a, a_lo[:, a % 2, :], a_hi[:, a % 2, :])

        dve.wait_ge(silu_t, 1)
        dve.tensor_scalar(silu_c, silu_c, 0.5, 0.5, ALU.mult, ALU.add).then_inc(silu_done, 1)
        dve.wait_ge(silu_done, 1)
        dve.tensor_tensor(silu_c, silu_c, c_col, ALU.mult).then_inc(silu_done, 1)
        dve.wait_ge(silu_done, 2)
        dve.wait_ge(acc_bias, 16)
        def normalise_x(ch):
            dve.wait_ge(x_rstd, ch + 1)
            for t in range(4 * ch, 4 * ch + 4):
                dve.tensor_scalar(xt[:, t, :], xt[:, t, :], rstd[:, t:t + 1], None, ALU.mult).then_inc(x_norm, 1)

        for n in range(16):
            dve.wait_ge(ada_in[n % 4], 16 * (n // 4 + 1))
            if n % KT:
                dve.wait_ge(ada_added, n)
            k, part = n % KT, 1 - n // KT
            sl = slice(part * 1024, (part + 1) * 1024)
            dve.scalar_tensor_tensor(out=ada_acc[:, sl], in0=ada[:, n % 4, :], scalar=silu_c[:, k:k + 1],
                                     in1=ada_acc[:, sl], op0=ALU.mult, op1=ALU.add).then_inc(ada_added, 1)
            if n == 13:
                dve.wait_ge(mod_mm, 1)
                dve.wait_ge(g_pre_in, 16)
                dve.scalar_tensor_tensor(out=scale, in0=ps[:, 7, 8:16], scalar=1.0, in1=g_pre, op0=ALU.add,
                                         op1=ALU.mult).then_inc(mod_done, 1)
                normalise_x(0)
        dve.wait_ge(mod_mm, 2)
        dve.tensor_copy(shift, ps[:, 7, 0:8]).then_inc(mod_done, 1)
        normalise_x(1)
        for r, (k0, k1) in enumerate(((0, 3), (3, 6), (6, 8))):
            split_lo(r, wv_lo[:, k0:k1, :], wv_hi[:, k0:k1, :],
                     raw[:, r % 2, 0:(k1 - k0) * WV_COLS].rearrange("p (k n) -> p k n", n=WV_COLS))

        def split_h(src, n, made, hi_s, lo_s):
            k, sl = n % KT, slice((n // KT) * CH, (n // KT + 1) * CH)
            dve.wait_ge(made, n + 1)
            dve.tensor_copy(act_hi[:, k, sl], src[:, n % 2, :]).then_inc(hi_s, 1)
            dve.wait_ge(hi_s, n + 1)
            dve.tensor_tensor(act_lo[:, k, sl], src[:, n % 2, :], full(act_hi[:, k, sl]), ALU.subtract).then_inc(lo_s, 1)

        def v_split(t):
            dve.wait_ge(v_hi, 2 * t + 2)
            dve.tensor_tensor(v_st[:, t, :, 64:128], ps[:, 4 + t % 4, 0:256].rearrange("p (f d) -> p f d", d=64),
                              full(v_st[:, t, :, 0:64]), ALU.subtract).then_inc(v_lo, 1)

        for n in range(2 * KT):
            split_h(h_tmp, n, h_made, h_hi, h_lo)
            if n >= 12:
                v_split(n - 12)
        split_a(0)
        split_a(1)
        for t in range(4, TT):
            v_split(t)
        dve.wait_ge(v_hi, 2 * TT)
        dve.tensor_scalar(gates[:, :, :], gates[:, :, :], 0.5, 0.5, ALU.mult, ALU.add).then_inc(gates_done, 1)

        def rope_cos_part(a, ch):
            i, g = 2 * FM_ROPE[a] + ch, 2 * a + ch
            dve.wait_ge(fm_act, g + 1)
            if i == 0:
                dve.wait_ge(cos_in, 32)
            if i in (2, 3):
                dve.wait_ge(rope_sum, i - 1)
            if i >= 4:
                dve.wait_ge(rope_hi, i - 3)
                dve.wait_ge(rope_lo, i - 3)
            dve.tensor_tensor(r_cos[:, i % 2, :], ps[:, g % 4, :], cos[:, ch * CH:(ch + 1) * CH], ALU.mult) \
                .then_inc(rope_cos, 1)

        def rope_lo_part(i):
            dve.wait_ge(rope_hi, i - 1)
            dve.tensor_tensor(r_lo[:, i % 2, :], r_cos[:, i % 2, :], full(r_hi[:, i % 2, :]), ALU.subtract) \
                .then_inc(rope_lo, 1)

        def make_blocks(kv):
            dve.wait_ge(bkx_in, 64 * (kv + 1))
            if kv:
                dve.wait_ge(cmp_mm, 1)
            for g in range(2):
                for h in range(2):
                    src = bkx[:, g, 16 * h:16 * h + 16 * N_CMP].rearrange("p (n l two) -> p l n two", l=8, two=2)[:, :, :, 0]
                    pe_b = pe_col[:, kv, 8 * h:8 * h + 8].unsqueeze(2).to_broadcast([P, 8, N_CMP])
                    ins = dve.tensor_tensor(bk[:, 8 * h:8 * h + 8, g, :], src, pe_b, ALU.add)
            ins.then_inc(bk_made, 1)

        def gelu(kv):
            x, t = gelu_x[:, kv, :], gelu_t[:, kv, :]
            n = 5 * kv
            dve.wait_ge(gelu_c, 2 * kv + 1)
            dve.tensor_tensor(t, x, x, ALU.mult).then_inc(gelu_d, 1)
            dve.wait_ge(gelu_d, n + 1)
            dve.tensor_scalar(t, t, 0.044715, 1.0, ALU.mult, ALU.add).then_inc(gelu_d, 1)
            dve.wait_ge(gelu_d, n + 2)
            dve.tensor_tensor(t, t, x, ALU.mult).then_inc(gelu_d, 1)
            dve.wait_ge(gelu_c, 2 * kv + 2)
            dve.scalar_tensor_tensor(out=t, in0=t, scalar=1.0, in1=x, op0=ALU.add, op1=ALU.mult).then_inc(gelu_d, 1)
            dve.wait_ge(gelu_d, n + 4)
            dve.tensor_scalar(t, t, 0.5, None, ALU.mult).then_inc(gelu_d, 1)

        def cmp_store():
            dve.wait_ge(cmp_hi, 3)
            for half in range(2):
                dve.tensor_tensor(kc_lo[64 * half:64 * half + 64, :, 0:N_CMP],
                                  ps[0:64, 6, 256:382].rearrange("p (g n) -> p g n", g=2),
                                  full(kc_hi[0:64, :, 0:N_CMP]), ALU.subtract).then_inc(cmp_lo, 1)
            dve.tensor_tensor(vc_st[0:N_CMP, :, 64:128], ps[0:N_CMP, 6, 384:512].rearrange("p (g d) -> p g d", g=2),
                              full(vc_st[0:N_CMP, :, 0:64]), ALU.subtract).then_inc(cmp_lo, 1)

        def pooled_part(g):
            w = POOL_SIZES[g]
            s, p = ps_ab[g % 2], ps_ab[(g + 1) % 2]
            dve.wait_ge(pool_add, sum(range(1, g + 2)))
            dve.tensor_tensor(s[:, PAD:PAD + w], s[:, PAD:PAD + w], inv_cnt[:, g, 0:w], ALU.mult).then_inc(pooled_w, 1)
            dve.scalar_tensor_tensor(out=p[:, PAD + w:], in0=s[:, PAD + w:], scalar=1.0 / w, in1=pu[:, PAD + w:],
                                     op0=ALU.mult, op1=ALU.subtract).then_inc(pooled, 1)
            dve.wait_ge(pooled_w, g + 1)
            dve.tensor_tensor(p[:, PAD:PAD + w], s[:, PAD:PAD + w], pu[:, PAD:PAD + w], ALU.subtract).then_inc(pooled, 1)
            dve.wait_ge(pooled_hi, g + 1)
            dve.tensor_tensor(pp_lo[:, :], p[:, PAD:], full(pp_hi[:, :]), ALU.subtract).then_inc(pooled_lo, 1)

        def ada2_add(n):
            k, part = n // 4, n % 4
            if n == 0:
                dve.wait_ge(acc2_bias, 16)
            dve.wait_ge(ada2_in[part], 16 * (k + 1))
            if k:
                dve.wait_ge(ada2_added, n - 3)
            dve.scalar_tensor_tensor(out=acc2[:, part, :], in0=ada2[:, part, :], scalar=silu_c[:, k:k + 1],
                                     in1=acc2[:, part, :], op0=ALU.mult, op1=ALU.add).then_inc(ada2_added, 1)

        def gt_rows(f):
            dve.wait_ge(gp_row_in, 32)
            for half in range(2):
                sl = slice(half * CH, (half + 1) * CH)
                dve.wait_ge(gt_mm, 2 * f + half + 1)
                dve.tensor_tensor(ada2[0:1, f, sl], ps[0:1, 4 + half, :], ada2[0:1, f, sl], ALU.mult).then_inc(gt_row, 1)

        def mod2_columns():
            dve.wait_ge(mod2_mm, 1)
            dve.tensor_copy(shift2, ps[:, 7, 0:8]).then_inc(mod2_done, 1)
            dve.scalar_tensor_tensor(out=scale2, in0=ps[:, 7, 8:16], scalar=1.0, in1=g_mlp, op0=ALU.add,
                                     op1=ALU.mult).then_inc(mod2_done, 1)

        for a in range(N_FM):
            if a in FM_ROPE:
                for ch in range(2):
                    rope_cos_part(a, ch)
                if a == 7:
                    gt_rows(0)
                    mod2_columns()
                    gt_rows(1)
                if a:
                    for ch in range(2):
                        rope_lo_part(2 * FM_ROPE[a] + ch)
            split_a(a + 2)
            for n in range(4 * KT):
                if ADD_AT[n] == a:
                    ada2_add(n)
            if a == 3:
                dve.wait_ge(const_in, 16 * N_SMALL)
                make_blocks(0)
            if a == 5:
                gelu(0)
                make_blocks(1)
            if a == 7:
                gelu(1)
            if a == 8:
                cmp_store()
                dve.wait_ge(wp_hi_s, 1)
                dve.tensor_tensor(wp_lo[:, :, :], wp_raw[:, :, :], full(wp_hi[:, :, :]), ALU.subtract).then_inc(wp_lo_s, 1)
            if a >= 8:
                pooled_part(a - 8)

        def transposed_lo(u, b):
            n = BANKS_BEFORE[u] + b
            dve.wait_ge(pthi, n + 1)
            w = 256 * min(2, len(key_tiles(u // 4)) - 2 * b)
            dve.tensor_tensor(pt_lo[:, n % 3, 0:w], ps[:, 4 + n % 2, 0:w], full(pt_hi[:, n % 3, 0:w]),
                              ALU.subtract).then_inc(ptlo, 1)

        def neg_max(u, s):
            c, n = u // 4, STEPS * u + s
            dve.wait_ge(score_mm, n + 1)
            k = 2 if s == 4 else 1
            if s < 4:
                parts = score_parts(c, s // 2)
                src = ps[:, 2 * (n % 2):2 * (n % 2) + len(parts), 0:parts[0][1]]
                dve.tensor_reduce(smax[:, n % 4, 0:1], src, AX.XY, ALU.max).then_inc(max_done, 1)
            else:
                src = ps[:, 2 * (n % 2), 0:P].rearrange("p (h n) -> p h n", h=2)
                dve.tensor_reduce(smax[:, n % 4, 0:2], src, AX.X, ALU.max).then_inc(max_done, 1)
            dve.wait_ge(max_done, n + 1)
            dve.tensor_scalar(negm[:, n % 4, 0:k], smax[:, n % 4, 0:k], NEG / 10, -HEAD_DIM ** -0.5, ALU.max,
                              ALU.mult).then_inc(negm_done, 1)

        def normalise(u, s):
            c, n = u // 4, STEPS * u + s
            heads = (0, 1) if s == 4 else (s % 2,)
            k = len(heads)
            dve.wait_ge(exp_done, n + 1)
            dve.tensor_scalar(ssum[:, n % 4, 0:k], ssum[:, n % 4, 0:k], 1e-30, None, ALU.max).then_inc(guard_done, 1)
            dve.wait_ge(guard_done, n + 1)
            dve.reciprocal(srec[:, n % 4, 0:k], ssum[:, n % 4, 0:k]).then_inc(rec_done, 1)
            dve.wait_ge(rec_done, n + 1)
            for x, hh in enumerate(heads):
                branch = s // 2
                head = 2 * (u % 4) + hh
                buf = (p_sel, p_win, p_cmp)[branch]
                w = 64 if s == 4 else sum(q[1] for q in score_parts(c, branch))
                gate = gates[:, c, 3 * head + (1, 2, 0)[branch]:3 * head + (1, 2, 0)[branch] + 1]
                ins = dve.tensor_scalar(buf[:, u % 2, hh, 0:w], buf[:, u % 2, hh, 0:w], srec[:, n % 4, x:x + 1], gate,
                                        ALU.mult, ALU.mult)
            ins.then_inc(norm_done, 1)

        dve.wait_ge(gates_done, 1)
        for it in range(UNITS + 1):
            half = HALF_OF.get(it)
            for i in range(SLOTS):
                if it < UNITS and i % 2 == 0:
                    neg_max(it, i // 2)
                if it:
                    for b in range(n_banks(it - 1)):
                        if tp_slot(it - 1, b) == i:
                            transposed_lo(it - 1, b)
                n = STEPS * it + i // 2 - 1
                if i % 2 == 0 and 0 <= n < STEPS * UNITS:
                    normalise(n // STEPS, n % STEPS)
                if i == 1 and half is not None and half % 2 == 0 and half + 2 < HALVES:
                    split_a(N_FM + half // 2 + 1)
            if it:
                v = it - 1
                dve.wait_ge(o_half, v + 1)
                if v >= 2:
                    dve.wait_ge(o_st[v % 2], 16 * (v // 2))
                dve.tensor_tensor(o_out[:, v % 2, :], ps[0:64, 6, 0:256], o_tmp[:, v % 2, :],
                                  ALU.add).then_inc(o_sum, 1)

        for i in range(8):
            dve.wait_ge(op_hi_s, i + 1)
            dve.tensor_tensor(op_lo[:, i, :], stage[:, i % 2, :], full(op_hi[:, i, :]), ALU.subtract).then_inc(op_lo_s, 1)
        def out_split(n):
            s = OUT_SLOT[n]
            split_lo(R_OUT + n, b_lo[s][:, :], b_hi[s][:, :])

        def merge_split(m):
            q, b = m
            s = (R_MERGE + b) % 2
            dve.wait_ge(hi_done, 2 * q + (R_MERGE + b + 1))
            dve.tensor_tensor(a_lo[:, b, :], raw[:, s, :], full(a_hi[:, b, :]), ALU.subtract).then_inc(lo_done, 1)

        def merged_lo(q, b):
            tile = bass.ds(2 * q + b, 1)
            dve.wait_ge(merge_hi, 2 * q + (b + 1))
            dve.scalar_tensor_tensor(out=act_lo[:, tile, :].rearrange("p k n -> p (k n)"), in0=m_a[:, b, :], scalar=0.5,
                                     in1=full(act_hi[:, tile, :]).rearrange("p k n -> p (k n)"), op0=ALU.mult,
                                     op1=ALU.subtract).then_inc(merge_lo, 1)

        def merge(q, first=False, last=False):
            for b in range(2):
                if not (last and b == 1):
                    merge_split((q, 1) if b == 0 else (q + 1, 0))
                else:
                    out_split(0)
                if not first:
                    dve.wait_ge(merge_lo, 2 * q + (b - 1))
                for ch in range(2):
                    g, sl = 2 * b + ch, slice(ch * CH, (ch + 1) * CH)
                    dve.wait_ge(merge_mm, 4 * q + (g + 1))
                    dve.wait_ge(mg_in[ch], 32 * q + 16 * (b + 1))
                    if not (first and b == 0):
                        dve.wait_ge(merge_sum, 4 * q + (g - 1))
                    for h, dst in ((0, m_a[:, b, sl]), (1, m_b[:, ch, :])):
                        ins = dve.scalar_tensor_tensor(out=dst, in0=mg[:, ch, h, :], scalar=1.0,
                                                       in1=ps[:, 2 * g + (1 - h), :], op0=ALU.add, op1=ALU.mult)
                    ins.then_inc(merge_ab, 1)
                if b:
                    merged_lo(q, 0)
                elif not first:
                    merged_lo(q - 1, 1)

        merge_split((0, 0))
        merge(0, first=True)
        with dve.Fori(1, KT // 2 - 1) as q:
            merge(q)
        merge(KT // 2 - 1, last=True)
        out_split(1)
        merged_lo(KT // 2 - 1, 1)
        for n in range(2, 8):
            out_split(n)

        def mlp_split(j, n):
            s = (R_MLP + n) % 2
            dve.wait_ge(hi_done, 8 * j + (R_MLP + n + 1))
            dst, hi = (a_lo[:, (A_MLP + n) % 2, :], a_hi[:, (A_MLP + n) % 2, :]) if n % 8 < 4 else \
                (b_lo[n - 4][:, :], b_hi[n - 4][:, :])
            dve.tensor_tensor(dst, raw[:, s, :], full(hi), ALU.subtract).then_inc(lo_done, 1)

        dve.wait_ge(gt_in, 32)
        for t in range(TT):
            yt = y[:, t, :]
            dve.wait_ge(y_rstd, t + 1)
            dve.scalar_tensor_tensor(out=yt, in0=yt, scalar=stat[:, t:t + 1], in1=gt1[:, :], op0=ALU.mult,
                                     op1=ALU.mult).then_inc(y_gated, 1)
            dve.wait_ge(y_gated, t + 1)
            dve.wait_ge(xi_in[t % 2], 16 * (t // 2 + 1))
            if t >= 2:
                dve.wait_ge(x1_st[t % 2], 16 * (t // 2))
                dve.wait_ge(x1_ms, t - 1)
            dve.tensor_tensor(x1[:, t % 2, :], yt, x_in[:, t % 2, :], ALU.add).then_inc(x1_made, 1)
            dve.wait_ge(x1_rstd, t + 1)
            dve.tensor_scalar(yt, x1[:, t % 2, :], stat[:, 8 + t:9 + t], None, ALU.mult).then_inc(x1n_made, 1)
            if t == 5:
                for m in range(KT):
                    split_h(h2_tmp, m, h2_made, h2_hi, h2_lo)
                mlp_split(0, 0)
                mlp_split(0, 1)

        for m in range(KT, 2 * KT):
            split_h(h2_tmp, m, h2_made, h2_hi, h2_lo)

        def final(t):
            yt = y[:, t, :]
            dve.wait_ge(f_rstd, t + 1)
            dve.scalar_tensor_tensor(out=yt, in0=yt, scalar=stat[:, 16 + t:17 + t], in1=gt2[:, :], op0=ALU.mult,
                                     op1=ALU.mult).then_inc(f_gated, 1)
            dve.wait_ge(f_gated, t + 1)
            dve.wait_ge(x1i_in[t % 2], 16 * (t // 2 + 1))
            if t >= 2:
                dve.wait_ge(out_st[t % 2], 16 * (t // 2))
            dve.tensor_tensor(fin[:, t % 2, :], yt, x1_in[:, t % 2, :], ALU.add).then_inc(f_made, 1)

        def mlp(j, first=False, last=False):
            for n in range(8):
                m, ch = 2 * (n // 4) + n % 2, (n // 2) % 2
                sl = slice(ch * CH, (ch + 1) * CH)
                if first and n == 4:
                    for s in range(2):
                        dve.wait_ge(x1_st[s], 16 * TT // 2)
                for x in MLP_SPLITS[n]:
                    mlp_split(j, x)
                dve.wait_ge(hid_hi_s, 8 * j + (n + 1))
                dve.tensor_tensor(hid_lo[:, m, sl], relu[:, n % 2, :], full(hid_hi[:, m, sl]), ALU.subtract) \
                    .then_inc(hid_lo_s, 1)
            if not last:
                mlp_split(j, 8)
                mlp_split(j, 9)
            for n in range(2 * TT):
                t, half = n // 2, n % 2
                yt = y[:, t, half * CH:(half + 1) * CH]
                dve.wait_ge(fc2_mm, 2 * TT * j + (n + 1))
                if first:
                    dve.tensor_copy(yt, ps[:, 4 + n % 4, :]).then_inc(y2_added, 1)
                else:
                    dve.wait_ge(y2_added, 2 * TT * j + (n - 2 * TT + 1))
                    dve.tensor_tensor(yt, ps[:, 4 + n % 4, :], yt, ALU.add).then_inc(y2_added, 1)
                if last and half and t:
                    final(t - 1)

        mlp(0, first=True)
        with dve.Fori(1, D_FF // CH - 1) as j:
            mlp(j)
        mlp(D_FF // CH - 1, last=True)
        final(TT - 1)

    @block.tensor
    def _(pe):
        def three(dst, wh, wl, mh, ml, start, stop):
            pe.matmul(dst, wh, mh, start=start, stop=False)
            pe.matmul(dst, wh, ml, start=False, stop=False)
            return pe.matmul(dst, wl, mh, start=False, stop=stop)

        def mod_columns(part):
            for n in range(8 * part, 8 * part + 8):
                ins = pe.matmul(ps[:, 7, n:n + 1], ada_acc[:, n * P:(n + 1) * P], ones[:, 0:1], start=True, stop=True)
            ins.then_inc(mod_mm, 1)

        def x_transposes(n):
            ch, k = n // KT, n % KT
            if n % KT == 0:
                pe.wait_ge(x_norm, 4 * ch + 4)
            if n >= 4:
                pe.wait_ge(h_made, n - 3)
            for t in range(4):
                ins = pe.transpose(ps[:, n % 4, t * P:(t + 1) * P], xt[:, 4 * ch + t, k * P:(k + 1) * P], ident[:, :])
            ins.then_inc(xt_mm, 1)

        def values_and_gates(ch, k):
            pe.wait_ge(h_lo, KT * ch + k + 1)
            for t in range(4 * ch, 4 * ch + 4):
                if ch and k == 0:
                    pe.wait_ge(v_lo, t - 3)
                    pe.wait_ge(v_hi, 2 * t - 6)
                tok = slice(t * P, (t + 1) * P)
                ins = three(ps[:, 4 + t % 4, 0:WV_COLS], act_hi[:, k, tok], act_lo[:, k, tok], wv_hi[:, k, :],
                            wv_lo[:, k, :], k == 0, k == KT - 1)
                if k == KT - 1:
                    ins.then_inc(v_mm, 1)

        pe.wait_ge(consts_made, CONSTS)
        pe.wait_ge(ada_added, 8)
        mod_columns(1)
        for n in range(4):
            x_transposes(n)
        pe.wait_ge(ada_added, 16)
        pe.wait_ge(mod_done, 1)
        mod_columns(0)
        for n in range(4, 12):
            x_transposes(n)
        pe.wait_ge(lo_done, 3)
        pe.wait_ge(mod_done, 2)
        for k in range(KT):
            values_and_gates(0, k)
            if k < 4:
                x_transposes(12 + k)
        for k in range(KT):
            values_and_gates(1, k)

        def project(a, bank, ch, ks, done=None):
            sl = slice(ch * CH, (ch + 1) * CH)
            for k in ks:
                w = slice(k * P, (k + 1) * P)
                ins = three(ps[:, bank, :], a_hi[:, a % 2, w], a_lo[:, a % 2, w], act_hi[:, k, sl], act_lo[:, k, sl],
                            k == 0, k == KT - 1)
            return ins

        def compress(kv):
            pe.wait_ge(cw_in, 16 * (kv + 1))
            pe.wait_ge(bk_made, kv + 1)
            if kv:
                pe.wait_ge(gelu_c, 1)
            for l in range(16):
                ins = pe.matmul(ps[0:64, 6, P * kv:P * kv + 126], cw1[:, l, :],
                                bk[:, l, :, :].rearrange("p g n -> p (g n)"), start=l == 0, stop=l == 15)
            ins.then_inc(cmp_mm, 1)

        def compress2():
            pe.wait_ge(gelu_d, 10)
            pe.matmul(ps[0:64, 6, 256:382], w2k[:, :], gelu_t[:, 0, :], start=True, stop=True).then_inc(cmp2_mm, 1)
            for g in range(2):
                ins = pe.matmul(ps[0:N_CMP, 6, 384 + 64 * g:448 + 64 * g], gelu_t[:, 1, N_CMP * g:N_CMP * (g + 1)],
                                w2v[:, :], start=True, stop=True)
            ins.then_inc(cmp2_mm, 1)

        def mix(g):
            pe.wait_ge(pooled_lo, g + 1)
            if g == 0:
                pe.wait_ge(wp_lo_s, 1)
            for ch in range(2):
                n, sl = 2 * g + ch, slice(ch * CH, (ch + 1) * CH)
                if n >= 2:
                    pe.wait_ge(mix_out, n - 1)
                three(ps[:, 4 + n % 2, :], wp_hi[:, g, :], wp_lo[:, g, :], pp_hi[:, sl], pp_lo[:, sl], True, True) \
                    .then_inc(mix_mm, 1)

        def second_modulation():
            pe.wait_ge(ada2_added, 4 * KT)
            pe.wait_ge(v_lo, TT)
            pe.wait_ge(v_hi, 2 * TT)
            for f, part in ((0, 0), (1, 3)):
                for half in range(2):
                    if f:
                        pe.wait_ge(gt_row, half + 1)
                    pe.matmul(ps[0:1, 4 + half, :], ones[:, 0:1], acc2[:, part, half * CH:(half + 1) * CH],
                              start=True, stop=True).then_inc(gt_mm, 1)
                if f == 0:
                    for n in range(16):
                        ins = pe.matmul(ps[:, 7, n:n + 1], acc2[:, 1 + n // KT, (n % KT) * P:(n % KT + 1) * P],
                                        ones[:, 0:1], start=True, stop=True)
                    ins.then_inc(mod2_mm, 1)

        def gate_part(h, ks):
            if 0 in ks:
                pe.wait_ge(lo_done, R_FM + N_FM + h // 2 + 1)
                if h >= 2:
                    pe.wait_ge(gate_tanh, h)
            ins = project(N_FM + h // 2, 6 if h == 1 else 7, h % 2, ks)
            if KT - 1 in ks:
                ins.then_inc(gate_mm, 1)

        for a in range(N_FM):
            pe.wait_ge(lo_done, R_FM + a + 1)
            for ch in range(2):
                g = 2 * a + ch
                if g >= 4:
                    pe.wait_ge(fm_act, g - 3)
                    if a - 2 in FM_ROPE:
                        pe.wait_ge(rope_cos, 2 * FM_ROPE[a - 2] + ch + 1)
                ins = project(a, g % 4, ch, range(KT))
                ins.then_inc(fm_mm, 1)
            if a == 4:
                compress(0)
            if a == 6:
                compress(1)
            if a == 7:
                second_modulation()
            if a == 8:
                compress2()
            if a >= 9:
                mix(a - 9)
        pe.wait_ge(mod2_done, 2)
        gate_part(0, range(KT))
        pe.wait_ge(cmp_lo, 3)
        gate_part(1, range(KT))
        mix(3)

        def scores(u, s):
            c, n = u // 4, STEPS * u + s
            g = (u % 4) // 2
            if n >= 2:
                pe.wait_ge(exp_done, n - 1)
            if s == 0 and u % 4 == 0:
                pe.wait_ge(q_in[c % 2], 16 * (c // 2 + 1))
            base = 2 * (n % 2)
            if s < 4:
                branch, q = s // 2, q_st[:, c % 2, 2 * (u % 4) + s % 2, :]
                parts = score_parts(c, branch)
                for x, (k0, w, _) in enumerate(parts):
                    dst = ps[:, base + x, 0:w]
                    last, far = x == len(parts) - 1, branch == 1 and c >= WINDOW // P and x == 0
                    pe.matmul(dst, q, k_hi[:, 2 * branch + g, k0:k0 + w], start=True, stop=False)
                    ins = pe.matmul(dst, q, k_lo[:, 2 * branch + g, k0:k0 + w], start=False, stop=True)
                    if far:
                        ins = pe.matmul(ps[:, base + x, 0:P], ident_b[:, :], mask_far[:, :], start=False, stop=True,
                                        skip_group_check=True)
                    if last:
                        ins = pe.matmul(ps[:, base + x, w - P:w], ident_b[:, :], mask_diag[:, :], start=False, stop=True,
                                        skip_group_check=True)
                ins.then_inc(score_mm, 1)
            else:
                for hh in range(2):
                    dst, q = ps[:, base, 64 * hh:64 * hh + 64], q_st[:, c % 2, 2 * (u % 4) + hh, :]
                    pe.matmul(dst, q, kc_hi[:, g, :], start=True, stop=False)
                    pe.matmul(dst, q, kc_lo[:, g, :], start=False, stop=False)
                    ins = pe.matmul(dst, ident_b[:, :], mask_cmp[:, c, :], start=False, stop=True)
                ins.then_inc(score_mm, 1)

        def transposes(u, b):
            c, n = u // 4, BANKS_BEFORE[u] + b
            if n >= 2:
                pe.wait_ge(ptlo, n - 1)
            elif n == 0:
                pe.wait_ge(mix_out, 8)
            for x, (branch, j) in enumerate(key_tiles(c)[2 * b:2 * b + 2]):
                pe.wait_ge(norm_done, STEPS * u + (2, 4, 5)[branch])
                for hh in range(2):
                    at = ps[:, 4 + n % 2, 256 * x + P * hh:256 * x + P * hh + P]
                    if branch == 2:
                        src = p_cmp[:, u % 2, hh, :]
                    else:
                        k = (j - (max(0, c - WINDOW // P) if branch else 0)) * P
                        src = (p_sel, p_win)[branch][:, u % 2, hh, k:k + P]
                    ins = pe.transpose(at, src, ident[:, :])
            ins.then_inc(tp_mm, 1)

        def value_products(u, b):
            c, n, g = u // 4, BANKS_BEFORE[u] + b, (u % 4) // 2
            pe.wait_ge(ptlo, n + 1)
            if b == 0:
                if u:
                    pe.wait_ge(o_sum, u)
                else:
                    pe.wait_ge(gate_tanh, 2)
            tiles = key_tiles(c)
            for x, (branch, j) in enumerate(tiles[2 * b:2 * b + 2]):
                v = vc_st[:, g, :] if branch == 2 else v_st[:, j, 2 * branch + g, :]
                dst = ps[:, 6, 0:256]
                first, last = b == 0 and x == 0, 2 * b + x == len(tiles) - 1
                pe.matmul(dst, v, pt_hi[:, n % 3, 256 * x:256 * x + 256], start=first, stop=False)
                ins = pe.matmul(dst, v, pt_lo[:, n % 3, 256 * x:256 * x + 256], start=False, stop=last)
            ins.then_inc(pv_mm, 1)

        pe.wait_ge(fm_act, 2 * N_FM)
        pe.wait_ge(rope_out[0], rope_out_count(ROPES - 2))
        pe.wait_ge(rope_out[1], rope_out_count(ROPES - 1))
        pe.wait_ge(cmp_lo, 3)
        for it in range(UNITS + 1):
            for i in range(SLOTS):
                if it < UNITS and i % 2 == 0:
                    scores(it, i // 2)
                if it:
                    for b in range(n_banks(it - 1)):
                        if tp_slot(it - 1, b) == i:
                            transposes(it - 1, b)
                if it in HALF_OF and i < KT:
                    gate_part(HALF_OF[it], (i,))
                if it:
                    for b in range(n_banks(it - 1)):
                        if tp_slot(it - 1, b) + 2 == i:
                            value_products(it - 1, b)
        gate_part(HALVES - 1, range(KT))

        def merge(q, first=False):
            for b in range(2):
                pe.wait_ge(lo_done, 2 * q + (R_MERGE + b + 1))
                for part in range(2):
                    if first and b == 0:
                        pe.wait_ge(op_lo_s, 4 * part + 4)
                    for ch in range(2):
                        g = 2 * b + ch
                        if part == 0 and not first:
                            pe.wait_ge(merge_ab, 4 * q + (g - 3))
                        for k in range(4 * part, 4 * part + 4):
                            w, sl = slice(k * P, (k + 1) * P), slice(ch * CH, (ch + 1) * CH)
                            ins = three(ps[:, 2 * g + part, :], a_hi[:, b, w], a_lo[:, b, w], op_hi[:, k, sl],
                                        op_lo[:, k, sl], k % 4 == 0, k % 4 == 3)
                        if part:
                            ins.then_inc(merge_mm, 1)
                    if part == 0:
                        ins.then_inc(merge_pool, 1)

        pe.wait_ge(gate_tanh, HALVES)
        pe.wait_ge(o_sum, UNITS)
        pe.wait_ge(ptlo, BANKS_BEFORE[UNITS])
        merge(0, first=True)
        with pe.Fori(1, KT // 2) as q:
            merge(q)

        def x1_transposes(half):
            pe.wait_ge(x1n_made, 4 * half + 4)
            for k in range(KT):
                m = KT * half + k
                if k >= 4:
                    pe.wait_ge(h2_made, m - 3)
                for t in range(4):
                    ins = pe.transpose(ps[:, 4 * half + m % 4, t * P:(t + 1) * P], y[:, 4 * half + t, k * P:(k + 1) * P],
                                       ident[:, :])
                ins.then_inc(x1t_mm, 1)

        pe.wait_ge(merge_lo, KT)
        pe.wait_ge(merge_hi, KT)
        for n in range(2 * TT):
            half, t = n // TT, n % TT
            if n >= 4:
                pe.wait_ge(y_out, n - 3)
            tok = slice(t * P, (t + 1) * P)
            for k in range(KT):
                if t == 0:
                    if n == 0 and k % 2 == 0:
                        pe.wait_ge(lo_done, R_OUT + k // 2 + 1)
                    elif k == 0:
                        pe.wait_ge(lo_done, R_OUT + 6)
                    elif half and k == 4:
                        pe.wait_ge(lo_done, R_OUT + 8)
                s, w = OUT_SLOT[4 * half + k // 2], slice((k % 2) * CH, (k % 2 + 1) * CH)
                ins = three(ps[:, 4 + n % 4, :], act_hi[:, k, tok], act_lo[:, k, tok], b_hi[s][:, w],
                            b_lo[s][:, w], k == 0, k == KT - 1)
            ins.then_inc(y_mm, 1)
            if n == TT + 5:
                x1_transposes(0)

        def mlp(j, first=False):
            for n in range(8):
                m, ch = 2 * (n // 4) + n % 2, (n // 2) % 2
                a = (A_MLP + m) % 2
                if ch == 0:
                    pe.wait_ge(lo_done, 8 * j + (R_MLP + m + 1))
                if first and n in (0, 2):
                    pe.wait_ge(h2_lo, KT * (ch + 1))
                if not (first and n < 4):
                    pe.wait_ge(relu_done, 8 * j + (n - 3))
                sl = slice(ch * CH, (ch + 1) * CH)
                for k in range(KT):
                    w = slice(k * P, (k + 1) * P)
                    ins = three(ps[:, n % 4, :], a_hi[:, a, w], a_lo[:, a, w], act_hi[:, k, sl], act_lo[:, k, sl],
                                k == 0, k == KT - 1)
                ins.then_inc(fc1_mm, 1)
                if first and n == 1:
                    x1_transposes(1)
            pe.wait_ge(lo_done, 8 * j + (R_MLP + 8))
            for n in range(2 * TT):
                t, half = n // 2, n % 2
                if n in (0, TT):
                    pe.wait_ge(hid_lo_s, 8 * j + (6, 8)[n // TT])
                if not (first and n < 4):
                    pe.wait_ge(y2_added, 2 * TT * j + (n - 3))
                elif n == 0:
                    pe.wait_ge(y_out, 2 * TT)
                tok, w = slice(t * P, (t + 1) * P), slice(half * CH, (half + 1) * CH)
                for k in range(4):
                    ins = three(ps[:, 4 + n % 4, :], hid_hi[:, k, tok], hid_lo[:, k, tok], b_hi[k][:, w], b_lo[k][:, w],
                                k == 0, k == 3)
                ins.then_inc(fc2_mm, 1)
        mlp(0, first=True)
        with pe.Fori(1, D_FF // CH) as j:
            mlp(j)

    block.__exit__(None, None, None)


_INS = ["x", "c", "w_ada", "b_ada", "g_pre_mix", "g_post_mix", "w_in", "cmp_pe_k", "cmp_w1_k", "cmp_w2_k", "cmp_pe_v",
        "cmp_w1_v", "cmp_w2_v", "w_pool", "pool_scale", "w_br_nsa", "w_br_pool", "w_out", "g_pre_mlp", "g_post_mlp",
        "w_fc1", "w_fc2"]


def shape_constants():
    half = HEAD_DIM // 2
    inv = (10000.0 ** (-np.arange(half, dtype=np.float64) / half)).astype(np.float32)
    ang = (inv[:, None] * np.arange(SEQ, dtype=np.float32)[None, :]).astype(np.float64)
    cos = np.tile(np.cos(ang), (4, 1)).astype(np.float32)
    sin = np.concatenate([-np.sin(ang), np.sin(ang)] * 2).astype(np.float32)
    cnt = np.minimum(np.arange(16)[None, :] + 1, np.array(POOL_SIZES)[:, None])
    inv_cnt = np.broadcast_to((1.0 / cnt).astype(np.float32), (P, 4, 16)).copy()
    return {"cos": cos, "sin": sin, "inv_cnt": inv_cnt}


def kernel(**inputs):
    import concourse.bacc as bacc
    from concourse.bass_utils import run_bass_kernel_spmd

    nc = bacc.Bacc("TRN2", target_bir_lowering=False, num_devices=1)
    arrays = {n: np.ascontiguousarray(inputs[n]) for n in _INS}
    arrays.update(shape_constants())
    aps = {n: nc.dram_tensor("in_" + n, a.shape, mybir.dt.from_np(a.dtype), kind="ExternalInput").ap()
           for n, a in arrays.items()}
    out = nc.dram_tensor("out", (1, SEQ, D_MODEL), mybir.dt.float32, kind="ExternalOutput").ap()
    hybrid_block(nc, aps, out)
    r = run_bass_kernel_spmd(nc, [{"in_" + n: a for n, a in arrays.items()}], core_ids=[0])
    return r.results[0]["out"]
```

```python
import numpy as np
import concourse.bass as bass
from concourse import mybir

D_MODEL, SEQ, D_FF = 1024, 1024, 4096
N_HEADS, HEAD_DIM, KV_WIDTH = 8, 64, 128
CMP_BLOCK, CMP_STRIDE, WINDOW, SEL_BLOCK, SEL_TOPK = 32, 16, 512, 64, 16
POOL_SIZES = (2, 4, 8, 16)
POOL_WIDTH = 512
EPS = 1e-6
P = 128
KT = D_MODEL // P
TT = SEQ // P
CH = 512
FULL_RATE = 256
N_CMP = (SEQ - CMP_BLOCK) // CMP_STRIDE + 1
NEG = -1e30
assert SEQ // SEL_BLOCK <= SEL_TOPK

C_Q, C_KC, C_VC, C_KS, C_VS, C_KW, C_VW, C_G, C_U, C_BR = 0, 512, 640, 768, 896, 1024, 1152, 1280, 1304, 1816
N_GATE = 3 * N_HEADS
WV_COLS = 2 * KV_WIDTH + N_GATE

FM_COLS = [C_KC, C_VC] + [C_Q + P * i for i in range(4)] + [C_KS, C_KW] + [C_U + P * i for i in range(4)] \
    + [C_BR + P * i for i in range(16)]
FM_ROPE = {0: 0, 2: 1, 3: 2, 4: 3, 5: 4, 6: 5, 7: 6}
Q_BLOCKS, K_BLOCKS = (2, 3, 4, 5), (6, 7)
N_FM = 12
N_BR = 16
UNITS = TT * N_HEADS // 2
STEPS = 5
SLOTS = 9
HALVES = 2 * N_BR
HALF_OF = dict(zip(range(UNITS + 4 - HALVES, UNITS + 1), range(2, HALVES - 1)))
assert len(HALF_OF) == HALVES - 3

R_FM, R_MERGE, R_OUT, R_MLP = 0, N_FM + N_BR, N_FM + N_BR + KT, N_FM + N_BR + 2 * KT
A_MLP = N_FM + N_BR + KT


def raw_dmas(r):
    return 2 if R_MERGE <= r < R_OUT else 1


def raw_count(r):
    return 16 * sum(raw_dmas(x) for x in range(r % 2, r + 1, 2))


def key_tiles(c):
    first = max(0, c - WINDOW // P)
    return [(0, j) for j in range(c + 1)] + [(1, j) for j in range(first, c + 1)] + [(2, 0)]


def n_banks(u):
    return (len(key_tiles(u // 4)) + 1) // 2


BANKS_BEFORE = [sum(n_banks(v) for v in range(u)) for u in range(UNITS + 1)]


def tp_slot(u, b):
    return b * 7 // n_banks(u)


def score_parts(c, branch):
    first = max(0, c - WINDOW // P) * P if branch else 0
    width = (c + 1) * P - first
    if width <= CH:
        return [(first, width, 0)]
    return [(first, width // 2, 0), (first + width // 2, width // 2, CH)]


def cmp_width(c):
    return min(64, (c + 1) * P // CMP_STRIDE)


def hybrid_block(nc, A, out):
    f32, f32r, bf16 = mybir.dt.float32, mybir.dt.float32r, mybir.dt.bfloat16
    ALU, ACT, AX = mybir.AluOpType, mybir.ActivationFunctionType, mybir.AxisListType

    def place(name, kb, shape, dt):
        pad = nc.sbuf_tensor(name + "_pad", [P, int(kb * 1024)], mybir.dt.uint8) if kb else None
        if pad:
            pad.__enter__()
        guard = nc.sbuf_tensor(name, shape, dt)
        t = guard.__enter__()
        guard.__exit__(None, None, None)
        if pad:
            pad.__exit__(None, None, None)
        return t

    def sem(name):
        return nc.semaphore(name).__enter__()

    def full(t):
        return t.bitcast(f32)

    ident = place("ident", 0, [P, P], f32)
    ones = place("ones", 0.5, [P, P], f32)
    ident_b = place("ident_b", 1, [P, P], bf16)
    mask_diag = place("mask_diag", 1.25, [P, P], bf16)
    mask_far = place("mask_far", 1.5, [P, P], bf16)
    mask_cmp = place("mask_cmp", 1.75, [P, TT, 64], bf16)
    gates = place("gates", 2.75, [P, TT, N_GATE], f32)
    col = place("col", 3.5, [P, 128], f32)
    c_col, silu_c, g_pre = col[:, 0:8], col[:, 8:16], col[:, 16:24]
    g_mlp, pool_sc, shift, scale = col[:, 24:32], col[:, 32:36], col[:, 40:48], col[:, 48:56]
    msq, half_neg = col[:, 56:64], col[:, 72:76]
    stat = col[:, 80:128]
    smax = place("smax", 4, [P, 4, 2], f32)
    negm = place("negm", 4.125, [P, 4, 2], f32)
    ssum = place("ssum", 4.25, [P, 4, 2], f32)
    srec = place("srec", 4.375, [P, 4, 2], f32)
    inv_cnt = place("inv_cnt", 4.5, [P, 4, 16], f32)
    pe_col = place("pe_col", 4.75, [P, 2, 16], f32)
    w2k = place("w2k", 5, [64, 64], f32)
    w2v = place("w2v", 5.25, [64, 64], f32)
    gelu_x = place("gelu_x", 5.5, [64, 2, 126], f32)
    gelu_t = place("gelu_t", 6.5, [64, 2, 126], f32)
    col2 = place("col2", 7.5, [P, 16], f32)
    shift2, scale2 = col2[:, 0:8], col2[:, 8:16]
    raw = place("raw", 8, [P, 2, 1024], f32)
    a_hi = place("a_hi", 16, [P, 2, 1024], f32r)
    a_lo = place("a_lo", 24, [P, 2, 1024], f32r)
    act_hi = place("act_hi", 32, [P, KT, SEQ], f32r)
    act_lo = place("act_lo", 64, [P, KT, SEQ], f32r)
    k_hi = place("k_hi", 96, [P, 4, SEQ], f32r)
    k_lo = place("k_lo", 112, [P, 4, SEQ], f32r)
    v_st = place("v_st", 128, [P, TT, 4, P], f32r)
    kc_hi = place("kc_hi", 144, [P, 2, 64], f32r)
    kc_lo = place("kc_lo", 144.5, [P, 2, 64], f32r)
    vc_st = place("vc_st", 145, [P, 2, P], f32r)
    xt = place("xt", 96, [P, TT, D_MODEL], f32)
    ada_acc = place("ada_acc", 128, [P, 2048], f32)
    h_tmp = place("h_tmp", 146, [P, 2, CH], f32)
    ada = place("ada", 154, [P, 8, 1024], f32)
    acc2 = place("acc2", 96, [P, 4, 1024], f32)
    ada2 = place("ada2", 112, [P, 4, 1024], f32)
    junk = place("junk", 150, [P, 1024], f32)
    kc_f = place("kc_f", 146, [P, SEQ], f32)
    vc_f = place("vc_f", 150, [P, SEQ], f32)
    cw1 = place("cw1", 154, [P, 16, 64], f32)
    cos = place("cos", 158, [P, SEQ], f32)
    sin = place("sin", 162, [P, SEQ], f32)
    r_swap = place("r_swap", 166, [P, 2, CH], f32)
    r_cos = place("r_cos", 170, [P, 2, CH], f32)
    r_sin = place("r_sin", 174, [P, 2, CH], f32)
    r_hi = place("r_hi", 178, [P, 2, CH], f32r)
    r_lo = place("r_lo", 182, [P, 2, CH], f32r)
    wv_hi = place("wv_hi", 186, [P, KT, WV_COLS], f32r)
    wv_lo = place("wv_lo", 194.75, [P, KT, WV_COLS], f32r)
    wv_raw = place("wv_raw", 194.75, [P, KT, WV_COLS], f32)
    bkx = place("bkx", 186, [P, 2, SEQ], f32)
    bk = place("bk", 194, [P, 16, 2, N_CMP], f32)
    PAD = 16
    pu = place("pu", 186, [P, PAD + SEQ], f32)
    ps_ab = [place("ps_a", 190.25, [P, PAD + SEQ], f32), place("ps_b", 194.5, [P, PAD + SEQ], f32)]
    pp_hi = place("pp_hi", 158, [P, SEQ], f32r)
    pp_lo = place("pp_lo", 162, [P, SEQ], f32r)
    wp_raw = place("wp_raw", 154, [P, 4, P], f32)
    wp_hi = place("wp_hi", 156, [P, 4, P], f32r)
    wp_lo = place("wp_lo", 203.5, [P, 4, P], f32r)
    pm = place("pm", 182, [P, 2, CH], f32)
    q_st = place("q_st", 146, [P, 2, N_HEADS, P], f32r)
    p_sel = place("p_sel", 154, [P, 2, 2, SEQ], f32)
    p_win = place("p_win", 170, [P, 2, 2, 640], f32)
    p_cmp = place("p_cmp", 180, [P, 2, 2, P], f32)
    pt_hi = place("pt_hi", 182, [P, 3, CH], f32r)
    pt_lo = place("pt_lo", 188, [P, 3, CH], f32r)
    o_tmp = place("o_tmp", 194, [64, 2, 256], f32)
    o_out = place("o_out", 196, [64, 2, 256], f32)
    g_out = place("g_out", 198.75, [P, 2, CH], f32)
    op_hi = [place("op_hi_pool", 96, [P, 4, SEQ], f32r), place("op_hi_att", 128, [P, 4, SEQ], f32r)]
    op_lo = [place("op_lo_pool", 112, [P, 4, SEQ], f32r), place("op_lo_att", 144, [P, 4, SEQ], f32r)]
    op_raw = [place("op_raw_pool", 112, [P, 4, SEQ], f32), place("op_raw_att", 144, [P, 4, SEQ], f32)]
    mg = place("mg", 184, [P, 2, 2, CH], f32)
    m_a = place("m_a", 192, [P, 2, SEQ], f32)
    m_b = place("m_b", 200, [P, 2, CH], f32)
    b_at = (168, 176, 96, 104, 112, 120)
    b_hi = [place(f"b_hi{i}", kb, [P, 1024], f32r) for i, kb in enumerate(b_at)]
    b_lo = [place(f"b_lo{i}", kb + 4, [P, 1024], f32r) for i, kb in enumerate(b_at)]
    y = place("y", 128, [P, TT, D_MODEL], f32)
    gt1 = place("gt1", 160, [P, 1024], f32)
    gt2 = place("gt2", 164, [P, 1024], f32)
    x_in = place("x_in", 184, [P, 2, 1024], f32)
    x1 = place("x1", 192, [P, 2, 1024], f32)
    junk2 = place("junk2", 200, [P, 1024], bf16)
    h2_tmp = place("h2_tmp", 202, [P, 2, CH], f32)
    hid_hi = place("hid_hi", 112, [P, 4, SEQ], f32r)
    hid_lo = place("hid_lo", 184, [P, 4, SEQ], f32r)
    relu = place("relu", 200, [P, 2, CH], f32)
    x1_in = place("x1_in", 32, [P, 2, 1024], f32)
    fin = place("fin", 40, [P, 2, 1024], f32)
    junk3 = place("junk3", 48, [P, 1024], bf16)

    ps = nc.psum_tensor("ps", [P, 8, CH], f32).__enter__()

    q_dram = nc.dram_tensor("q_dram", (TT, P, N_HEADS, P), f32, kind="Internal").ap()
    pool_dram = nc.dram_tensor("pool_dram", (POOL_WIDTH, SEQ), f32, kind="Internal").ap()
    o_dram = nc.dram_tensor("o_dram", (N_HEADS * HEAD_DIM, SEQ), f32, kind="Internal").ap()
    g_dram = nc.dram_tensor("g_dram", (2, KT, 2, P, CH), f32, kind="Internal").ap()
    gt_dram = nc.dram_tensor("gt_dram", (2, D_MODEL), f32, kind="Internal").ap()
    x1_dram = nc.dram_tensor("x1_dram", (SEQ, D_MODEL), f32, kind="Internal").ap()

    x_v = A["x"][0].rearrange("(t p) d -> p t d", p=P)
    x1_v = x1_dram.rearrange("(t p) d -> p t d", p=P)
    out_v = out[0].rearrange("(t p) d -> p t d", p=P)
    w_ada, b_ada = A["w_ada"][0], A["b_ada"]
    w_in_v = A["w_in"][0].rearrange("(k p) n -> p k n", p=P)
    w_brn_v = A["w_br_nsa"][0].rearrange("(k p) n -> p k n", p=P)
    w_brp_v = A["w_br_pool"][0].rearrange("(k p) n -> p k n", p=P)
    w_out_v = A["w_out"][0].rearrange("(k p) n -> p k n", p=P)
    w_fc1_v = A["w_fc1"][0].rearrange("(k p) n -> p k n", p=P)
    w_fc2_v = A["w_fc2"][0].rearrange("(k p) n -> p k n", p=P)

    c_in, g_pre_in = sem("c_in"), sem("g_pre_in")
    const_in, cos_in, wp_in = sem("const_in"), sem("cos_in"), sem("wp_in")
    consts_made, acc_zero, acc_bias = sem("consts_made"), sem("acc_zero"), sem("acc_bias")
    silu_steps = sem("silu_steps")
    ada_in = [sem(f"ada_in{i}") for i in range(8)]
    wv_in, wv_hi_s, wv_lo_s = sem("wv_in"), sem("wv_hi_s"), sem("wv_lo_s")
    ada_added, mod_mm, mod_done = sem("ada_added"), sem("mod_mm"), sem("mod_done")
    x_arr = [sem(f"x_arr{i}") for i in range(4)]
    x_sq, x_ms, x_rstd, x_norm = sem("x_sq"), sem("x_ms"), sem("x_rstd"), sem("x_norm")
    xt_mm, h_made, h_hi, h_lo = sem("xt_mm"), sem("h_made"), sem("h_hi"), sem("h_lo")
    raw_in = [sem("raw_in0"), sem("raw_in1")]
    hi_done, lo_done = sem("hi_done"), sem("lo_done")
    v_mm, v_hi, v_lo = sem("v_mm"), sem("v_hi"), sem("v_lo")
    fm_mm, fm_act = sem("fm_mm"), sem("fm_act")
    rope_cos, rope_sin, rope_sum, rope_hi, rope_lo = (sem("rope_" + n) for n in ("cos", "sin", "sum", "hi", "lo"))
    rope_out = [sem("rope_out0"), sem("rope_out1")]
    cw_in, bkx_in, bk_made = sem("cw_in"), sem("bkx_in"), sem("bk_made")
    cmp_mm, gelu_c, gelu_d, cmp2_mm = sem("cmp_mm"), sem("gelu_c"), sem("gelu_d"), sem("cmp2_mm")
    cmp_hi, cmp_lo = sem("cmp_hi"), sem("cmp_lo")
    pool_zero, pool_add, pooled, pooled_hi, pooled_lo = (
        sem(n) for n in ("pool_zero", "pool_add", "pooled", "pooled_hi", "pooled_lo"))
    wp_hi_s, wp_lo_s, mix_mm, mix_out = sem("wp_hi_s"), sem("wp_lo_s"), sem("mix_mm"), sem("mix_out")
    mix_st = [sem("mix_st0"), sem("mix_st1")]
    gates_done, cmp_zero = sem("gates_done"), sem("cmp_zero")
    q_in = [sem("q_in0"), sem("q_in1")]
    score_mm, max_done, negm_done, exp_done, guard_done, rec_done, norm_done = (
        sem(n) for n in ("score_mm", "max_done", "negm_done", "exp_done", "guard_done", "rec_done", "norm_done"))
    tp_mm, pthi, ptlo, pv_mm = (sem(n) for n in ("tp_mm", "pthi", "ptlo", "pv_mm"))
    o_half, o_sum, gate_mm, gate_tanh = sem("o_half"), sem("o_sum"), sem("gate_mm"), sem("gate_tanh")
    o_st = [sem("o_st0"), sem("o_st1")]
    g_st = [sem("g_st0"), sem("g_st1")]
    op_in = [sem(f"op_in{i}") for i in range(4)]
    op_hi_s, op_lo_s, ada2_added = sem("op_hi_s"), sem("op_lo_s"), sem("ada2_added")
    ada2_in = [sem(f"ada2_in{i}") for i in range(4)]
    gp_row_in, gt_mm, gt_row, gt_st, gt_in = (sem(n) for n in ("gp_row_in", "gt_mm", "gt_row", "gt_st", "gt_in"))
    merge_pool = sem("merge_pool")
    mg_in = [sem("mg_in0"), sem("mg_in1")]
    merge_mm, merge_ab, merge_sum, merge_hi, merge_lo = (
        sem(n) for n in ("merge_mm", "merge_ab", "merge_sum", "merge_hi", "merge_lo"))
    mod2_mm, mod2_done = sem("mod2_mm"), sem("mod2_done")
    pooled_w, y_gated, x1n_made, f_gated = sem("pooled_w"), sem("y_gated"), sem("x1n_made"), sem("f_gated")
    y_mm, y_out, y_ms, y_rstd, y_scaled, x1_made, x1_ms, x1_rstd, x1_norm = (
        sem(n) for n in ("y_mm", "y_out", "y_ms", "y_rstd", "y_scaled", "x1_made", "x1_ms", "x1_rstd", "x1_norm"))
    xi_in = [sem("xi_in0"), sem("xi_in1")]
    x1_st = [sem("x1_st0"), sem("x1_st1")]
    x1t_mm, h2_made, h2_hi, h2_lo = sem("x1t_mm"), sem("h2_made"), sem("h2_hi"), sem("h2_lo")
    fc1_mm, relu_done, sq_done, hid_hi_s, hid_lo_s = (
        sem(n) for n in ("fc1_mm", "relu_done", "sq_done", "hid_hi_s", "hid_lo_s"))
    fc2_mm, y2_added = sem("fc2_mm"), sem("y2_added")
    x1i_in = [sem("x1i_in0"), sem("x1i_in1")]
    f_ms, f_rstd, f_scaled, f_made = sem("f_ms"), sem("f_rstd"), sem("f_scaled"), sem("f_made")
    out_st = [sem("out_st0"), sem("out_st1")]

    OUT_SLOT = (0, 1, 2, 3, 4, 5, 0, 1)
    MLP_SPLITS = ((), (), (2,), (3,), (4,), (5, 6), (7,), ())
    N_SMALL, CONSTS = 7, 12
    ROPES = 2 * len(FM_ROPE)
    K_DMAS, Q_DMAS = 8, 4

    def rope_out_count(i):
        return 16 * sum((Q_DMAS if j < 10 else K_DMAS) for j in range(2 + i % 2, i + 1, 2))

    ADD_AT, n_pieces = {}, 0
    for a, count in enumerate((4, 4, 7, 4, 3, 4, 3, 3), -1):
        ADD_AT.update((n, a) for n in range(n_pieces, n_pieces + count))
        n_pieces += count
    assert n_pieces == 4 * KT
    LOAD_AT = {n: ADD_AT[n - 4] + 2 if n >= 4 else 0 for n in range(4 * KT)}

    block = nc.Block().__enter__()

    @block.sync
    def _(sp):
        def load_raw(r, parts):
            if r >= 2:
                sp.wait_ge(lo_done, r - 1)
            for dst, s in parts:
                sp.dma_start(dst, s).then_inc(raw_in[r % 2], 16)

        def raw_k(r):
            return raw[:, r % 2, :].rearrange("p (k n) -> p k n", n=P)

        def load_fm(a):
            load_raw(R_FM + a, parts=((raw_k(R_FM + a), w_in_v[:, :, FM_COLS[a]:FM_COLS[a] + P]),))

        def ada_piece(n):
            if n >= 8:
                sp.wait_ge(ada_added, n - 7)
            k, part = n % KT, 1 - n // KT
            sp.dma_start(ada[:, n % 8, :], w_ada[k * P:(k + 1) * P, part * 1024:(part + 1) * 1024]) \
              .then_inc(ada_in[n % 8], 16)

        with nc.allow_non_contiguous_dma(reason="a few columns"):
            sp.dma_start(c_col, A["c"].rearrange("a (k p) -> p (a k)", p=P)).then_inc(c_in, 16)
        for n in range(4):
            ada_piece(n)
        sp.wait_ge(acc_zero, 1)
        sp.dma_start(ada_acc[0:1, :], b_ada[:, 0:2048]).then_inc(acc_bias, 16)
        with nc.allow_non_contiguous_dma(reason="a few columns"):
            sp.dma_start(g_pre, A["g_pre_mix"].rearrange("a (k p) -> p (a k)", p=P)).then_inc(g_pre_in, 16)
        for n in range(4, 16):
            ada_piece(n)
        for t in range(4):
            sp.dma_start(xt[:, t, :], x_v[:, t, :]).then_inc(x_arr[t], 16)
        sp.dma_start(wv_raw[:, :, 0:P], w_in_v[:, :, C_VS:C_VS + P]).then_inc(wv_in, 16)
        sp.dma_start(wv_raw[:, :, P:WV_COLS], w_in_v[:, :, C_VW:C_VW + P + N_GATE]).then_inc(wv_in, 16)
        for t in range(4, TT):
            sp.wait_ge(x_arr[t % 4], 16)
            sp.dma_start(xt[:, t, :], x_v[:, t, :]).then_inc(x_arr[t % 4], 16)
        for a in range(2):
            load_fm(a)
        sp.wait_ge(ada_added, 16)
        with nc.allow_non_contiguous_dma(reason="a few columns"):
            for dst, s in ((g_mlp, A["g_pre_mlp"].rearrange("a (k p) -> p (a k)", p=P)),
                           (pool_sc, A["pool_scale"].rearrange("a (k p) -> p (a k)", p=P)),
                           (inv_cnt[:, :, :], A["inv_cnt"]),
                           (pe_col[:, 0, :], A["cmp_pe_k"][0].rearrange("(l two) d -> (two d) l", two=2)),
                           (pe_col[:, 1, :], A["cmp_pe_v"][0].rearrange("(l two) d -> (two d) l", two=2)),
                           (w2k[:, :], A["cmp_w2_k"][0]), (w2v[:, :], A["cmp_w2_v"][0])):
                sp.dma_start(dst, s).then_inc(const_in, 16)
        sp.dma_start(cos[:, :], A["cos"]).then_inc(cos_in, 16)
        sp.dma_start(sin[:, :], A["sin"]).then_inc(cos_in, 16)

        def ada2_piece(n):
            if n < 4:
                sp.wait_ge(xt_mm, 2 * KT)
            else:
                sp.wait_ge(ada2_added, n - 3)
            k, part = n // 4, n % 4
            sp.dma_start(ada2[:, part, :], w_ada[k * P:(k + 1) * P, 2048 + part * 1024:3072 + part * 1024]) \
              .then_inc(ada2_in[part], 16)

        def rope_stores(a):
            for ch in range(2):
                i = 2 * FM_ROPE[a] + ch
                sp.wait_ge(rope_lo, i - 1)
                for part, kd in ((r_hi, k_hi), (r_lo, k_lo)):
                    for g in range(2):
                        src = full(part[64 * g:64 * g + 64, i % 2, :])
                        if a in K_BLOCKS:
                            for half in range(2):
                                rows, row = slice(64 * half, 64 * half + 64), 2 * (a - K_BLOCKS[0]) + g
                                sp.dma_start(full(kd[rows, row, ch * CH:(ch + 1) * CH]), src).then_inc(rope_out[i % 2], 16)
                        else:
                            row = 0 if part is r_hi else 64
                            sp.dma_start(q_dram[4 * ch:4 * ch + 4, row:row + 64, 2 * (a - Q_BLOCKS[0]) + g, :]
                                         .rearrange("c d q -> d c q"),
                                         src.rearrange("d (c q) -> d c q", q=P)).then_inc(rope_out[i % 2], 16)

        def cmp_load(kv):
            if kv:
                sp.wait_ge(cmp_mm, 1)
            else:
                sp.wait_ge(h_lo, 16)
            sp.dma_start(cw1[:, :, :], A["cmp_w1_v" if kv else "cmp_w1_k"][0]
                         .rearrange("(l p) j -> p l j", p=P)).then_inc(cw_in, 16)
            if kv:
                sp.wait_ge(fm_act, 4)
                sp.wait_ge(bk_made, 1)
            else:
                sp.wait_ge(rope_sum, 2)
                sp.wait_ge(v_mm, TT)
            src = vc_f if kv else kc_f
            for g in range(2):
                for odd in range(2):
                    sp.dma_start(bkx[64 * odd:64 * odd + 64, g, 0:SEQ - odd],
                                 src[64 * g:64 * g + 64, odd:SEQ]).then_inc(bkx_in, 16)

        def bias2():
            sp.wait_ge(acc_zero, 2)
            sp.dma_start(acc2[0:1, :, :], b_ada[:, 2048:6144].rearrange("a (f n) -> a f n", n=1024)) \
              .then_inc(acc_bias, 16)

        for a in range(N_FM):
            if a:
                load_fm(a + 1)
            if a == 0:
                bias2()
            if a == 3:
                cmp_load(0)
            if a == 6:
                cmp_load(1)
            for n in range(4 * KT):
                if LOAD_AT[n] == a:
                    ada2_piece(n)
            if a - 2 in FM_ROPE and 0 < a - 2 < 6:
                rope_stores(a - 2)
            if a == 8:
                sp.wait_ge(cmp_mm, 2)
                sp.dma_start(wp_raw[:, :, :], A["w_pool"][0].rearrange("g c d -> c g d")).then_inc(wp_in, 16)
                for f, g in enumerate(("g_post_mix", "g_post_mlp")):
                    sp.wait_ge(ada2_added, 4 * KT)
                    sp.dma_start(ada2[0:1, f, :], A[g]).then_inc(gp_row_in, 16)
            if a == 9:
                sp.wait_ge(gt_row, 4)
                sp.dma_start(gt_dram.rearrange("(a f) n -> a f n", a=1), ada2[0:1, 0:2, :]).then_inc(gt_st, 16)
                sp.wait_ge(gt_st, 16)
                sp.wait_ge(mod2_mm, 1)
                rope_stores(6)
            if a == 10:
                rope_stores(7)

        def mix_store(g):
            for n in (2 * g, 2 * g + 1):
                sp.wait_ge(mix_out, n + 1)
                sp.dma_start(pool_dram[g * P:(g + 1) * P, (n % 2) * CH:(n % 2 + 1) * CH],
                               pm[:, n % 2, :]).then_inc(mix_st[n % 2], 16)

        def load_q(c):
            if c == 0:
                for s in range(2):
                    sp.wait_ge(rope_out[s], rope_out_count(ROPES - 2 + s))
                sp.wait_ge(bkx_in, 128)
            if c >= 2:
                sp.wait_ge(score_mm, STEPS * 4 * (c - 1))
            sp.dma_start(full(q_st[:, c % 2, :, :]), q_dram[c]).then_inc(q_in[c % 2], 16)

        load_fm(N_FM + 1)
        mix_store(0)
        load_q(0)
        load_q(1)
        mix_store(1)
        for m in range(2, N_BR):
            load_fm(N_FM + m)
            if m == 2:
                mix_store(2)
                mix_store(3)
            if m % 2 == 1 and m // 2 + 1 < TT and m >= 3:
                load_q(m // 2 + 1)

        def merge_weights(q, b):
            r = R_MERGE + b
            sp.wait_ge(lo_done, 2 * q + (r - 1))
            cols = bass.ds(2 * P * q + b * P, P)
            sp.dma_start(raw_k(r)[:, 0:4, :], w_brp_v[:, :, cols]).then_inc(raw_in[r % 2], 16)
            sp.dma_start(raw_k(r)[:, 4:8, :], w_brn_v[:, :, cols]).then_inc(raw_in[r % 2], 16)

        def merge_gates(q, b, first=False):
            for ch in range(2):
                if not first:
                    sp.wait_ge(merge_ab, 4 * q + (2 * b + ch - 1))
                sp.dma_start(mg[:, ch, :, :], g_dram[:, bass.ds(2 * q + b, 1), ch, :, :]
                             .rearrange("h m p n -> p (h m) n")).then_inc(mg_in[ch], 16)

        merge_weights(0, 0)
        merge_weights(0, 1)
        for s in range(2):
            sp.wait_ge(mix_st[s], 16 * 4)
        sp.wait_ge(score_mm, STEPS * UNITS)
        for i in range(4):
            sp.dma_start(op_raw[0][:, i, :], pool_dram[i * P:(i + 1) * P, :]).then_inc(op_in[i], 16)
        sp.wait_ge(pv_mm, BANKS_BEFORE[UNITS])
        for i in range(4):
            for v in (UNITS - 5 + i, UNITS - 4 + i):
                sp.wait_ge(o_st[v % 2], 16 * (v // 2 + 1))
            sp.wait_ge(op_in[i], 16)
            sp.dma_start(op_raw[1][:, i, :], o_dram[i * P:(i + 1) * P, :]).then_inc(op_in[i], 16)
        for s in range(2):
            sp.wait_ge(g_st[s], 16 * HALVES // 2)
        merge_gates(0, 0, first=True)
        with sp.Fori(1, KT // 2) as q:
            merge_weights(q, 0)
            merge_gates(q - 1, 1)
            merge_weights(q, 1)
            merge_gates(q, 0)

        for n in range(8):
            r, half, s = R_OUT + n, n // 4, n % 4
            if n == 2:
                merge_gates(KT // 2 - 1, 1)
            sp.wait_ge(lo_done, r - 1)
            sp.dma_start(raw[:, r % 2, :].rearrange("p (k n) -> p k n", n=CH),
                         w_out_v[:, 2 * s:2 * s + 2, half * CH:(half + 1) * CH]).then_inc(raw_in[r % 2], 16)
            if n == 3:
                for f, dst in enumerate((gt1, gt2)):
                    sp.dma_start(dst[:, :], gt_dram[f:f + 1, :].to_broadcast([P, D_MODEL])).then_inc(gt_in, 16)
                sp.wait_ge(merge_lo, KT)
                for t in range(2):
                    sp.dma_start(x_in[:, t, :], x_v[:, t, :]).then_inc(xi_in[t], 16)

        def mlp_loads(j, ns=range(8)):
            for n in ns:
                sp.wait_ge(lo_done, 8 * j + (R_MLP + n - 1))
                s = (R_MLP + n) % 2
                if n < 4:
                    src = w_fc1_v[:, :, bass.ds(j * CH + n * P, P)]
                    sp.dma_start(raw_k(s), src).then_inc(raw_in[s], 16)
                else:
                    sp.dma_start(raw[:, s, :], w_fc2_v[:, bass.ds(4 * j + (n - 4), 1), :]
                                 .rearrange("p k n -> p (k n)")).then_inc(raw_in[s], 16)

        for t in range(2, TT):
            sp.wait_ge(x1_made, t - 1)
            sp.dma_start(x_in[:, t % 2, :], x_v[:, t, :]).then_inc(xi_in[t % 2], 16)
            if t == 5:
                mlp_loads(0, range(0, 2))
        mlp_loads(0, range(2, 8))
        with sp.Fori(1, D_FF // CH) as j:
            mlp_loads(j)
        sp.wait_ge(fc1_mm, 8 * (D_FF // CH))
        for s in range(2):
            sp.wait_ge(x1_st[s], 16 * TT // 2)
        for t in range(TT + 1):
            if t >= 2:
                sp.wait_ge(f_made, t - 1)
            if t < TT:
                sp.dma_start(x1_in[:, t % 2, :], x1_v[:, t, :]).then_inc(x1i_in[t % 2], 16)
            if t >= 2:
                sp.dma_start(out_v[:, t - 2, :], fin[:, t % 2, :]).then_inc(out_st[t % 2], 16)
        sp.wait_ge(f_made, TT)
        sp.dma_start(out_v[:, TT - 1, :], fin[:, (TT - 1) % 2, :]).then_inc(out_st[(TT - 1) % 2], 16)
        for s in range(2):
            sp.wait_ge(out_st[s], 16 * TT // 2)

    @block.gpsimd
    def _(pool):
        def made(ins):
            made.n += 1
            ins.then_inc(consts_made, 1)
        made.n = 0
        pool.memset(ada_acc[:, :], 0.0).then_inc(acc_zero, 1)
        for t, v in ((ident, 0.0), (ident_b, 0.0), (mask_diag, 0.0), (mask_far, 0.0), (ones, 1.0), (half_neg, -0.5)):
            made(pool.memset(t if t is half_neg else t[:, :], v))
        made(pool.memset(mask_cmp[:, :, :], 0.0))
        pool.wait_ge(consts_made, made.n)
        for t in (ident, ident_b):
            made(pool.affine_select(out=t[:, :], in_=t[:, :], compare_op=ALU.not_equal, fill=1.0,
                                    base=0, pattern=[[-1, P]], channel_multiplier=1))
        made(pool.affine_select(out=mask_diag[:, :], in_=mask_diag[:, :], compare_op=ALU.is_ge, fill=NEG,
                                base=0, pattern=[[-1, P]], channel_multiplier=1))
        made(pool.affine_select(out=mask_far[:, :], in_=mask_far[:, :], compare_op=ALU.is_gt, fill=NEG,
                                base=0, pattern=[[1, P]], channel_multiplier=-1))
        made(pool.affine_select(out=mask_cmp[:, :, :], in_=mask_cmp[:, :, :], compare_op=ALU.is_ge, fill=NEG,
                                base=1 - CMP_BLOCK, pattern=[[P, TT], [-CMP_STRIDE, 64]], channel_multiplier=1))
        assert made.n == CONSTS
        pool.memset(full(kc_hi[:, :, :]), 0.0).then_inc(cmp_zero, 1)
        pool.memset(full(kc_lo[:, :, :]), 0.0).then_inc(cmp_zero, 1)
        pool.memset(full(vc_st[:, :, :]), 0.0).then_inc(cmp_zero, 1)
        def rstd_of(ms, t, sem_in, sem_ms, sem_out):
            pool.wait_ge(sem_in, t + 1)
            pool.tensor_scalar(ms, ms, 1.0 / D_MODEL, EPS, ALU.mult, ALU.add).then_inc(sem_ms, 1)
            pool.wait_ge(sem_ms, t + 1)
            pool.tensor_tensor(ms, ms, half_neg[:, 0:1], ALU.pow).then_inc(sem_out, 1)

        def x_rstd_of(t):
            rstd_of(msq[:, t:t + 1], t, x_sq, x_ms, x_rstd)

        for t in range(4):
            x_rstd_of(t)
        for i in range(4):
            pool.wait_ge(wv_hi_s, i + 1)
            pool.tensor_tensor(wv_lo[:, 2 * i:2 * i + 2, :], wv_raw[:, 2 * i:2 * i + 2, :],
                               full(wv_hi[:, 2 * i:2 * i + 2, :]), ALU.subtract).then_inc(wv_lo_s, 1)
            if i:
                x_rstd_of(3 + i)
        x_rstd_of(7)
        pool.wait_ge(xt_mm, 2 * KT)
        pool.memset(acc2[:, :, :], 0.0).then_inc(acc_zero, 1)
        pool.wait_ge(cos_in, 32)
        for a, k in FM_ROPE.items():
            for ch in range(2):
                i, sl = 2 * k + ch, slice(ch * CH, (ch + 1) * CH)
                pool.wait_ge(fm_act, 2 * a + ch + 1)
                pool.tensor_tensor(r_sin[:, i % 2, :], r_swap[:, i % 2, :], sin[:, sl], ALU.mult).then_inc(rope_sin, 1)
                pool.wait_ge(rope_sin, i + 1)
                pool.wait_ge(rope_cos, i + 1)
                dst = kc_f[:, sl] if a == 0 else r_cos[:, i % 2, :]
                pool.tensor_tensor(dst, r_cos[:, i % 2, :], r_sin[:, i % 2, :], ALU.add).then_inc(rope_sum, 1)
        pool.wait_ge(cmp_mm, 2)
        for t in (pu, ps_ab[0], ps_ab[1]):
            pool.memset(t[:, 0:PAD], 0.0).then_inc(pool_zero, 1)
        pool.wait_ge(pool_zero, 3)
        n_add = 0

        for g in range(3):
            pool.wait_ge(fm_act, 2 * (8 + g) + 2)
            if g:
                pool.wait_ge(pooled_lo, g)
            src = pu
            for step in range(g + 1):
                dst, back = ps_ab[step % 2], 1 << step
                if step:
                    pool.wait_ge(pool_add, n_add)
                pool.tensor_tensor(dst[:, PAD:], src[:, PAD:], src[:, PAD - back:PAD + SEQ - back], ALU.add) \
                    .then_inc(pool_add, 1)
                n_add += 1
                src = dst
        pool.wait_ge(rope_out[0], rope_out_count(ROPES - 2))
        pool.wait_ge(rope_out[1], rope_out_count(ROPES - 1))
        pool.memset(p_cmp[:, :, :, :], 0.0).then_inc(cmp_zero, 1)
        def gate_store(h):
            m = h // 2
            pool.wait_ge(gate_tanh, h + 1)
            pool.dma_start(g_dram[m // KT, m % KT, h % 2], g_out[:, h % 2, :]).then_inc(g_st[h % 2], 16)


        def guards(u, s):
            n, k = STEPS * u + s, 2 if s == 4 else 1
            pool.wait_ge(exp_done, n + 1)
            pool.tensor_scalar(ssum[:, n % 4, 0:k], ssum[:, n % 4, 0:k], 1e-30, None, ALU.max).then_inc(guard_done, 1)

        def split_gate_block(a):
            pool.wait_ge(lo_done, R_FM + a)
            pool.wait_ge(hi_done, R_FM + a + 1)
            pool.tensor_tensor(a_lo[:, a % 2, :], raw[:, (R_FM + a) % 2, :], full(a_hi[:, a % 2, :]),
                               ALU.subtract).then_inc(lo_done, 1)

        for it in range(UNITS + 1):
            half = HALF_OF.get(it)
            if it < UNITS:
                guards(it, 0)
            if half is not None and half % 2 == 0 and half + 2 < HALVES:
                split_gate_block(N_FM + half // 2 + 1)
            if it < UNITS:
                for s in range(1, STEPS):
                    guards(it, s)
            if it == 0:
                gate_store(0)
                gate_store(1)
            if half is not None:
                gate_store(half)
            if it:
                v = it - 1
                pool.wait_ge(o_sum, v + 1)
                c, pair = v // 4, v % 4
                pool.dma_start(o_dram[pair * P:(pair + 1) * P, c * P:(c + 1) * P].rearrange("(h d) q -> d h q", h=2),
                               o_out[:, v % 2, :].rearrange("d (h q) -> d h q", h=2)).then_inc(o_st[v % 2], 16)
        gate_store(HALVES - 1)

        with pool.Fori(0, KT // 2) as q:
            for b in range(2):
                for ch in range(2):
                    sl = slice(ch * CH, (ch + 1) * CH)
                    pool.wait_ge(merge_ab, 4 * q + (2 * b + ch + 1))
                    pool.tensor_tensor(m_a[:, b, sl], m_a[:, b, sl], m_b[:, ch, :], ALU.add).then_inc(merge_sum, 1)

        for t in range(TT + 1):
            if t < TT:
                rstd_of(stat[:, t:t + 1], t, y_ms, y_scaled, y_rstd)
            if t:
                v = t - 1
                rstd_of(stat[:, 8 + v:9 + v], v, x1_ms, x1_norm, x1_rstd)
                pool.dma_start(x1_v[:, v, :], x1[:, v % 2, :]).then_inc(x1_st[v % 2], 16)

        def squares(j):
            for n in range(8):
                pool.wait_ge(relu_done, 8 * j + (n + 1))
                pool.tensor_tensor(relu[:, n % 2, :], relu[:, n % 2, :], relu[:, n % 2, :], ALU.mult).then_inc(sq_done, 1)

        squares(0)
        with pool.Fori(1, D_FF // CH) as j:
            squares(j)
        for t in range(TT):
            rstd_of(stat[:, 16 + t:17 + t], t, f_ms, f_scaled, f_rstd)

    @block.scalar
    def _(act):
        def split_hi(r, dst, free):
            act.wait_ge(raw_in[r % 2], raw_count(r))
            if free:
                act.wait_ge(*free)
            act.activation(dst, raw[:, r % 2, :], ACT.Copy).then_inc(hi_done, 1)

        def split_a(a):
            free = None
            if a >= 2:
                free = (fm_mm, 2 * a - 2) if a - 2 < N_FM else (gate_mm, 2 * (a - 2 - N_FM) + 2)
            split_hi(R_FM + a, a_hi[:, a % 2, :], free)

        act.wait_ge(c_in, 16)
        act.activation(silu_c, c_col, ACT.Tanh, scale=0.5).then_inc(silu_steps, 1)
        def square_x(t):
            act.wait_ge(x_arr[t % 4], 16 * (t // 4 + 1))
            if t:
                act.wait_ge(x_sq, t)
            act.activation(junk[:, :], xt[:, t, :], ACT.Square, accum_out=msq[:, t:t + 1]).then_inc(x_sq, 1)

        for t in range(4):
            square_x(t)

        def v_evict(t):
            b = 4 + t % 4
            act.wait_ge(v_mm, t + 1)
            act.activation(v_st[:, t, :, 0:64], ps[:, b, 0:256].rearrange("p (f d) -> p f d", d=64),
                           ACT.Copy).then_inc(v_hi, 1)
            act.activation(gates[:, t, :], ps[:, b, 256:WV_COLS], ACT.Tanh, scale=0.5).then_inc(v_hi, 1)

        def wv_split(i):
            act.activation(wv_hi[:, 2 * i:2 * i + 2, :], wv_raw[:, 2 * i:2 * i + 2, :], ACT.Copy).then_inc(wv_hi_s, 1)

        act.wait_ge(wv_in, 32)
        wv_split(0)
        act.wait_ge(mod_done, 2)
        for n in range(2 * KT):
            act.wait_ge(xt_mm, n + 1)
            if n >= 2:
                act.wait_ge(h_lo, n - 1)
            k = n % KT
            act.activation(h_tmp[:, n % 2, :], ps[:, n % 4, :], ACT.Identity, scale=scale[:, k:k + 1],
                           bias=shift[:, k:k + 1]).then_inc(h_made, 1)
            if n < 3:
                wv_split(n + 1)
            if 1 <= n < 5:
                square_x(n + 3)
            if 8 <= n < 12:
                v_evict(n - 8)
        split_a(0)
        split_a(1)
        for t in range(4, TT):
            v_evict(t)

        def rope_hi_part(i):
            act.wait_ge(rope_sum, i + 1)
            if i >= 4:
                act.wait_ge(rope_out[i % 2], rope_out_count(i - 2))
            act.activation(r_hi[:, i % 2, :], r_cos[:, i % 2, :], ACT.Copy).then_inc(rope_hi, 1)

        def fm_evict(a, ch):
            g = 2 * a + ch
            act.wait_ge(fm_mm, g + 1)
            bank, sl = g % 4, slice(ch * CH, (ch + 1) * CH)
            if a in FM_ROPE:
                i = 2 * FM_ROPE[a] + ch
                if i >= 2:
                    act.wait_ge(rope_sin, i - 1)
                for q in range(4):
                    ins = act.activation(r_swap[32 * q:32 * q + 32, i % 2, :],
                                         ps[32 * (q ^ 1):32 * (q ^ 1) + 32, bank, :], ACT.Copy)
                ins.then_inc(fm_act, 1)
            elif a == 1:
                act.activation(vc_f[:, sl], ps[:, bank, :], ACT.Copy).then_inc(fm_act, 1)
            else:
                if ch == 0:
                    if a == 8:
                        act.wait_ge(pool_zero, 3)
                    else:
                        act.wait_ge(pooled_lo, a - 8)
                act.activation(pu[:, PAD + ch * CH:PAD + (ch + 1) * CH], ps[:, bank, :], ACT.Copy).then_inc(fm_act, 1)

        def gelu(kv):
            act.wait_ge(cmp_mm, kv + 1)
            act.activation(gelu_x[:, kv, :], ps[0:64, 6, P * kv:P * kv + 126], ACT.Copy).then_inc(gelu_c, 1)
            act.wait_ge(gelu_d, 5 * kv + 3)
            act.activation(gelu_t[:, kv, :], gelu_t[:, kv, :], ACT.Tanh, scale=float(np.sqrt(2 / np.pi))).then_inc(gelu_c, 1)

        def cmp_store():
            act.wait_ge(cmp_zero, 3)
            act.wait_ge(cmp2_mm, 2)
            for half in range(2):
                act.activation(kc_hi[64 * half:64 * half + 64, :, 0:N_CMP],
                               ps[0:64, 6, 256:382].rearrange("p (g n) -> p g n", g=2), ACT.Copy).then_inc(cmp_hi, 1)
            act.activation(vc_st[0:N_CMP, :, 0:64], ps[0:N_CMP, 6, 384:512].rearrange("p (g d) -> p g d", g=2),
                           ACT.Copy).then_inc(cmp_hi, 1)

        def pooled_hi_part(g):
            act.wait_ge(pooled, 2 * g + 2)
            if g:
                act.wait_ge(mix_mm, 2 * g)
            act.activation(pp_hi[:, :], ps_ab[(g + 1) % 2][:, PAD:], ACT.Copy).then_inc(pooled_hi, 1)

        def mix_evict(g):
            for ch in range(2):
                n = 2 * g + ch
                if n < 2:
                    act.wait_ge(rope_out[n], rope_out_count(ROPES - 2 + n))
                act.wait_ge(mix_mm, n + 1)
                if n >= 2:
                    act.wait_ge(mix_st[n % 2], 16 * (n // 2))
                act.activation(pm[:, n % 2, :], ps[:, 4 + n % 2, :], ACT.Copy, scale=pool_sc[:, g:g + 1]) \
                    .then_inc(mix_out, 1)

        for a in range(N_FM):
            if a - 1 in FM_ROPE and 1 < a < 8:
                for ch in range(2):
                    rope_hi_part(2 * FM_ROPE[a - 1] + ch)
            for ch in range(2):
                fm_evict(a, ch)
            split_a(a + 2)
            if a == 5:
                act.wait_ge(const_in, 16 * N_SMALL)
                gelu(0)
            if a == 7:
                gelu(1)
            if a == 8:
                cmp_store()
            if a == 8:
                act.wait_ge(wp_in, 16)
                act.activation(wp_hi[:, :, :], wp_raw[:, :, :], ACT.Copy).then_inc(wp_hi_s, 1)
            if a >= 8:
                pooled_hi_part(a - 8)
            if a == 8:
                for ch in range(2):
                    rope_hi_part(ROPES - 2 + ch)
            if a >= 9:
                mix_evict(a - 9)

        def gate_evict(h):
            act.wait_ge(gate_mm, h + 1)
            if h >= 2:
                act.wait_ge(g_st[h % 2], 16 * (h // 2))
            act.activation(g_out[:, h % 2, :], ps[:, 6 if h == 1 else 7, :], ACT.Tanh, scale=0.5).then_inc(gate_tanh, 1)

        gate_evict(0)
        gate_evict(1)
        mix_evict(3)

        act.wait_ge(cmp_zero, 4)

        def exps(u, s):
            c, n = u // 4, STEPS * u + s
            act.wait_ge(negm_done, n + 1)
            if u >= 2 and s == 0:
                act.wait_ge(tp_mm, BANKS_BEFORE[u - 1])
            if s < 4:
                hh, branch = s % 2, s // 2
                parts = score_parts(c, branch)
                w = parts[0][1]
                src = ps[:, 2 * (n % 2):2 * (n % 2) + len(parts), 0:w]
                dst = (p_sel, p_win)[branch][:, u % 2, hh, 0:w * len(parts)].rearrange("p (a w) -> p a w", w=w)
                act.activation(dst, src, ACT.Exp, bias=negm[:, n % 4, 0:1], scale=HEAD_DIM ** -0.5,
                               accum_out=ssum[:, n % 4, 0:1]).then_inc(exp_done, 1)
            else:
                w = cmp_width(c)
                for hh in range(2):
                    ins = act.activation(p_cmp[:, u % 2, hh, 0:w], ps[:, 2 * (n % 2), 64 * hh:64 * hh + w],
                                         ACT.Exp, bias=negm[:, n % 4, hh:hh + 1], scale=HEAD_DIM ** -0.5,
                                         accum_out=ssum[:, n % 4, hh:hh + 1])
                ins.then_inc(exp_done, 1)

        def transposed_hi(u, b):
            n = BANKS_BEFORE[u] + b
            act.wait_ge(tp_mm, n + 1)
            if n == 0:
                for s in range(2):
                    act.wait_ge(mix_st[s], 16 * 4)
            if n >= 3:
                act.wait_ge(pv_mm, n - 2)
            w = 256 * min(2, len(key_tiles(u // 4)) - 2 * b)
            act.activation(pt_hi[:, n % 3, 0:w], ps[:, 4 + n % 2, 0:w], ACT.Copy).then_inc(pthi, 1)

        def merge_w_hi(q, b, free):
            r = R_MERGE + b
            act.wait_ge(raw_in[r % 2], 32 * q + raw_count(r))
            act.wait_ge(*free)
            act.activation(a_hi[:, b, :], raw[:, r % 2, :], ACT.Copy).then_inc(hi_done, 1)

        for it in range(UNITS + 1):
            half = HALF_OF.get(it)
            for i in range(SLOTS):
                if it:
                    for b in range(n_banks(it - 1)):
                        if tp_slot(it - 1, b) == i:
                            transposed_hi(it - 1, b)
                if i == SLOTS - 1 and half is not None:
                    gate_evict(half)
                if it < UNITS and i % 2 == 0:
                    exps(it, i // 2)
                if i == 1 and half is not None and half % 2 == 0 and half + 2 < HALVES:
                    split_a(N_FM + half // 2 + 1)
                if i == 1 and it == UNITS:
                    merge_w_hi(0, 0, (gate_mm, HALVES - 2))
            if it:
                v = it - 1
                act.wait_ge(pv_mm, BANKS_BEFORE[v + 1])
                if v >= 2:
                    act.wait_ge(o_sum, v - 1)
                act.activation(o_tmp[:, v % 2, :], ps[64:128, 6, 0:256], ACT.Copy).then_inc(o_half, 1)

        def out_w_hi(n):
            r, s = R_OUT + n, OUT_SLOT[n]
            act.wait_ge(raw_in[r % 2], raw_count(r))
            if 2 <= n < 6:
                act.wait_ge(merge_pool, KT)
            if n >= 6:
                act.wait_ge(y_mm, TT)
            act.activation(b_hi[s][:, :], raw[:, r % 2, :], ACT.Copy).then_inc(hi_done, 1)

        for i in range(KT):
            act.wait_ge(op_in[i % 4], 16 * (i // 4 + 1))
            act.activation(op_hi[i // 4][:, i % 4, :], op_raw[i // 4][:, i % 4, :], ACT.Copy).then_inc(op_hi_s, 1)
            if i == 3:
                gate_evict(HALVES - 1)
                merge_w_hi(0, 1, (gate_mm, HALVES))
        with act.Fori(0, KT // 2 - 1) as q:
            for b in range(2):
                act.wait_ge(merge_sum, 4 * q + (2 * b + 2))
                merge_w_hi(q + 1, b, (merge_mm, 4 * q + (2 * b + 2)))
                act.activation(act_hi[:, bass.ds(2 * q + b, 1), :].rearrange("p k n -> p (k n)"), m_a[:, b, :],
                               ACT.Copy, scale=0.5).then_inc(merge_hi, 1)
        for b in range(2):
            m = KT - 2 + b
            for n in ((0,), (1, 2, 3))[b]:
                out_w_hi(n)
            act.wait_ge(merge_sum, 2 * m + 2)
            act.activation(act_hi[:, m, :], m_a[:, b, :], ACT.Copy, scale=0.5).then_inc(merge_hi, 1)

        def h2_evict(half):
            for k in range(KT):
                m = KT * half + k
                act.wait_ge(x1t_mm, m + 1)
                if m >= 2:
                    act.wait_ge(h2_lo, m - 1)
                act.activation(h2_tmp[:, m % 2, :], ps[:, 4 * half + m % 4, :], ACT.Identity, scale=scale2[:, k:k + 1],
                               bias=shift2[:, k:k + 1]).then_inc(h2_made, 1)

        def y_evict(n):
            act.wait_ge(y_mm, n + 1)
            act.activation(y[:, n % TT, (n // TT) * CH:(n // TT + 1) * CH], ps[:, 4 * (n // TT) + n % 4, :], ACT.Copy) \
                .then_inc(y_out, 1)

        def x1_square(t):
            act.wait_ge(x1_made, t + 1)
            act.wait_ge(y_ms, min(t + 2, TT))
            act.activation(junk2[:, :], x1[:, t % 2, :], ACT.Square, accum_out=stat[:, 8 + t:9 + t]).then_inc(x1_ms, 1)

        def y_second_half():
            for t in range(TT):
                y_evict(TT + t)
                act.wait_ge(y_out, TT + t + 1)
                if t >= 2:
                    act.wait_ge(x1_ms, t - 1)
                act.activation(junk2[:, :], y[:, t, :], ACT.Square, accum_out=stat[:, t:t + 1]).then_inc(y_ms, 1)
                if t:
                    x1_square(t - 1)
                if t == 5:
                    h2_evict(0)
                    mlp_split(0, 0, first=True)
                    mlp_split(0, 1, first=True)
            act.wait_ge(x1_ms, TT - 1)
            x1_square(TT - 1)

        def mlp_split(j, n, first=False):
            s = (R_MLP + n) % 2
            act.wait_ge(raw_in[s], 64 * j + raw_count(R_MLP + n))
            if n < 4:
                if first and n < 2:
                    act.wait_ge(merge_mm, 2 * KT - 2 + 2 * n)
                else:
                    act.wait_ge(fc1_mm, 8 * j + (-1, 0, 3, 4)[n])
                act.activation(a_hi[:, (A_MLP + n) % 2, :], raw[:, s, :], ACT.Copy).then_inc(hi_done, 1)
            else:
                if first:
                    act.wait_ge(y_mm, 2 * TT)
                else:
                    act.wait_ge(fc2_mm, 2 * TT * j)
                act.activation(b_hi[n - 4][:, :], raw[:, s, :], ACT.Copy).then_inc(hi_done, 1)

        for n in range(4, 6):
            out_w_hi(n)
        for n in range(TT):
            y_evict(n)
        out_w_hi(6)
        out_w_hi(7)
        y_second_half()

        def mlp(j, first=False):
            if not first:
                mlp_split(j, 0)
                mlp_split(j, 1)
            for n in range(8):
                m, ch = 2 * (n // 4) + n % 2, (n // 2) % 2
                act.wait_ge(fc1_mm, 8 * j + (n + 1))
                if not (first and n < 2):
                    act.wait_ge(hid_lo_s, 8 * j + (n - 1))
                elif n == 1:
                    act.wait_ge(h2_lo, 2 * KT)
                act.activation(relu[:, n % 2, :], ps[:, n % 4, :], ACT.Relu).then_inc(relu_done, 1)
                for x in MLP_SPLITS[n]:
                    mlp_split(j, x, first)
                act.wait_ge(sq_done, 8 * j + (n + 1))
                act.activation(hid_hi[:, m, ch * CH:(ch + 1) * CH], relu[:, n % 2, :], ACT.Copy).then_inc(hid_hi_s, 1)

        h2_evict(1)
        mlp(0, first=True)
        with act.Fori(1, D_FF // CH) as j:
            mlp(j)
        for t in range(TT):
            act.wait_ge(y2_added, 2 * TT * (D_FF // CH - 1) + 2 * t + 2)
            if t:
                act.wait_ge(f_ms, t)
            act.activation(junk3[:, :], y[:, t, :], ACT.Square, accum_out=stat[:, 16 + t:17 + t]).then_inc(f_ms, 1)

    @block.vector
    def _(dve):
        def split_lo(r, dst, hi, src=None):
            dve.wait_ge(hi_done, r + 1)
            dve.tensor_tensor(dst, raw[:, r % 2, :] if src is None else src, full(hi), ALU.subtract).then_inc(lo_done, 1)

        def split_a(a):
            split_lo(R_FM + a, a_lo[:, a % 2, :], a_hi[:, a % 2, :])

        dve.wait_ge(silu_steps, 1)
        dve.tensor_scalar(silu_c, silu_c, 0.5, 0.5, ALU.mult, ALU.add).then_inc(silu_steps, 1)
        dve.wait_ge(silu_steps, 2)
        dve.tensor_tensor(silu_c, silu_c, c_col, ALU.mult).then_inc(silu_steps, 1)
        dve.wait_ge(silu_steps, 3)
        dve.wait_ge(acc_bias, 16)
        def normalise_x(t):
            dve.wait_ge(x_rstd, t + 1)
            dve.tensor_scalar(xt[:, t, :], xt[:, t, :], msq[:, t:t + 1], None, ALU.mult).then_inc(x_norm, 1)

        for n in range(16):
            dve.wait_ge(ada_in[n % 8], 16 * (n // 8 + 1))
            if n % KT:
                dve.wait_ge(ada_added, n)
            k, part = n % KT, 1 - n // KT
            sl = slice(part * 1024, (part + 1) * 1024)
            dve.scalar_tensor_tensor(out=ada_acc[:, sl], in0=ada[:, n % 8, :], scalar=silu_c[:, k:k + 1],
                                     in1=ada_acc[:, sl], op0=ALU.mult, op1=ALU.add).then_inc(ada_added, 1)
            if n == 10:
                dve.wait_ge(mod_mm, 1)
                dve.wait_ge(g_pre_in, 16)
                dve.scalar_tensor_tensor(out=scale, in0=ps[:, 7, 8:16], scalar=1.0, in1=g_pre, op0=ALU.add,
                                         op1=ALU.mult).then_inc(mod_done, 1)
        for t in range(3):
            normalise_x(t)
        dve.wait_ge(mod_mm, 2)
        dve.tensor_copy(shift, ps[:, 7, 0:8]).then_inc(mod_done, 1)
        normalise_x(3)

        def split_h(src, n, made, hi_s, lo_s):
            k, sl = n % KT, slice((n // KT) * CH, (n // KT + 1) * CH)
            dve.wait_ge(made, n + 1)
            dve.tensor_copy(act_hi[:, k, sl], src[:, n % 2, :]).then_inc(hi_s, 1)
            dve.wait_ge(hi_s, n + 1)
            dve.tensor_tensor(act_lo[:, k, sl], src[:, n % 2, :], full(act_hi[:, k, sl]), ALU.subtract).then_inc(lo_s, 1)

        def v_split(t):
            dve.wait_ge(v_hi, 2 * t + 2)
            dve.tensor_tensor(v_st[:, t, :, 64:128], ps[:, 4 + t % 4, 0:256].rearrange("p (f d) -> p f d", d=64),
                              full(v_st[:, t, :, 0:64]), ALU.subtract).then_inc(v_lo, 1)

        for n in range(2 * KT):
            split_h(h_tmp, n, h_made, h_hi, h_lo)
            if 4 <= n < 8:
                normalise_x(n)
            if 8 <= n < 12:
                v_split(n - 8)
        split_a(0)
        split_a(1)
        for t in range(4, TT):
            v_split(t)
        dve.wait_ge(v_hi, 2 * TT)
        dve.tensor_scalar(gates[:, :, :], gates[:, :, :], 0.5, 0.5, ALU.mult, ALU.add).then_inc(gates_done, 1)

        def rope_cos_part(a, ch):
            i, g = 2 * FM_ROPE[a] + ch, 2 * a + ch
            dve.wait_ge(fm_act, g + 1)
            if i == 0:
                dve.wait_ge(cos_in, 32)
            if i in (2, 3):
                dve.wait_ge(rope_sum, i - 1)
            if i >= 4:
                dve.wait_ge(rope_hi, i - 3)
                dve.wait_ge(rope_lo, i - 3)
            dve.tensor_tensor(r_cos[:, i % 2, :], ps[:, g % 4, :], cos[:, ch * CH:(ch + 1) * CH], ALU.mult) \
                .then_inc(rope_cos, 1)

        def rope_lo_part(i):
            dve.wait_ge(rope_hi, i - 1)
            dve.tensor_tensor(r_lo[:, i % 2, :], r_cos[:, i % 2, :], full(r_hi[:, i % 2, :]), ALU.subtract) \
                .then_inc(rope_lo, 1)

        def make_blocks(kv):
            dve.wait_ge(bkx_in, 64 * (kv + 1))
            if kv:
                dve.wait_ge(cmp_mm, 1)
            for g in range(2):
                for h in range(2):
                    src = bkx[:, g, 16 * h:16 * h + 16 * N_CMP].rearrange("p (n l two) -> p l n two", l=8, two=2)[:, :, :, 0]
                    pe_b = pe_col[:, kv, 8 * h:8 * h + 8].unsqueeze(2).to_broadcast([P, 8, N_CMP])
                    ins = dve.tensor_tensor(bk[:, 8 * h:8 * h + 8, g, :], src, pe_b, ALU.add)
            ins.then_inc(bk_made, 1)

        def gelu(kv):
            x, t = gelu_x[:, kv, :], gelu_t[:, kv, :]
            n = 5 * kv
            dve.wait_ge(gelu_c, 2 * kv + 1)
            dve.tensor_tensor(t, x, x, ALU.mult).then_inc(gelu_d, 1)
            dve.wait_ge(gelu_d, n + 1)
            dve.tensor_scalar(t, t, 0.044715, 1.0, ALU.mult, ALU.add).then_inc(gelu_d, 1)
            dve.wait_ge(gelu_d, n + 2)
            dve.tensor_tensor(t, t, x, ALU.mult).then_inc(gelu_d, 1)
            dve.wait_ge(gelu_c, 2 * kv + 2)
            dve.scalar_tensor_tensor(out=t, in0=t, scalar=1.0, in1=x, op0=ALU.add, op1=ALU.mult).then_inc(gelu_d, 1)
            dve.wait_ge(gelu_d, n + 4)
            dve.tensor_scalar(t, t, 0.5, None, ALU.mult).then_inc(gelu_d, 1)

        def cmp_store():
            dve.wait_ge(cmp_hi, 3)
            for half in range(2):
                dve.tensor_tensor(kc_lo[64 * half:64 * half + 64, :, 0:N_CMP],
                                  ps[0:64, 6, 256:382].rearrange("p (g n) -> p g n", g=2),
                                  full(kc_hi[0:64, :, 0:N_CMP]), ALU.subtract).then_inc(cmp_lo, 1)
            dve.tensor_tensor(vc_st[0:N_CMP, :, 64:128], ps[0:N_CMP, 6, 384:512].rearrange("p (g d) -> p g d", g=2),
                              full(vc_st[0:N_CMP, :, 0:64]), ALU.subtract).then_inc(cmp_lo, 1)

        def pooled_part(g):
            w = POOL_SIZES[g]
            s, p = ps_ab[g % 2], ps_ab[(g + 1) % 2]
            if g == 3:
                dve.wait_ge(fm_act, 2 * N_FM)
                src = pu
                for step in range(4):
                    dst, back = ps_ab[step % 2], 1 << step
                    dve.wait_ge(pool_add, 6 + step)
                    if step == 0:
                        dve.wait_ge(pooled_lo, 3)
                    dve.tensor_tensor(dst[:, PAD:], src[:, PAD:], src[:, PAD - back:PAD + SEQ - back], ALU.add) \
                        .then_inc(pool_add, 1)
                    src = dst
            dve.wait_ge(pool_add, sum(range(1, g + 2)))
            dve.tensor_tensor(s[:, PAD:PAD + w], s[:, PAD:PAD + w], inv_cnt[:, g, 0:w], ALU.mult).then_inc(pooled_w, 1)
            dve.scalar_tensor_tensor(out=p[:, PAD + w:], in0=s[:, PAD + w:], scalar=1.0 / w, in1=pu[:, PAD + w:],
                                     op0=ALU.mult, op1=ALU.subtract).then_inc(pooled, 1)
            dve.wait_ge(pooled_w, g + 1)
            dve.tensor_tensor(p[:, PAD:PAD + w], s[:, PAD:PAD + w], pu[:, PAD:PAD + w], ALU.subtract).then_inc(pooled, 1)
            dve.wait_ge(pooled_hi, g + 1)
            dve.tensor_tensor(pp_lo[:, :], p[:, PAD:], full(pp_hi[:, :]), ALU.subtract).then_inc(pooled_lo, 1)

        def ada2_add(n):
            k, part = n // 4, n % 4
            if n == 0:
                dve.wait_ge(acc_bias, 32)
            dve.wait_ge(ada2_in[part], 16 * (k + 1))
            if k:
                dve.wait_ge(ada2_added, n - 3)
            dve.scalar_tensor_tensor(out=acc2[:, part, :], in0=ada2[:, part, :], scalar=silu_c[:, k:k + 1],
                                     in1=acc2[:, part, :], op0=ALU.mult, op1=ALU.add).then_inc(ada2_added, 1)

        def gt_rows(f):
            dve.wait_ge(gp_row_in, 32)
            for half in range(2):
                sl = slice(half * CH, (half + 1) * CH)
                dve.wait_ge(gt_mm, 2 * f + half + 1)
                dve.tensor_tensor(ada2[0:1, f, sl], ps[0:1, 4 + half, :], ada2[0:1, f, sl], ALU.mult).then_inc(gt_row, 1)

        def mod2_columns():
            dve.wait_ge(mod2_mm, 1)
            dve.tensor_copy(shift2, ps[:, 7, 0:8]).then_inc(mod2_done, 1)
            dve.scalar_tensor_tensor(out=scale2, in0=ps[:, 7, 8:16], scalar=1.0, in1=g_mlp, op0=ALU.add,
                                     op1=ALU.mult).then_inc(mod2_done, 1)

        for n in range(4):
            ada2_add(n)
        for a in range(N_FM):
            if a - 1 in FM_ROPE and 1 < a < 8:
                for ch in range(2):
                    rope_lo_part(2 * FM_ROPE[a - 1] + ch)
            if a in FM_ROPE:
                for ch in range(2):
                    rope_cos_part(a, ch)
            split_a(a + 2)
            if a == 7:
                gt_rows(0)
                mod2_columns()
                gt_rows(1)
            if a == 3:
                dve.wait_ge(const_in, 16 * N_SMALL)
                make_blocks(0)
            if a == 5:
                gelu(0)
                make_blocks(1)
            for n in range(4 * KT):
                if ADD_AT[n] == a:
                    ada2_add(n)
            if a == 7:
                gelu(1)
            if a == 8:
                cmp_store()
                dve.wait_ge(wp_hi_s, 1)
                dve.tensor_tensor(wp_lo[:, :, :], wp_raw[:, :, :], full(wp_hi[:, :, :]), ALU.subtract).then_inc(wp_lo_s, 1)
            if a >= 8:
                pooled_part(a - 8)
            if a == 8:
                for ch in range(2):
                    rope_lo_part(ROPES - 2 + ch)

        def transposed_lo(u, b):
            n = BANKS_BEFORE[u] + b
            dve.wait_ge(pthi, n + 1)
            w = 256 * min(2, len(key_tiles(u // 4)) - 2 * b)
            dve.tensor_tensor(pt_lo[:, n % 3, 0:w], ps[:, 4 + n % 2, 0:w], full(pt_hi[:, n % 3, 0:w]),
                              ALU.subtract).then_inc(ptlo, 1)

        def neg_max(u, s):
            c, n = u // 4, STEPS * u + s
            dve.wait_ge(score_mm, n + 1)
            k = 2 if s == 4 else 1
            if s < 4:
                parts = score_parts(c, s // 2)
                src = ps[:, 2 * (n % 2):2 * (n % 2) + len(parts), 0:parts[0][1]]
                dve.tensor_reduce(smax[:, n % 4, 0:1], src, AX.XY, ALU.max).then_inc(max_done, 1)
            else:
                src = ps[:, 2 * (n % 2), 0:P].rearrange("p (h n) -> p h n", h=2)[:, :, 0:cmp_width(c)]
                dve.tensor_reduce(smax[:, n % 4, 0:2], src, AX.X, ALU.max).then_inc(max_done, 1)
            dve.wait_ge(max_done, n + 1)
            dve.tensor_scalar(negm[:, n % 4, 0:k], smax[:, n % 4, 0:k], NEG / 10, -HEAD_DIM ** -0.5, ALU.max,
                              ALU.mult).then_inc(negm_done, 1)

        def normalise(u, s):
            c, n = u // 4, STEPS * u + s
            heads = (0, 1) if s == 4 else (s % 2,)
            k = len(heads)
            dve.wait_ge(guard_done, n + 1)
            dve.reciprocal(srec[:, n % 4, 0:k], ssum[:, n % 4, 0:k]).then_inc(rec_done, 1)
            dve.wait_ge(rec_done, n + 1)
            for x, hh in enumerate(heads):
                branch = s // 2
                buf = (p_sel, p_win, p_cmp)[branch]
                w = cmp_width(c) if s == 4 else sum(q[1] for q in score_parts(c, branch))
                at = 3 * (2 * (u % 4) + hh) + (1, 2, 0)[branch]
                ins = dve.tensor_scalar(buf[:, u % 2, hh, 0:w], buf[:, u % 2, hh, 0:w], srec[:, n % 4, x:x + 1],
                                        gates[:, c, at:at + 1], ALU.mult, ALU.mult)
            ins.then_inc(norm_done, 1)

        def merge_split(m):
            q, b = m
            s = (R_MERGE + b) % 2
            dve.wait_ge(hi_done, 2 * q + (R_MERGE + b + 1))
            dve.tensor_tensor(a_lo[:, b, :], raw[:, s, :], full(a_hi[:, b, :]), ALU.subtract).then_inc(lo_done, 1)

        dve.wait_ge(gates_done, 1)
        for it in range(UNITS + 1):
            for i in range(SLOTS):
                if it < UNITS and i % 2 == 0:
                    neg_max(it, i // 2)
                if it:
                    for b in range(n_banks(it - 1)):
                        if tp_slot(it - 1, b) == i:
                            transposed_lo(it - 1, b)
                n = STEPS * it + i // 2 - 1
                if i % 2 == 0 and 0 <= n < STEPS * UNITS:
                    normalise(n // STEPS, n % STEPS)
                if i == 1 and it == UNITS:
                    dve.wait_ge(lo_done, R_MERGE)
                    merge_split((0, 0))
            if it:
                v = it - 1
                dve.wait_ge(o_half, v + 1)
                if v >= 2:
                    dve.wait_ge(o_st[v % 2], 16 * (v // 2))
                dve.tensor_tensor(o_out[:, v % 2, :], ps[0:64, 6, 0:256], o_tmp[:, v % 2, :],
                                  ALU.add).then_inc(o_sum, 1)

        for i in range(KT):
            hi, lo = op_hi[i // 4][:, i % 4, :], op_lo[i // 4][:, i % 4, :]
            dve.wait_ge(op_hi_s, i + 1)
            dve.tensor_tensor(lo, op_raw[i // 4][:, i % 4, :], full(hi), ALU.subtract).then_inc(op_lo_s, 1)
            if i == 3:
                merge_split((0, 1))

        def out_split(n):
            s = OUT_SLOT[n]
            split_lo(R_OUT + n, b_lo[s][:, :], b_hi[s][:, :])

        def merged_lo(q, b):
            tile = bass.ds(2 * q + b, 1)
            dve.wait_ge(merge_hi, 2 * q + (b + 1))
            dve.scalar_tensor_tensor(out=act_lo[:, tile, :].rearrange("p k n -> p (k n)"), in0=m_a[:, b, :], scalar=0.5,
                                     in1=full(act_hi[:, tile, :]).rearrange("p k n -> p (k n)"), op0=ALU.mult,
                                     op1=ALU.subtract).then_inc(merge_lo, 1)

        def merge(q, first=False, last=False):
            for b in range(2):
                if last and b == 1:
                    out_split(0)
                    out_split(1)
                elif not (first and b == 0):
                    merge_split((q, 1) if b == 0 else (q + 1, 0))
                if b:
                    merged_lo(q, 0)
                elif not first:
                    merged_lo(q - 1, 1)
                if not first:
                    dve.wait_ge(merge_lo, 2 * q + (b - 1))
                for ch in range(2):
                    g, sl = 2 * b + ch, slice(ch * CH, (ch + 1) * CH)
                    if last and b == 1 and ch == 0:
                        out_split(2)
                        out_split(3)
                    dve.wait_ge(merge_mm, 4 * q + (g + 1))
                    dve.wait_ge(mg_in[ch], 32 * q + 16 * (b + 1))
                    if not (first and b == 0):
                        dve.wait_ge(merge_sum, 4 * q + (g - 1))
                    for h, dst in ((0, m_a[:, b, sl]), (1, m_b[:, ch, :])):
                        ins = dve.scalar_tensor_tensor(out=dst, in0=mg[:, ch, h, :], scalar=1.0,
                                                       in1=ps[:, 2 * g + (1 - h), :], op0=ALU.add, op1=ALU.mult)
                    ins.then_inc(merge_ab, 1)

        merge(0, first=True)
        with dve.Fori(1, KT // 2 - 1) as q:
            merge(q)
        merge(KT // 2 - 1, last=True)
        merged_lo(KT // 2 - 1, 1)
        for n in range(4, 8):
            out_split(n)

        def mlp_split(j, n):
            s = (R_MLP + n) % 2
            dve.wait_ge(hi_done, 8 * j + (R_MLP + n + 1))
            dst, hi = (a_lo[:, (A_MLP + n) % 2, :], a_hi[:, (A_MLP + n) % 2, :]) if n % 8 < 4 else \
                (b_lo[n - 4][:, :], b_hi[n - 4][:, :])
            dve.tensor_tensor(dst, raw[:, s, :], full(hi), ALU.subtract).then_inc(lo_done, 1)

        dve.wait_ge(gt_in, 32)
        def x1_scale(t):
            dve.wait_ge(x1_rstd, t + 1)
            dve.tensor_scalar(y[:, t, :], x1[:, t % 2, :], stat[:, 8 + t:9 + t], None, ALU.mult).then_inc(x1n_made, 1)

        for t in range(TT):
            yt = y[:, t, :]
            dve.wait_ge(y_rstd, t + 1)
            dve.scalar_tensor_tensor(out=yt, in0=yt, scalar=stat[:, t:t + 1], in1=gt1[:, :], op0=ALU.mult,
                                     op1=ALU.mult).then_inc(y_gated, 1)
            dve.wait_ge(y_gated, t + 1)
            dve.wait_ge(xi_in[t % 2], 16 * (t // 2 + 1))
            if t >= 2:
                dve.wait_ge(x1_st[t % 2], 16 * (t // 2))
                dve.wait_ge(x1_ms, t - 1)
                dve.wait_ge(x1n_made, t - 1)
            dve.tensor_tensor(x1[:, t % 2, :], yt, x_in[:, t % 2, :], ALU.add).then_inc(x1_made, 1)
            if t:
                x1_scale(t - 1)
            if t == 5:
                for m in range(KT):
                    split_h(h2_tmp, m, h2_made, h2_hi, h2_lo)
                mlp_split(0, 0)
                mlp_split(0, 1)
        x1_scale(TT - 1)

        for m in range(KT, 2 * KT):
            split_h(h2_tmp, m, h2_made, h2_hi, h2_lo)

        def final_scale(t):
            dve.wait_ge(y2_added, 2 * TT * (D_FF // CH - 1) + 2 * t + 2)
            dve.tensor_tensor(fin[:, t % 2, :], y[:, t, :], gt2[:, :], ALU.mult).then_inc(f_gated, 1)

        def final(t):
            dve.wait_ge(f_rstd, t + 1)
            dve.wait_ge(f_gated, t + 1)
            dve.wait_ge(x1i_in[t % 2], 16 * (t // 2 + 1))
            dve.scalar_tensor_tensor(out=fin[:, t % 2, :], in0=fin[:, t % 2, :], scalar=stat[:, 16 + t:17 + t],
                                     in1=x1_in[:, t % 2, :], op0=ALU.mult, op1=ALU.add).then_inc(f_made, 1)

        def mlp(j, first=False, last=False):
            for n in range(8):
                m, ch = 2 * (n // 4) + n % 2, (n // 2) % 2
                sl = slice(ch * CH, (ch + 1) * CH)
                if first and n == 4:
                    for s in range(2):
                        dve.wait_ge(x1_st[s], 16 * TT // 2)
                for x in MLP_SPLITS[n]:
                    mlp_split(j, x)
                dve.wait_ge(hid_hi_s, 8 * j + (n + 1))
                dve.tensor_tensor(hid_lo[:, m, sl], relu[:, n % 2, :], full(hid_hi[:, m, sl]), ALU.subtract) \
                    .then_inc(hid_lo_s, 1)
            if not last:
                mlp_split(j, 8)
                mlp_split(j, 9)
            for n in range(2 * TT):
                t, half = n // 2, n % 2
                yt = y[:, t, half * CH:(half + 1) * CH]
                dve.wait_ge(fc2_mm, 2 * TT * j + (n + 1))
                if first:
                    dve.tensor_copy(yt, ps[:, 4 + n % 4, :]).then_inc(y2_added, 1)
                else:
                    dve.wait_ge(y2_added, 2 * TT * j + (n - 2 * TT + 1))
                    dve.tensor_tensor(yt, ps[:, 4 + n % 4, :], yt, ALU.add).then_inc(y2_added, 1)
                if last and half:
                    if t:
                        final(t - 1)
                    if t >= 2:
                        dve.wait_ge(out_st[t % 2], 16 * (t // 2))
                    final_scale(t)

        mlp(0, first=True)
        with dve.Fori(1, D_FF // CH - 1) as j:
            mlp(j)
        mlp(D_FF // CH - 1, last=True)
        final(TT - 1)

    @block.tensor
    def _(pe):
        def three(dst, wh, wl, mh, ml, start, stop):
            pe.matmul(dst, wh, mh, start=start, stop=False)
            pe.matmul(dst, wh, ml, start=False, stop=False)
            return pe.matmul(dst, wl, mh, start=False, stop=stop)

        def mod_columns(part):
            for n in range(8 * part, 8 * part + 8):
                ins = pe.matmul(ps[:, 7, n:n + 1], ada_acc[:, n * P:(n + 1) * P], ones[:, 0:1], start=True, stop=True)
            ins.then_inc(mod_mm, 1)

        def x_transposes(n):
            ch, k = n // KT, n % KT
            if n % KT == 0:
                pe.wait_ge(x_norm, 4 * ch + 4)
            if n >= 4:
                pe.wait_ge(h_made, n - 3)
            for t in range(4):
                ins = pe.transpose(ps[:, n % 4, t * P:(t + 1) * P], xt[:, 4 * ch + t, k * P:(k + 1) * P], ident[:, :])
            ins.then_inc(xt_mm, 1)

        def values_and_gates(ch, k):
            pe.wait_ge(h_lo, KT * ch + k + 1)
            for t in range(4 * ch, 4 * ch + 4):
                if ch and k == 0:
                    pe.wait_ge(v_lo, t - 3)
                    pe.wait_ge(v_hi, 2 * t - 6)
                tok = slice(t * P, (t + 1) * P)
                ins = three(ps[:, 4 + t % 4, 0:WV_COLS], act_hi[:, k, tok], act_lo[:, k, tok], wv_hi[:, k, :],
                            wv_lo[:, k, :], k == 0, k == KT - 1)
                if k == KT - 1:
                    ins.then_inc(v_mm, 1)

        pe.wait_ge(consts_made, CONSTS)
        pe.wait_ge(ada_added, 8)
        mod_columns(1)
        pe.wait_ge(ada_added, 16)
        pe.wait_ge(mod_done, 1)
        mod_columns(0)
        for n in range(8):
            x_transposes(n)
        pe.wait_ge(mod_done, 2)
        for k in range(KT):
            pe.wait_ge(wv_lo_s, k // 2 + 1)
            values_and_gates(0, k)
            if k >= 4:
                x_transposes(4 + k)
        for k in range(KT):
            if k < 4:
                x_transposes(12 + k)
            values_and_gates(1, k)

        def project(a, bank, ch, ks, done=None):
            sl = slice(ch * CH, (ch + 1) * CH)
            for k in ks:
                w = slice(k * P, (k + 1) * P)
                ins = three(ps[:, bank, :], a_hi[:, a % 2, w], a_lo[:, a % 2, w], act_hi[:, k, sl], act_lo[:, k, sl],
                            k == 0, k == KT - 1)
            return ins

        def compress(kv):
            pe.wait_ge(cw_in, 16 * (kv + 1))
            pe.wait_ge(bk_made, kv + 1)
            if kv:
                pe.wait_ge(gelu_c, 1)
            for l in range(16):
                ins = pe.matmul(ps[0:64, 6, P * kv:P * kv + 126], cw1[:, l, :],
                                bk[:, l, :, :].rearrange("p g n -> p (g n)"), start=l == 0, stop=l == 15)
            ins.then_inc(cmp_mm, 1)

        def compress2():
            pe.wait_ge(gelu_d, 10)
            pe.matmul(ps[0:64, 6, 256:382], w2k[:, :], gelu_t[:, 0, :], start=True, stop=True).then_inc(cmp2_mm, 1)
            for g in range(2):
                ins = pe.matmul(ps[0:N_CMP, 6, 384 + 64 * g:448 + 64 * g], gelu_t[:, 1, N_CMP * g:N_CMP * (g + 1)],
                                w2v[:, :], start=True, stop=True)
            ins.then_inc(cmp2_mm, 1)

        def mix(g):
            pe.wait_ge(pooled_lo, g + 1)
            if g == 0:
                pe.wait_ge(wp_lo_s, 1)
            for ch in range(2):
                n, sl = 2 * g + ch, slice(ch * CH, (ch + 1) * CH)
                if n >= 2:
                    pe.wait_ge(mix_out, n - 1)
                three(ps[:, 4 + n % 2, :], wp_hi[:, g, :], wp_lo[:, g, :], pp_hi[:, sl], pp_lo[:, sl], True, True) \
                    .then_inc(mix_mm, 1)

        def second_modulation():
            pe.wait_ge(ada2_added, 4 * KT)
            pe.wait_ge(v_lo, TT)
            pe.wait_ge(v_hi, 2 * TT)
            for f, part in ((0, 0), (1, 3)):
                for half in range(2):
                    if f:
                        pe.wait_ge(gt_row, half + 1)
                    pe.matmul(ps[0:1, 4 + half, :], ones[:, 0:1], acc2[:, part, half * CH:(half + 1) * CH],
                              start=True, stop=True).then_inc(gt_mm, 1)
                if f == 0:
                    for n in range(16):
                        ins = pe.matmul(ps[:, 7, n:n + 1], acc2[:, 1 + n // KT, (n % KT) * P:(n % KT + 1) * P],
                                        ones[:, 0:1], start=True, stop=True)
                    ins.then_inc(mod2_mm, 1)

        def gate_part(h, ks):
            if 0 in ks:
                pe.wait_ge(lo_done, R_FM + N_FM + h // 2 + 1)
                if h >= 2:
                    pe.wait_ge(gate_tanh, h)
            ins = project(N_FM + h // 2, 6 if h == 1 else 7, h % 2, ks)
            if KT - 1 in ks:
                ins.then_inc(gate_mm, 1)

        for a in range(N_FM):
            pe.wait_ge(lo_done, R_FM + a + 1)
            for ch in range(2):
                g = 2 * a + ch
                if g >= 4:
                    pe.wait_ge(fm_act, g - 3)
                    if a - 2 in FM_ROPE:
                        pe.wait_ge(rope_cos, 2 * FM_ROPE[a - 2] + ch + 1)
                ins = project(a, g % 4, ch, range(KT))
                ins.then_inc(fm_mm, 1)
            if a == 4:
                compress(0)
            if a == 6:
                compress(1)
            if a == 7:
                second_modulation()
            if a == 8:
                compress2()
            if a >= 9:
                mix(a - 9)
        pe.wait_ge(mod2_done, 2)
        gate_part(0, range(KT))
        pe.wait_ge(cmp_lo, 3)
        gate_part(1, range(KT))
        mix(3)

        def scores(u, s):
            c, n = u // 4, STEPS * u + s
            g = (u % 4) // 2
            if n >= 2:
                pe.wait_ge(exp_done, n - 1)
            if s == 0 and u % 4 == 0:
                pe.wait_ge(q_in[c % 2], 16 * (c // 2 + 1))
            base = 2 * (n % 2)
            if s < 4:
                branch, q = s // 2, q_st[:, c % 2, 2 * (u % 4) + s % 2, :]
                parts = score_parts(c, branch)
                for x, (k0, w, _) in enumerate(parts):
                    last, far = x == len(parts) - 1, branch == 1 and c >= WINDOW // P and x == 0
                    wide = max(w, FULL_RATE)
                    dst = ps[:, base + x, 0:wide]
                    pe.matmul(dst, q, k_hi[:, 2 * branch + g, k0:k0 + wide], start=True, stop=False)
                    ins = pe.matmul(dst, q, k_lo[:, 2 * branch + g, k0:k0 + wide], start=False, stop=True)
                    if far:
                        ins = pe.matmul(ps[:, base + x, 0:P], ident_b[:, :], mask_far[:, :], start=False, stop=True,
                                        skip_group_check=True)
                    if last:
                        ins = pe.matmul(ps[:, base + x, w - P:w], ident_b[:, :], mask_diag[:, :], start=False, stop=True,
                                        skip_group_check=True)
            else:
                for hh in range(2):
                    w = cmp_width(c)
                    dst, q = ps[:, base, 64 * hh:64 * hh + w], q_st[:, c % 2, 2 * (u % 4) + hh, :]
                    pe.matmul(dst, q, kc_hi[:, g, 0:w], start=True, stop=False)
                    pe.matmul(dst, q, kc_lo[:, g, 0:w], start=False, stop=False)
                    ins = pe.matmul(dst, ident_b[:, :], mask_cmp[:, c, 0:w], start=False, stop=True)
            ins.then_inc(score_mm, 1)

        def transposes(u, b):
            c, n = u // 4, BANKS_BEFORE[u] + b
            if n >= 2:
                pe.wait_ge(ptlo, n - 1)
            elif n == 0:
                pe.wait_ge(mix_out, 8)
            for x, (branch, j) in enumerate(key_tiles(c)[2 * b:2 * b + 2]):
                pe.wait_ge(norm_done, STEPS * u + (2, 4, 5)[branch])
                for hh in range(2):
                    at = ps[:, 4 + n % 2, 256 * x + P * hh:256 * x + P * hh + P]
                    if branch == 2:
                        src = p_cmp[:, u % 2, hh, :]
                    else:
                        k = (j - (max(0, c - WINDOW // P) if branch else 0)) * P
                        src = (p_sel, p_win)[branch][:, u % 2, hh, k:k + P]
                    ins = pe.transpose(at, src, ident[:, :])
            ins.then_inc(tp_mm, 1)

        def value_products(u, b):
            c, n, g = u // 4, BANKS_BEFORE[u] + b, (u % 4) // 2
            pe.wait_ge(ptlo, n + 1)
            if b == 0:
                if u:
                    pe.wait_ge(o_sum, u)
                else:
                    pe.wait_ge(gate_tanh, 2)
            tiles = key_tiles(c)
            for x, (branch, j) in enumerate(tiles[2 * b:2 * b + 2]):
                v = vc_st[:, g, :] if branch == 2 else v_st[:, j, 2 * branch + g, :]
                dst = ps[:, 6, 0:256]
                first, last = b == 0 and x == 0, 2 * b + x == len(tiles) - 1
                pe.matmul(dst, v, pt_hi[:, n % 3, 256 * x:256 * x + 256], start=first, stop=False)
                ins = pe.matmul(dst, v, pt_lo[:, n % 3, 256 * x:256 * x + 256], start=False, stop=last)
            ins.then_inc(pv_mm, 1)

        pe.wait_ge(fm_act, 2 * N_FM)
        pe.wait_ge(rope_out[0], rope_out_count(ROPES - 2))
        pe.wait_ge(rope_out[1], rope_out_count(ROPES - 1))
        pe.wait_ge(cmp_lo, 3)
        for it in range(UNITS + 1):
            for i in range(SLOTS):
                if it < UNITS and i % 2 == 0:
                    scores(it, i // 2)
                if it:
                    for b in range(n_banks(it - 1)):
                        if tp_slot(it - 1, b) == i:
                            transposes(it - 1, b)
                if it in HALF_OF and i < KT:
                    gate_part(HALF_OF[it], (i,))
                if it:
                    for b in range(n_banks(it - 1)):
                        if tp_slot(it - 1, b) + 2 == i:
                            value_products(it - 1, b)
        gate_part(HALVES - 1, range(KT))

        def merge_part(q, b, part, first):
            for ch in range(2):
                g = 2 * b + ch
                if part == 0 and not first:
                    pe.wait_ge(merge_ab, 4 * q + (g - 3))
                for k in range(4):
                    if first and b == 0:
                        pe.wait_ge(op_lo_s, 4 * part + k + 1)
                    w, sl = slice((4 * part + k) * P, (4 * part + k + 1) * P), slice(ch * CH, (ch + 1) * CH)
                    ins = three(ps[:, 2 * g + part, :], a_hi[:, b, w], a_lo[:, b, w], op_hi[part][:, k, sl],
                                op_lo[part][:, k, sl], k == 0, k == 3)
                if part:
                    ins.then_inc(merge_mm, 1)
            if part == 0:
                ins.then_inc(merge_pool, 1)

        pe.wait_ge(exp_done, STEPS * UNITS)
        pe.wait_ge(lo_done, R_MERGE + 1)
        merge_part(0, 0, 0, True)
        pe.wait_ge(gate_tanh, HALVES)
        pe.wait_ge(o_sum, UNITS)
        pe.wait_ge(ptlo, BANKS_BEFORE[UNITS])
        pe.wait_ge(lo_done, R_MERGE + 2)
        merge_part(0, 1, 0, True)
        merge_part(0, 0, 1, True)
        merge_part(0, 1, 1, True)
        with pe.Fori(1, KT // 2) as q:
            for b in range(2):
                pe.wait_ge(lo_done, 2 * q + (R_MERGE + b + 1))
                for part in range(2):
                    merge_part(q, b, part, False)

        def x1_transposes(m):
            half, k = m // KT, m % KT
            if k == 0:
                pe.wait_ge(x1n_made, 4 * half + 4)
            if k >= 4:
                pe.wait_ge(h2_made, m - 3)
            for t in range(4):
                ins = pe.transpose(ps[:, 4 * half + m % 4, t * P:(t + 1) * P], y[:, 4 * half + t, k * P:(k + 1) * P],
                                   ident[:, :])
            ins.then_inc(x1t_mm, 1)

        def out_product(n, k):
            half, t = n // TT, n % TT
            s, w = OUT_SLOT[4 * half + k // 2], slice((k % 2) * CH, (k % 2 + 1) * CH)
            tok = slice(t * P, (t + 1) * P)
            ins = three(ps[:, 4 * half + n % 4, :], act_hi[:, k, tok], act_lo[:, k, tok], b_hi[s][:, w],
                        b_lo[s][:, w], k == 0, k == KT - 1)
            if k == KT - 1:
                ins.then_inc(y_mm, 1)

        pe.wait_ge(merge_lo, KT - 1)
        pe.wait_ge(merge_hi, KT - 1)
        for n in range(4):
            for k in range(KT - 1):
                if n == 0 and k % 2 == 0:
                    pe.wait_ge(lo_done, R_OUT + k // 2 + 1)
                out_product(n, k)
        pe.wait_ge(merge_lo, KT)
        pe.wait_ge(merge_hi, KT)
        for n in range(4):
            out_product(n, KT - 1)
        for n in range(4, 2 * TT):
            if n in range(4, TT) or n >= TT + 4:
                pe.wait_ge(y_out, n - 3)
            if n == TT + 6:
                for m in range(4):
                    x1_transposes(m)
            for k in range(KT):
                if n == TT and k in (0, 4):
                    pe.wait_ge(lo_done, R_OUT + (6, 8)[k // 4])
                out_product(n, k)
                if n == TT + 6 and 2 <= k < 6:
                    x1_transposes(2 + k)

        def mlp(j, first=False):
            for n in range(8):
                m, ch = 2 * (n // 4) + n % 2, (n // 2) % 2
                a = (A_MLP + m) % 2
                if ch == 0:
                    pe.wait_ge(lo_done, 8 * j + (R_MLP + m + 1))
                if first and n == 0:
                    pe.wait_ge(h2_lo, KT)
                if first and n == 2:
                    for m in range(4):
                        x1_transposes(KT + m)
                if not (first and n < 4):
                    pe.wait_ge(relu_done, 8 * j + (n - 3))
                sl = slice(ch * CH, (ch + 1) * CH)
                for k in range(KT):
                    w = slice(k * P, (k + 1) * P)
                    if first and n == 2:
                        pe.wait_ge(h2_lo, KT + k + 1)
                        if k < 4:
                            x1_transposes(KT + 4 + k)
                    ins = three(ps[:, n % 4, :], a_hi[:, a, w], a_lo[:, a, w], act_hi[:, k, sl], act_lo[:, k, sl],
                                k == 0, k == KT - 1)
                ins.then_inc(fc1_mm, 1)
            pe.wait_ge(lo_done, 8 * j + (R_MLP + 8))
            for n in range(2 * TT):
                t, half = n // 2, n % 2
                if n in (0, TT):
                    pe.wait_ge(hid_lo_s, 8 * j + (6, 8)[n // TT])
                if not (first and n < 4):
                    pe.wait_ge(y2_added, 2 * TT * j + (n - 3))
                elif n == 0:
                    pe.wait_ge(y_out, 2 * TT)
                tok, w = slice(t * P, (t + 1) * P), slice(half * CH, (half + 1) * CH)
                for k in range(4):
                    ins = three(ps[:, 4 + n % 4, :], hid_hi[:, k, tok], hid_lo[:, k, tok], b_hi[k][:, w], b_lo[k][:, w],
                                k == 0, k == 3)
                ins.then_inc(fc2_mm, 1)
        mlp(0, first=True)
        with pe.Fori(1, D_FF // CH) as j:
            mlp(j)

    block.__exit__(None, None, None)


_INS = ["x", "c", "w_ada", "b_ada", "g_pre_mix", "g_post_mix", "w_in", "cmp_pe_k", "cmp_w1_k", "cmp_w2_k", "cmp_pe_v",
        "cmp_w1_v", "cmp_w2_v", "w_pool", "pool_scale", "w_br_nsa", "w_br_pool", "w_out", "g_pre_mlp", "g_post_mlp",
        "w_fc1", "w_fc2"]


def shape_constants():
    half = HEAD_DIM // 2
    inv = (10000.0 ** (-np.arange(half, dtype=np.float64) / half)).astype(np.float32)
    ang = (inv[:, None] * np.arange(SEQ, dtype=np.float32)[None, :]).astype(np.float64)
    cos = np.tile(np.cos(ang), (4, 1)).astype(np.float32)
    sin = np.concatenate([-np.sin(ang), np.sin(ang)] * 2).astype(np.float32)
    cnt = np.minimum(np.arange(16)[None, :] + 1, np.array(POOL_SIZES)[:, None])
    inv_cnt = np.broadcast_to((1.0 / cnt).astype(np.float32), (P, 4, 16)).copy()
    return {"cos": cos, "sin": sin, "inv_cnt": inv_cnt}


def kernel(**inputs):
    import concourse.bacc as bacc
    from concourse.bass_utils import run_bass_kernel_spmd

    nc = bacc.Bacc("TRN2", target_bir_lowering=False, num_devices=1)
    arrays = {n: np.ascontiguousarray(inputs[n]) for n in _INS}
    arrays.update(shape_constants())
    aps = {n: nc.dram_tensor("in_" + n, a.shape, mybir.dt.from_np(a.dtype), kind="ExternalInput").ap()
           for n, a in arrays.items()}
    out = nc.dram_tensor("out", (1, SEQ, D_MODEL), mybir.dt.float32, kind="ExternalOutput").ap()
    hybrid_block(nc, aps, out)
    r = run_bass_kernel_spmd(nc, [{"in_" + n: a for n, a in arrays.items()}], core_ids=[0])
    return r.results[0]["out"]
```
